# Optimizing a Trainium2 kernel written in Bass

```python
import jax, jax.numpy as jnp
from jax import lax
import numpy as np

D_MODEL = 1024
BATCH = 1
SEQ = 512
DEPTH = 1

GRID_W = 64
CTX_LEN = 256
D_MIX = D_MODEL
SSD_WIDTH = D_MIX // 2
SSD_HEADDIM = 64
SSD_HEADS = SSD_WIDTH // SSD_HEADDIM
SSD_GROUPS = 2
HEADS_PER_GROUP = SSD_HEADS // SSD_GROUPS
SSD_STATE = 128
SSD_CONV = 3
SSD_CHUNK = 128
XBC_WIDTH = SSD_WIDTH + 2 * SSD_GROUPS * SSD_STATE
FNET_WIDTH = D_MIX // 4
FNET_GROUPS = 4
FNET_GDIM = FNET_WIDTH // FNET_GROUPS
POOL_WINDOWS = (2, 4, 8, 16)
POOL_WIDTH = D_MIX // 4
POOL_GDIM = POOL_WIDTH // len(POOL_WINDOWS)
D_FF = 256 * ((8 * D_MODEL // 3 + 255) // 256)
FFN_CONV = 3
OFF_Z = 0
OFF_XBC = OFF_Z + SSD_WIDTH
OFF_DT = OFF_XBC + XBC_WIDTH
OFF_FNET = OFF_DT + 2 * SSD_HEADS
OFF_POOL = OFF_FNET + FNET_WIDTH
N_IN = OFF_POOL + POOL_WIDTH
ALPHA = (2.0 * DEPTH) ** 0.25
BETA = (8.0 * DEPTH) ** -0.25
EPS = 1e-6


def layer_norm(x):
    xf = x.astype(jnp.float32)
    mu = jnp.mean(xf, -1, keepdims=True)
    var = jnp.mean(jnp.square(xf - mu), -1, keepdims=True)
    return ((xf - mu) * lax.rsqrt(var + EPS)).astype(x.dtype)

def ada(cvec, w, b):
    m = jax.nn.silu(cvec) @ w + b
    return [mi[:, None, :] for mi in jnp.split(m, 6, axis=-1)]

def modulate(x, shift, scale):
    return layer_norm(x) * (1 + scale) + shift

def post_norm(x, y, gate, g, b):
    return layer_norm(ALPHA * x + gate * y) * g + b

def dwconv1d(x, w, b):
    k = w.shape[0]
    left = (k - 1) // 2
    y = lax.conv_general_dilated(x, w[:, None, :], window_strides=(1,), padding=[(left, k - 1 - left)],
                                 dimension_numbers=("NWC", "WIO", "NWC"), feature_group_count=x.shape[-1])
    return y + b

def dwconv2d_grid(x, w, b):
    bsz, L, C = x.shape
    rows = L // GRID_W
    xg = x.reshape(bsz, rows, GRID_W, C)
    y = lax.conv_general_dilated(xg, w[:, :, None, :], window_strides=(1, 1), padding=[(1, 1), (1, 1)],
                                 dimension_numbers=("NHWC", "HWIO", "NHWC"), feature_group_count=C)
    return y.reshape(bsz, L, C) + b

def segsum(a):
    T = a.shape[-1]
    cs = jnp.cumsum(a, axis=-1)
    seg = cs[..., :, None] - cs[..., None, :]
    mask = jnp.tril(jnp.ones((T, T), dtype=bool))
    return jnp.where(mask, seg, -jnp.inf)

def ssd_chunked(X, dA, B, C, init_state):
    b, L, h, p = X.shape
    n = B.shape[-1]
    nc = L // SSD_CHUNK
    X = X.astype(jnp.float32).reshape(b, nc, SSD_CHUNK, h, p)
    B = B.astype(jnp.float32).reshape(b, nc, SSD_CHUNK, h, n)
    C = C.astype(jnp.float32).reshape(b, nc, SSD_CHUNK, h, n)
    A = dA.astype(jnp.float32).reshape(b, nc, SSD_CHUNK, h).transpose(0, 3, 1, 2)
    A_cs = jnp.cumsum(A, axis=-1)
    Lmat = jnp.exp(segsum(A))
    y_diag = jnp.einsum("bclhn,bcshn,bhcls,bcshp->bclhp", C, B, Lmat, X)
    decay_states = jnp.exp(A_cs[..., -1:] - A_cs)
    states = jnp.einsum("bclhn,bhcl,bclhp->bchpn", B, decay_states, X)
    states = jnp.concatenate([init_state[:, None].astype(jnp.float32), states], axis=1)
    chunk_decay = jnp.exp(segsum(jnp.pad(A_cs[..., -1], ((0, 0), (0, 0), (1, 0)))))
    new_states = jnp.einsum("bhzc,bchpn->bzhpn", chunk_decay, states)
    states, final_state = new_states[:, :-1], new_states[:, -1]
    y_off = jnp.einsum("bclhn,bchpn,bhcl->bclhp", C, states, jnp.exp(A_cs))
    return (y_diag + y_off).reshape(b, L, h, p), final_state

def ssd_final_state(X, dA, B):
    cs = jnp.cumsum(dA, axis=1)
    return jnp.einsum("blh,blhn,blhp->bhpn", jnp.exp(cs[:, -1:] - cs), B.astype(jnp.float32), X)

def rev(a):
    return jnp.flip(a, axis=1)

def ssd_prep(u, conv_w, conv_b, dt_bias, a_log):
    bsz, L, _ = u.shape
    xbc = jax.nn.silu(dwconv1d(u[..., OFF_XBC:OFF_DT], conv_w, conv_b))
    xs = xbc[..., :SSD_WIDTH].reshape(bsz, L, SSD_HEADS, SSD_HEADDIM)
    gn = SSD_GROUPS * SSD_STATE
    bm = xbc[..., SSD_WIDTH:SSD_WIDTH + gn].reshape(bsz, L, SSD_GROUPS, SSD_STATE)
    cm = xbc[..., SSD_WIDTH + gn:].reshape(bsz, L, SSD_GROUPS, SSD_STATE)
    bm = jnp.repeat(bm, HEADS_PER_GROUP, axis=2)
    cm = jnp.repeat(cm, HEADS_PER_GROUP, axis=2)
    dt_raw = u[..., OFF_DT:OFF_FNET].reshape(bsz, L, 2, SSD_HEADS)
    dt = jax.nn.softplus((dt_raw + dt_bias).astype(jnp.float32))
    dA = dt * (-jnp.exp(a_log.astype(jnp.float32)))
    return xs, bm, cm, dt, dA

def ssd_bidir(xs, bm, cm, dt, dA, init_f, init_b):
    x32 = xs.astype(jnp.float32)
    y_f, s_f = ssd_chunked(x32 * dt[:, :, 0, :, None], dA[:, :, 0], bm, cm, init_f)
    y_b, s_b = ssd_chunked(rev(x32 * dt[:, :, 1, :, None]), rev(dA[:, :, 1]), rev(bm), rev(cm), init_b)
    return y_f + rev(y_b), s_f, s_b

def ssd_gate_norm(y, xs, z, d_skip, norm_w):
    bsz, L = z.shape[:2]
    y = (y + xs.astype(jnp.float32) * d_skip.astype(jnp.float32)[:, None]).reshape(bsz, L, SSD_WIDTH)
    y = (y * jax.nn.silu(z.astype(jnp.float32))).reshape(bsz, L, SSD_GROUPS, SSD_WIDTH // SSD_GROUPS)
    y = (y * lax.rsqrt(jnp.mean(y * y, -1, keepdims=True) + EPS)).reshape(bsz, L, SSD_WIDTH)
    return (y * norm_w).astype(z.dtype)

def fourier_mix(f, w):
    bsz, L, _ = f.shape
    fg = f.astype(jnp.float32).reshape(bsz, L, FNET_GROUPS, FNET_GDIM)
    spec = jnp.fft.fft2(fg, axes=(1, 3), norm="ortho").real
    y = jnp.einsum("blgc,gcd->blgd", spec.astype(f.dtype), w)
    return y.reshape(bsz, L, FNET_WIDTH)

def pool_mix(p, w, scale):
    bsz, L, _ = p.shape
    pf = p.astype(jnp.float32)
    cs = jnp.pad(jnp.cumsum(pf, axis=1), ((0, 0), (1, 0), (0, 0)))
    pos = jnp.arange(L)
    outs = []
    for gi, win in enumerate(POOL_WINDOWS):
        left = win // 2
        right = win - 1 - left
        hi = jnp.minimum(pos + right + 1, L)
        lo = jnp.maximum(pos - left, 0)
        sl = slice(gi * POOL_GDIM, (gi + 1) * POOL_GDIM)
        csg = cs[..., sl]
        mean = (csg[:, hi] - csg[:, lo]) / (hi - lo).astype(jnp.float32)[None, :, None]
        outs.append(mean - pf[..., sl])
    pooled = jnp.stack(outs, axis=2).astype(p.dtype)
    y = jnp.einsum("blgc,gcd->blgd", pooled, w).reshape(bsz, L, POOL_WIDTH)
    return y * scale

def token_mixer(u, init_f, init_b, conv_w, conv_b, dt_bias, a_log, d_skip, norm_w, fnet_w, pool_w, pool_scale, w_out):
    xs, bm, cm, dt, dA = ssd_prep(u, conv_w, conv_b, dt_bias, a_log)
    y, s_f, s_b = ssd_bidir(xs, bm, cm, dt, dA, init_f, init_b)
    y_ssd = ssd_gate_norm(y, xs, u[..., OFF_Z:OFF_XBC], d_skip, norm_w)
    y_fnet = fourier_mix(u[..., OFF_FNET:OFF_POOL], fnet_w)
    y_pool = pool_mix(u[..., OFF_POOL:N_IN], pool_w, pool_scale)
    return jnp.concatenate([y_ssd, y_fnet, y_pool], axis=-1) @ w_out, s_f, s_b

def ctx_scan_states(u, conv_w, conv_b, dt_bias, a_log):
    xs, bm, _, dt, dA = ssd_prep(u, conv_w, conv_b, dt_bias, a_log)
    x32 = xs.astype(jnp.float32)
    s_f = ssd_final_state(x32 * dt[:, :, 0, :, None], dA[:, :, 0], bm)
    s_b = ssd_final_state(rev(x32 * dt[:, :, 1, :, None]), rev(dA[:, :, 1]), rev(bm))
    return s_f, s_b

def conv_ffn(h, w_up, conv_w, conv_b, w_down, grid):
    a = h @ w_up
    a = dwconv2d_grid(a, conv_w, conv_b) if grid else dwconv1d(a, conv_w[1], conv_b)
    val, gate = jnp.split(a, 2, axis=-1)
    return (jax.nn.gelu(gate) * val) @ w_down

def first_inputs(seed: int = 0) -> dict:
    key = jax.random.key(seed)
    ks = jax.random.split(key, 25)
    f32 = jnp.float32

    def nrm(k, shape, s):
        return s * jax.random.normal(k, shape, f32)

    dt0 = jnp.exp(jax.random.uniform(ks[9], (DEPTH, 2, SSD_HEADS), f32, np.log(1e-3), np.log(1e-1)))
    return {
        "x": nrm(ks[0], (BATCH, SEQ, D_MODEL), 1.0),
        "c": nrm(ks[1], (BATCH, D_MODEL), 1.0),
        "ctx": nrm(ks[2], (BATCH, CTX_LEN, D_MODEL), 1.0),
        "c_ctx": nrm(ks[3], (D_MODEL,), 1.0),
        "w_ada": nrm(ks[4], (DEPTH, D_MODEL, 6 * D_MODEL), 0.5 * D_MODEL ** -0.5),
        "b_ada": nrm(ks[5], (DEPTH, 6 * D_MODEL), 0.02),
        "w_in": nrm(ks[6], (DEPTH, D_MODEL, N_IN), D_MODEL ** -0.5),
        "ssd_conv_w": nrm(ks[7], (DEPTH, SSD_CONV, XBC_WIDTH), SSD_CONV ** -0.5),
        "ssd_conv_b": nrm(ks[8], (DEPTH, XBC_WIDTH), 0.02),
        "ssd_dt_bias": dt0 + jnp.log(-jnp.expm1(-dt0)),
        "ssd_a_log": jnp.log(jax.random.uniform(ks[10], (DEPTH, 2, SSD_HEADS), f32, 1.0, 16.0)),
        "ssd_d": 1.0 + nrm(ks[11], (DEPTH, SSD_HEADS), 0.1),
        "ssd_norm_w": 1.0 + nrm(ks[12], (DEPTH, SSD_WIDTH), 0.1),
        "fnet_w": nrm(ks[13], (DEPTH, FNET_GROUPS, FNET_GDIM, FNET_GDIM), FNET_GDIM ** -0.5),
        "pool_w": nrm(ks[14], (DEPTH, len(POOL_WINDOWS), POOL_GDIM, POOL_GDIM), POOL_GDIM ** -0.5),
        "pool_scale": 1.0 + nrm(ks[15], (DEPTH, POOL_WIDTH), 0.1),
        "w_out": nrm(ks[16], (DEPTH, D_MIX, D_MODEL), BETA * D_MIX ** -0.5),
        "ln1_g": 1.0 + nrm(ks[17], (DEPTH, D_MODEL), 0.1),
        "ln1_b": nrm(ks[18], (DEPTH, D_MODEL), 0.02),
        "ffn_w_up": nrm(ks[19], (DEPTH, D_MODEL, 2 * D_FF), D_MODEL ** -0.5),
        "ffn_conv_w": nrm(ks[20], (DEPTH, FFN_CONV, FFN_CONV, 2 * D_FF), 1.0 / FFN_CONV),
        "ffn_conv_b": nrm(ks[21], (DEPTH, 2 * D_FF), 0.02),
        "ffn_w_down": nrm(ks[22], (DEPTH, D_FF, D_MODEL), BETA * D_FF ** -0.5),
        "ln2_g": 1.0 + nrm(ks[23], (DEPTH, D_MODEL), 0.1),
        "ln2_b": nrm(ks[24], (DEPTH, D_MODEL), 0.02),
    }

def first_block(x, c, ctx, c_ctx, w_ada, b_ada, w_in, ssd_conv_w, ssd_conv_b, ssd_dt_bias, ssd_a_log, ssd_d,
              ssd_norm_w, fnet_w, pool_w, pool_scale, w_out, ln1_g, ln1_b, ffn_w_up, ffn_conv_w, ffn_conv_b,
              ffn_w_down, ln2_g, ln2_b):
    bsz = x.shape[0]
    zero_state = jnp.zeros((bsz, SSD_HEADS, SSD_HEADDIM, SSD_STATE), jnp.float32)
    for l in range(DEPTH):
        last = l == DEPTH - 1
        sh1, sc1, g1, sh2, sc2, g2 = ada(c, w_ada[l], b_ada[l])
        csh1, csc1, cg1, csh2, csc2, cg2 = ada(c_ctx[None, :], w_ada[l], b_ada[l])
        mixer_p = (ssd_conv_w[l], ssd_conv_b[l], ssd_dt_bias[l], ssd_a_log[l], ssd_d[l], ssd_norm_w[l],
                   fnet_w[l], pool_w[l], pool_scale[l], w_out[l])
        u_ctx = modulate(ctx, csh1, csc1) @ w_in[l]
        u_lat = modulate(x, sh1, sc1) @ w_in[l]
        if last:
            s_f, s_b = ctx_scan_states(u_ctx, ssd_conv_w[l], ssd_conv_b[l], ssd_dt_bias[l], ssd_a_log[l])
        else:
            mix_ctx, s_f, s_b = token_mixer(u_ctx, zero_state, zero_state, *mixer_p)
        mix_lat, _, _ = token_mixer(u_lat, s_f, s_b, *mixer_p)
        x = post_norm(x, mix_lat, g1, ln1_g[l], ln1_b[l])
        ffn_lat = conv_ffn(modulate(x, sh2, sc2), ffn_w_up[l], ffn_conv_w[l], ffn_conv_b[l], ffn_w_down[l], True)
        x = post_norm(x, ffn_lat, g2, ln2_g[l], ln2_b[l])
        if not last:
            ctx = post_norm(ctx, mix_ctx, cg1, ln1_g[l], ln1_b[l])
            ffn_ctx = conv_ffn(modulate(ctx, csh2, csc2), ffn_w_up[l], ffn_conv_w[l], ffn_conv_b[l], ffn_w_down[l], False)
            ctx = post_norm(ctx, ffn_ctx, cg2, ln2_g[l], ln2_b[l])
    return x


DEPTH_2 = 2

BLOCK = 128
WINDOW = 128
ROPE_BASE = 10000.0
N_MOD = 6
D_FF_2 = 4 * D_MODEL

A_HEADS = 4
A_HEAD_DIM = D_MODEL // 8
A_WIDTH = A_HEADS * A_HEAD_DIM
A_GATES = 4 * A_HEADS
B_HEADS = 8
B_KV_HEADS = 2
B_HEAD_DIM = D_MODEL // 16
B_WIDTH = B_HEADS * B_HEAD_DIM
B_KV_WIDTH = B_KV_HEADS * B_HEAD_DIM
AB_IN = 4 * A_WIDTH + A_GATES + B_WIDTH + 2 * B_KV_WIDTH
AB_OUT = A_WIDTH + B_WIDTH
C_HEADS = 8
C_KV_HEADS = 2
C_HEAD_DIM = D_MODEL // 8
C_WIDTH = C_HEADS * C_HEAD_DIM
C_KV_WIDTH = C_KV_HEADS * C_HEAD_DIM
C_IN = C_WIDTH + 2 * C_KV_WIDTH


def rms_norm(x, g):
    xf = x.astype(jnp.float32)
    y = xf * lax.rsqrt(jnp.mean(xf * xf, axis=-1, keepdims=True) + EPS)
    return (y * g.astype(jnp.float32)).astype(x.dtype)

def modulate_2(x, g, mod, i):
    return rms_norm(x, g) * (1 + mod[:, :, i + 1]) + mod[:, :, i]

def sq_relu_mlp(h, w1, w2):
    return jnp.square(jax.nn.relu(h @ w1)) @ w2

def axial_rope_tables(n_tokens, head_dim):
    rows = n_tokens // GRID_W
    row = jnp.broadcast_to(jnp.arange(rows)[:, None], (rows, GRID_W)).reshape(n_tokens).astype(jnp.float32)
    col = jnp.broadcast_to(jnp.arange(GRID_W)[None, :], (rows, GRID_W)).reshape(n_tokens).astype(jnp.float32)
    pairs_per_axis = head_dim // 4
    inv_freq = ROPE_BASE ** (-jnp.arange(pairs_per_axis, dtype=jnp.float32) / pairs_per_axis)
    ang = jnp.concatenate([row[:, None] * inv_freq, col[:, None] * inv_freq], axis=-1)
    return jnp.cos(ang), jnp.sin(ang)

def apply_rope(x, cos, sin):
    half = x.shape[-1] // 2
    xf = x.astype(jnp.float32)
    x1, x2 = xf[..., :half], xf[..., half:]
    cs, sn = cos[:, None, :], sin[:, None, :]
    return jnp.concatenate([x1 * cs - x2 * sn, x2 * cs + x1 * sn], axis=-1).astype(x.dtype)

def gqa_attend(q, k, v, sink=None):
    b, tq, hq, d = q.shape
    hkv = k.shape[2]
    g = hq // hkv
    s = jnp.einsum('bqhgd,bkhd->bhgqk', q.reshape(b, tq, hkv, g, d), k).astype(jnp.float32) * d ** -0.5
    if sink is None:
        p = jax.nn.softmax(s, axis=-1)
    else:
        s_sink = jnp.broadcast_to(sink.astype(jnp.float32).reshape(1, hkv, g, 1, 1), s.shape[:-1] + (1,))
        p = jax.nn.softmax(jnp.concatenate([s, s_sink], axis=-1), axis=-1)[..., :-1]
    o = jnp.einsum('bhgqk,bkhd->bqhgd', p.astype(v.dtype), v)
    return o.reshape(b, tq, hq * d)

def banded_window_attention(q, k, v, k_ctx, v_ctx, sink):
    b, t, hq, d = q.shape
    hkv = k.shape[2]
    g = hq // hkv
    nb = t // BLOCK
    n_ctx = k_ctx.shape[1]
    nw = 3 * BLOCK
    scale = d ** -0.5
    qb = jnp.moveaxis(q.reshape(b, nb, BLOCK, hkv, g, d), 1, 0)

    def band(a):
        a = jnp.pad(a, ((0, 0), (BLOCK, BLOCK), (0, 0), (0, 0))).reshape(b, nb + 2, BLOCK, hkv, d)
        a = jnp.concatenate([a[:, :-2], a[:, 1:-1], a[:, 2:]], axis=2)
        return jnp.moveaxis(a, 1, 0)

    kw, vw = band(k), band(v)
    qpos = jnp.arange(nb)[:, None, None] * BLOCK + jnp.arange(BLOCK)[None, :, None]
    kpos = (jnp.arange(nb)[:, None, None] - 1) * BLOCK + jnp.arange(nw)[None, None, :]
    valid = (jnp.abs(kpos - qpos) <= WINDOW) & (kpos >= 0) & (kpos < t)
    sink_l = sink.astype(jnp.float32).reshape(1, hkv, g, 1, 1)

    def one_block(args):
        qn, kn, vn, valid_n = args
        s_win = jnp.einsum('bqhgd,bkhd->bhgqk', qn, kn).astype(jnp.float32) * scale
        s_win = jnp.where(valid_n, s_win, -jnp.inf)
        s_ctx = jnp.einsum('bqhgd,bchd->bhgqc', qn, k_ctx).astype(jnp.float32) * scale
        s_sink = jnp.broadcast_to(sink_l, s_win.shape[:-1] + (1,))
        p = jax.nn.softmax(jnp.concatenate([s_win, s_ctx, s_sink], axis=-1), axis=-1).astype(v.dtype)
        o = (jnp.einsum('bhgqk,bkhd->bqhgd', p[..., :nw], vn)
             + jnp.einsum('bhgqc,bchd->bqhgd', p[..., nw:nw + n_ctx], v_ctx))
        return o.reshape(b, BLOCK, hq * d)

    o = lax.map(one_block, (qb, kw, vw, valid))
    return jnp.moveaxis(o, 0, 1).reshape(b, t, hq * d)

def mlstm_dir(q, k, v, log_i, log_f, state):
    n_chunks = q.shape[2] // BLOCK

    def to_chunks(a):
        a = a.reshape(a.shape[:2] + (n_chunks, BLOCK) + a.shape[3:])
        return jnp.moveaxis(a, 2, 0)

    lower = jnp.tril(jnp.ones((BLOCK, BLOCK), dtype=bool))

    def step(carry, inp):
        c_mat, n_vec, m = carry
        qc, kc, vc, ic, fc = inp
        bcum = jnp.cumsum(fc, axis=-1)
        d_log = jnp.where(lower, bcum[..., :, None] - bcum[..., None, :] + ic[..., None, :], -jnp.inf)
        inter_log = bcum + m[..., None]
        m_t = jnp.maximum(inter_log, jnp.max(d_log, axis=-1))
        inter_w = jnp.exp(inter_log - m_t)
        s = jnp.einsum('bhtd,bhsd->bhts', qc, kc) * jnp.exp(d_log - m_t[..., None])
        num = inter_w[..., None] * jnp.einsum('bhtd,bhde->bhte', qc, c_mat) + jnp.einsum('bhts,bhse->bhte', s, vc)
        den = inter_w * jnp.einsum('bhtd,bhd->bht', qc, n_vec) + jnp.sum(s, axis=-1)
        h = num / jnp.maximum(jnp.abs(den), jnp.exp(-m_t))[..., None]
        b_last = bcum[..., -1]
        w_log = b_last[..., None] - bcum + ic
        m_new = jnp.maximum(b_last + m, jnp.max(w_log, axis=-1))
        carry_w = jnp.exp(b_last + m - m_new)
        w = jnp.exp(w_log - m_new[..., None])
        c_new = carry_w[..., None, None] * c_mat + jnp.einsum('bhs,bhsd,bhse->bhde', w, kc, vc)
        n_new = carry_w[..., None] * n_vec + jnp.einsum('bhs,bhsd->bhd', w, kc)
        return (c_new, n_new, m_new), h

    state, h = lax.scan(step, state, (to_chunks(q), to_chunks(k), to_chunks(v), to_chunks(log_i), to_chunks(log_f)))
    h = jnp.moveaxis(h, 0, 2)
    return h.reshape(h.shape[:2] + (-1, h.shape[-1])), state

def mlstm_bidir(q, k, v, gates, state_f, state_b):
    li_f, lf_f, li_b, lf_b = gates
    h_f, st_f = mlstm_dir(q, k, v, li_f, lf_f, state_f)
    flip = lambda a: jnp.flip(a, axis=2)
    h_b, st_b = mlstm_dir(flip(q), flip(k), flip(v), flip(li_b), flip(lf_b), state_b)
    return h_f + flip(h_b), st_f, st_b

def ab_mixer(h_ctx, h_lat, w_in, gate_b, a_norm_g, q_norm_g, k_norm_g, sink, w_out, need_ctx):
    batch = h_lat.shape[0]
    sizes = [A_WIDTH] * 4 + [A_GATES, B_WIDTH, B_KV_WIDTH]
    bounds = [int(s) for s in np.cumsum(sizes)]

    def project(h):
        t = h.shape[1]
        qa, ka, va, oa, ga, qb, kb, vb = jnp.split(h @ w_in, bounds, axis=-1)
        heads_a = lambda a: a.reshape(batch, t, A_HEADS, A_HEAD_DIM).transpose(0, 2, 1, 3).astype(jnp.float32)
        qa, ka, va = heads_a(qa), heads_a(ka) * A_HEAD_DIM ** -0.5, heads_a(va)
        g = (ga + gate_b).astype(jnp.float32).reshape(batch, t, 4, A_HEADS).transpose(2, 0, 3, 1)
        gates = (g[0], jax.nn.log_sigmoid(g[1]), g[2], jax.nn.log_sigmoid(g[3]))
        qb = rms_norm(qb.reshape(batch, t, B_HEADS, B_HEAD_DIM), q_norm_g)
        kb = rms_norm(kb.reshape(batch, t, B_KV_HEADS, B_HEAD_DIM), k_norm_g)
        vb = vb.reshape(batch, t, B_KV_HEADS, B_HEAD_DIM)
        return (qa, ka, va, gates), oa, (qb, kb, vb)

    def mlstm_out(h, oa):
        h = rms_norm(h.transpose(0, 2, 1, 3), a_norm_g.reshape(A_HEADS, A_HEAD_DIM))
        return (h.reshape(h.shape[0], h.shape[1], A_WIDTH) * jax.nn.sigmoid(oa)).astype(oa.dtype)

    a_c, oa_c, (qb_c, kb_c, vb_c) = project(h_ctx)
    a_l, oa_l, (qb_l, kb_l, vb_l) = project(h_lat)
    zero = (jnp.zeros((batch, A_HEADS, A_HEAD_DIM, A_HEAD_DIM), jnp.float32),
            jnp.zeros((batch, A_HEADS, A_HEAD_DIM), jnp.float32),
            jnp.zeros((batch, A_HEADS), jnp.float32))
    ha_c, st_f, st_b = mlstm_bidir(*a_c, zero, zero)
    ha_l, _, _ = mlstm_bidir(*a_l, st_f, st_b)
    cos, sin = axial_rope_tables(h_lat.shape[1], B_HEAD_DIM)
    qb_l, kb_l = apply_rope(qb_l, cos, sin), apply_rope(kb_l, cos, sin)
    ob_l = banded_window_attention(qb_l, kb_l, vb_l, kb_c, vb_c, sink)
    y_lat = jnp.concatenate([mlstm_out(ha_l, oa_l), ob_l.astype(oa_l.dtype)], axis=-1) @ w_out
    y_ctx = None
    if need_ctx:
        ob_c = gqa_attend(qb_c, kb_c, vb_c, sink)
        y_ctx = jnp.concatenate([mlstm_out(ha_c, oa_c), ob_c.astype(oa_c.dtype)], axis=-1) @ w_out
    return y_ctx, y_lat

def c_mixer(h_ctx, h_lat, w_in, q_norm_g, k_norm_g, w_out, need_ctx):
    def project(h):
        b, t, _ = h.shape
        q, k, v = jnp.split(h @ w_in, [C_WIDTH, C_WIDTH + C_KV_WIDTH], axis=-1)
        q = rms_norm(q.reshape(b, t, C_HEADS, C_HEAD_DIM), q_norm_g)
        k = rms_norm(k.reshape(b, t, C_KV_HEADS, C_HEAD_DIM), k_norm_g)
        return q, k, v.reshape(b, t, C_KV_HEADS, C_HEAD_DIM)

    q_c, k_c, v_c = project(h_ctx)
    q_l, k_l, v_l = project(h_lat)
    b, t = h_lat.shape[:2]
    cos, sin = axial_rope_tables(t, C_HEAD_DIM)
    q_l, k_l = apply_rope(q_l, cos, sin), apply_rope(k_l, cos, sin)
    k_all = jnp.concatenate([k_c, k_l], axis=1)
    v_all = jnp.concatenate([v_c, v_l], axis=1)
    q_blocks = jnp.moveaxis(q_l.reshape(b, t // BLOCK, BLOCK, C_HEADS, C_HEAD_DIM), 1, 0)
    o = lax.map(lambda qb: gqa_attend(qb, k_all, v_all), q_blocks)
    y_lat = jnp.moveaxis(o, 0, 1).reshape(b, t, C_WIDTH) @ w_out
    y_ctx = gqa_attend(q_c, k_c, v_c) @ w_out if need_ctx else None
    return y_ctx, y_lat

def second_inputs(seed: int = 0) -> dict:
    key = jax.random.key(seed)
    ks = jax.random.split(key, 24)
    n_even = (DEPTH_2 + 1) // 2
    n_odd = DEPTH_2 // 2
    f32 = jnp.float32
    nrm = lambda k, shape, scale: jax.random.normal(k, shape, f32) * scale
    gain = lambda k, shape: 1.0 + 0.05 * jax.random.normal(k, shape, f32)
    gate_b = jnp.concatenate([
        nrm(ks[9], (n_even, A_HEADS), 0.1),
        jax.random.uniform(ks[10], (n_even, A_HEADS), f32, 3.0, 6.0),
        nrm(ks[11], (n_even, A_HEADS), 0.1),
        jax.random.uniform(ks[12], (n_even, A_HEADS), f32, 3.0, 6.0)], axis=-1)
    return {
        'x': nrm(ks[0], (BATCH, SEQ, D_MODEL), 1.0),
        'c': nrm(ks[1], (BATCH, D_MODEL), 1.0),
        'ctx': nrm(ks[2], (BATCH, CTX_LEN, D_MODEL), 1.0),
        'c_ctx': nrm(ks[3], (D_MODEL,), 1.0),
        'ada_w': nrm(ks[4], (DEPTH_2, D_MODEL, N_MOD * D_MODEL), 0.5 * D_MODEL ** -0.5),
        'ada_b': nrm(ks[5], (DEPTH_2, N_MOD * D_MODEL), 0.02),
        'norm1_g': gain(ks[6], (DEPTH_2, D_MODEL)),
        'norm2_g': gain(ks[7], (DEPTH_2, D_MODEL)),
        'ab_w_in': nrm(ks[8], (n_even, D_MODEL, AB_IN), D_MODEL ** -0.5),
        'ab_gate_b': gate_b,
        'mlstm_norm_g': gain(ks[13], (n_even, A_WIDTH)),
        'swa_q_norm_g': gain(ks[14], (n_even, B_HEAD_DIM)),
        'swa_k_norm_g': gain(ks[15], (n_even, B_HEAD_DIM)),
        'swa_sink': nrm(ks[16], (n_even, B_HEADS), 0.5),
        'ab_w_out': nrm(ks[17], (n_even, AB_OUT, D_MODEL), AB_OUT ** -0.5),
        'c_w_in': nrm(ks[18], (n_odd, D_MODEL, C_IN), D_MODEL ** -0.5),
        'c_q_norm_g': gain(ks[19], (n_odd, C_HEAD_DIM)),
        'c_k_norm_g': gain(ks[20], (n_odd, C_HEAD_DIM)),
        'c_w_out': nrm(ks[21], (n_odd, C_WIDTH, D_MODEL), C_WIDTH ** -0.5),
        'mlp_w1': nrm(ks[22], (DEPTH_2, D_MODEL, D_FF_2), D_MODEL ** -0.5),
        'mlp_w2': nrm(ks[23], (DEPTH_2, D_FF_2, D_MODEL), D_FF_2 ** -0.5),
    }

def second_block(x, c, ctx, c_ctx, ada_w, ada_b, norm1_g, norm2_g, ab_w_in, ab_gate_b, mlstm_norm_g,
              swa_q_norm_g, swa_k_norm_g, swa_sink, ab_w_out, c_w_in, c_q_norm_g, c_k_norm_g, c_w_out,
              mlp_w1, mlp_w2):
    batch = x.shape[0]
    for layer in range(DEPTH_2):
        last = layer == DEPTH_2 - 1
        mod_l = (jax.nn.silu(c) @ ada_w[layer] + ada_b[layer]).reshape(batch, 1, N_MOD, D_MODEL)
        mod_c = (jax.nn.silu(c_ctx) @ ada_w[layer] + ada_b[layer]).reshape(1, 1, N_MOD, D_MODEL)
        h_l = modulate_2(x, norm1_g[layer], mod_l, 0)
        h_c = modulate_2(ctx, norm1_g[layer], mod_c, 0)
        j = layer // 2
        if layer % 2 == 0:
            y_c, y_l = ab_mixer(h_c, h_l, ab_w_in[j], ab_gate_b[j], mlstm_norm_g[j], swa_q_norm_g[j],
                                swa_k_norm_g[j], swa_sink[j], ab_w_out[j], not last)
        else:
            y_c, y_l = c_mixer(h_c, h_l, c_w_in[j], c_q_norm_g[j], c_k_norm_g[j], c_w_out[j], not last)
        x = x + mod_l[:, :, 2] * y_l
        x = x + mod_l[:, :, 5] * sq_relu_mlp(modulate_2(x, norm2_g[layer], mod_l, 3), mlp_w1[layer], mlp_w2[layer])
        if not last:
            ctx = ctx + mod_c[:, :, 2] * y_c
            ctx = ctx + mod_c[:, :, 5] * sq_relu_mlp(modulate_2(ctx, norm2_g[layer], mod_c, 3), mlp_w1[layer], mlp_w2[layer])
    return x


def setup_inputs(seed=0):
    out = dict(first_inputs(seed))
    for name, value in second_inputs(seed + 1).items():
        if name != "x":
            out[name + "_2"] = value
    return out


def reference(
    x, c, ctx, c_ctx, w_ada, b_ada, w_in, ssd_conv_w, ssd_conv_b, ssd_dt_bias, ssd_a_log, ssd_d,
    ssd_norm_w, fnet_w, pool_w, pool_scale, w_out, ln1_g, ln1_b, ffn_w_up, ffn_conv_w,
    ffn_conv_b, ffn_w_down, ln2_g, ln2_b, c_2, ctx_2, c_ctx_2, ada_w_2, ada_b_2, norm1_g_2,
    norm2_g_2, ab_w_in_2, ab_gate_b_2, mlstm_norm_g_2, swa_q_norm_g_2, swa_k_norm_g_2,
    swa_sink_2, ab_w_out_2, c_w_in_2, c_q_norm_g_2, c_k_norm_g_2, c_w_out_2, mlp_w1_2, mlp_w2_2,
):
    x = first_block(
        x, c, ctx, c_ctx, w_ada, b_ada, w_in, ssd_conv_w, ssd_conv_b, ssd_dt_bias, ssd_a_log,
        ssd_d, ssd_norm_w, fnet_w, pool_w, pool_scale, w_out, ln1_g, ln1_b, ffn_w_up,
        ffn_conv_w, ffn_conv_b, ffn_w_down, ln2_g, ln2_b,
    )
    return second_block(
        x, c_2, ctx_2, c_ctx_2, ada_w_2, ada_b_2, norm1_g_2, norm2_g_2, ab_w_in_2, ab_gate_b_2,
        mlstm_norm_g_2, swa_q_norm_g_2, swa_k_norm_g_2, swa_sink_2, ab_w_out_2, c_w_in_2,
        c_q_norm_g_2, c_k_norm_g_2, c_w_out_2, mlp_w1_2, mlp_w2_2,
    )


_drawn_inputs = setup_inputs


def setup_inputs(seed=0):
    import zlib

    import numpy as np

    out = dict(_drawn_inputs(seed))
    spreads = {}
    factors = {'ctx': 8.0,
     'c_ctx': 8.0,
     'b_ada': 3.841,
     'ssd_conv_b': 8.0,
     'ssd_d': 8.0,
     'ssd_norm_w': 4.563,
     'pool_scale': 7.954,
     'ffn_conv_b': 8.0,
     'norm1_g_2': 3.568,
     'mlstm_norm_g_2': 8.0,
     'swa_q_norm_g_2': 8.0,
     'swa_k_norm_g_2': 8.0,
     'swa_sink_2': 8.0,
     'c_q_norm_g_2': 8.0,
     'c_k_norm_g_2': 8.0}
    for name, (base, spread) in spreads.items():
        noise = np.random.default_rng([zlib.crc32(name.encode()), seed]).standard_normal(out[name].shape)
        drawn = base * np.exp(spread * noise) if base else spread * noise
        out[name] = __import__('jax').numpy.asarray(drawn.astype(out[name].dtype))
    for name, factor in factors.items():
        out[name] = (out[name] * factor).astype(out[name].dtype)
    return out
```

```python
from contextlib import ExitStack

import numpy as np
import concourse.bass as bass
from concourse import mybir

F32 = mybir.dt.float32
ALU = mybir.AluOpType
ACT = mybir.ActivationFunctionType
AX_X = mybir.AxisListType.X

P = 128
D = 1024
KT = D // P
LAT, CTX = 512, 256
TOK = LAT + CTX
CH = 128
NLAT, NCTX = LAT // CH, CTX // CH
NCH = NLAT + NCTX
BOTH = [(0, LAT), (LAT, CTX)]
ONLY_LAT = [(0, LAT)]
GRID_W = 64
GRID_H = LAT // GRID_W
EPS = 1e-6
ALPHA = 2.0 ** 0.25

SLAB = 256
NS = 4
D_FF = 2816
FT = D_FF // P
D_FF2 = 4096
MT = D_FF2 // P
OFF_XBC, OFF_DT, OFF_FNET, OFF_POOL = 512, 1536, 1552, 1808
N_CONV = 8
A_HEADS = 4
B_HEADS = 8
AB_O, AB_G, AB_QB, AB_KB = 1536, 2048, 2064, 2576

(IDENT, ONES, BLK64, U_LE, U_GE, ROT32, ROT64, SWAP, M_PREV, M_NEXT, DFT_C, DFT_S, SEL, TINY) = range(14)
N_MATS = SEL + A_HEADS + 1
TINY = SEL + A_HEADS
T_CB, T_SB, T_CC, T_SC, T_CNT = 0, 1, 2, 3, 4
NEG = -1e30


def shape_constants():
    i = np.arange(P)
    m = np.zeros((N_MATS, P, P), np.float64)
    m[IDENT] = np.eye(P)
    m[ONES] = 1
    m[BLK64] = i[:, None] // 64 == i[None, :] // 64
    m[U_LE] = i[:, None] <= i[None, :]
    m[U_GE] = i[:, None] >= i[None, :]
    for n, half in ((ROT32, 32), (ROT64, 64)):
        for f in range(P):
            up = f % (2 * half) < half
            m[n, f + half if up else f - half, f] = -1 if up else 1
    m[SWAP] = np.roll(np.eye(P), 64, axis=0)
    m[M_PREV] = np.where(i[None, :] >= i[:, None], 0, NEG)
    m[M_NEXT] = np.where(i[None, :] <= i[:, None], 0, NEG)
    ang = 2 * np.pi * ((i[:, None] * i[None, :]) % 64) / 64
    ortho = 1 / np.sqrt(LAT * 64)
    m[DFT_C] = m[BLK64] * np.cos(ang) * ortho
    m[DFT_S] = -m[BLK64] * np.sin(ang) * ortho
    for h in range(A_HEADS):
        m[SEL + h, h] = 1
    m[TINY, :, 0] = EPS
    t = np.zeros((6, P, LAT), np.float64)
    pos = np.arange(LAT)
    for n, head in ((T_CB, 64), (T_CC, 128)):
        pairs = head // 4
        inv = (np.float32(10000.0) ** (-np.arange(pairs, dtype=np.float32) / pairs)).astype(np.float32)
        ang = np.concatenate([(pos // GRID_W)[:, None].astype(np.float32) * inv,
                              (pos % GRID_W)[:, None].astype(np.float32) * inv], axis=1).T.astype(np.float64)
        ang = np.tile(ang, (P // (head // 2), 1))
        t[n], t[n + 1] = np.cos(ang), np.sin(ang)
    for g, win in enumerate((2, 4, 8, 16)):
        left = win // 2
        hi, lo = np.minimum(pos + win - left, LAT), np.maximum(pos - left, 0)
        t[T_CNT + g // 2, (g % 2) * 64:(g % 2) * 64 + 64] = 1.0 / (hi - lo)
    ang = 2 * np.pi * ((pos[:, None] * pos[None, :]) % LAT) / LAT
    dft = np.stack([np.cos(ang), np.sin(ang)])
    return m.astype(np.float32), t.astype(np.float32), dft.astype(np.float32)


class Tally:

    def __init__(self, sem):
        self.sem, self.base = sem, 0

    def at(self, n):
        return self.base + n

    def close(self, n):
        self.base += n


class Order:

    def __init__(self, sem):
        self.sem, self.n = sem, 0

    def mark(self, ins):
        ins.then_inc(self.sem, 1)
        self.n += 1
        return self.n

    def step(self, eng, ins):
        eng.wait_ge(self.sem, self.mark(ins))


def program(nc, w, out, stop=None, dumps=None):
    ctx = ExitStack()
    with ctx:
        def sb(name, shape):
            return ctx.enter_context(nc.sbuf_tensor(name, shape, F32))

        def tally(name):
            return Tally(ctx.enter_context(nc.semaphore(name)))

        def order(name):
            return Order(ctx.enter_context(nc.semaphore(name)))

        xT = sb("xT", [P, KT, TOK])
        hT = sb("hT", [P, KT, TOK])
        ring = sb("ring", [P, NS, KT, SLAB])
        big = sb("big", [P, 24576])
        mean = sb("mean", [P, TOK])
        rstd = sb("rstd", [P, TOK])
        squares = sb("squares", [P, 3, LAT])
        mats = sb("mats", [P, N_MATS, P])
        cols = sb("cols", [P, 768])
        mod = sb("mod", [P, 48, 2])
        scl = sb("scl", [P, 2, 8, 2])
        sil = sb("sil", [P, 2, 8, 2])
        rows = sb("rows", [P, 64])
        dskip = sb("dskip", [P, 4])
        small = sb("small", [P, 512])
        wnarrow = sb("wnarrow", [P, KT, 16])
        ps = ctx.enter_context(nc.psum_tensor("ps", [P, 8, 512], F32))

        ident, ones, blk64 = mats[:, IDENT, :], mats[:, ONES, :], mats[:, BLK64, :]
        eps_col = mats[:, TINY, 0:1]

        slot_loaded = [ctx.enter_context(nc.semaphore(f"slot_loaded{s}")) for s in range(NS)]
        mm_done = ctx.enter_context(nc.semaphore("mm_done"))
        loaded = tally("loaded")
        stored = tally("stored")
        mm_free = tally("mm_free")
        tr_ready, tr_free_v, tr_free_a = tally("tr_ready"), tally("tr_free_v"), tally("tr_free_a")
        v_order, a_order, g_order = order("v_order"), order("a_order"), order("g_order")
        N = {n: tally("norm_" + n) for n in ("sum", "mean", "centered", "sq", "sq_used", "std", "scaled")}
        S = {}

        def named(*names):
            for n in names:
                if n not in S:
                    S[n] = tally(n)
            return {n: S[n] for n in names}


        stream = []
        signals = [0]

        def add_slabs(name, layer, row_groups, col_starts, n_signals):
            first = len(stream)
            for j, c in enumerate(col_starts):
                for r0, kt in row_groups:
                    stream.append((name, layer, r0, kt, c))
                    signals.append(signals[-1] + (n_signals[j] if isinstance(n_signals, list) else n_signals))
            return first

        whole = [(0, KT)]
        cols_of = lambda start, n: [start + SLAB * i for i in range(n)]
        W = {}
        W["ada"] = add_slabs("w_ada", 0, whole, cols_of(0, 24), 1)
        W["in"] = add_slabs("w_in", 0, whole, cols_of(OFF_XBC, 4) + cols_of(0, 2) + [OFF_FNET, OFF_POOL],
                            [4, 4, 4, 2, 2, 2, 2, 2])
        W["out"] = add_slabs("w_out", 0, whole, cols_of(0, 4), 2)
        W["up"] = add_slabs("ffn_w_up", 0, whole, [c for j in range(FT // 2) for c in (SLAB * j, D_FF + SLAB * j)],
                            2)
        DOWN_ROWS = [(0, 8), (1024, 8), (2048, 6)]
        W["down"] = add_slabs("ffn_w_down", 0, DOWN_ROWS, cols_of(0, 4), 2)
        W["ada0"] = add_slabs("ada_w_2", 0, whole, cols_of(0, 24), 1)
        W["ab"] = add_slabs("ab_w_in_2", 0, whole,
                            cols_of(0, 4) + cols_of(1024, 4) + cols_of(AB_QB, 2) + [AB_KB],
                            [4] * 4 + [NCH] * 2 + [4] * 2 + [4] * 2 + [2 + NCH])
        W["ab_out"] = add_slabs("ab_w_out_2", 0, whole, cols_of(0, 4), 4)
        MLP_ROWS = [(1024 * g, 8) for g in range(4)]
        W["w1_0"] = add_slabs("mlp_w1_2", 0, whole, cols_of(0, 16), 4)
        W["w2_0"] = add_slabs("mlp_w2_2", 0, MLP_ROWS, cols_of(0, 4), 4)
        W["ada1"] = add_slabs("ada_w_2", 1, whole, cols_of(0, 24), 1)
        W["c"] = add_slabs("c_w_in_2", 0, whole, cols_of(0, 6), [2] * 4 + [4, NCH])
        W["c_out"] = add_slabs("c_w_out_2", 0, whole, cols_of(0, 4), 2)
        W["w1_1"] = add_slabs("mlp_w1_2", 1, whole, cols_of(0, 16), 2)
        W["w2_1"] = add_slabs("mlp_w2_2", 1, MLP_ROWS, cols_of(0, 4), 2)
        issued = [0]

        def slab_source(entry, shift=0):
            name, layer, r0, kt, c = entry
            m = w[name][layer, r0:r0 + kt * P, :].rearrange("(k p) n -> p k n", p=P)
            return m[:, :, bass.ds(c + shift, SLAB)] if not isinstance(shift, int) or shift else m[:, :, c:c + SLAB]

        def load_slabs(sp, upto):
            upto = min(upto, len(stream))
            n = issued[0]

            def one(n, i=None, delta=0, per_turn=0):
                if n >= NS:
                    used = signals[n - NS + 1]
                    sp.wait_ge(mm_done, used if i is None else i * per_turn + used)
                kt = stream[n][3]
                src = slab_source(stream[n], 0 if i is None else i * delta)
                sp.dma_start(ring[:, n % NS, 0:kt, :], src).then_inc(slot_loaded[n % NS], 16)

            while n < upto:
                group = stream[n:n + NS]
                reps, delta = 1, 0
                if n >= NS and n + 2 * NS <= upto:
                    delta = stream[n + NS][4] - stream[n][4]
                    per_turn = signals[n] - signals[n - NS]
                    while n + NS * (reps + 1) <= upto and all(
                            signals[n + NS * (reps - 1) + s + 1] == signals[n - NS + s + 1] + per_turn * reps and
                            stream[n + NS * reps + s] == (*group[s][:4], group[s][4] + delta * reps)
                            for s in range(NS)):
                        reps += 1
                if reps >= 3:
                    with sp.Fori(0, reps) as i:
                        for s in range(NS):
                            one(n + s, i, delta, per_turn)
                    n += NS * reps
                else:
                    one(n)
                    n += 1
            issued[0] = n

        def wait_slab(pe, n, i=None, slabs_per_turn=0):
            v = 16 * (n // NS + 1)
            pe.wait_ge(slot_loaded[n % NS], v if i is None else i * (16 * slabs_per_turn // NS) + v)

        def turns(eng, count, period, body, peel=0):
            n = count // period
            for j in range(peel * period):
                body(None, j)
            if n - peel >= 2:
                with eng.Fori(peel, n) as i:
                    for j in range(period):
                        body(i, j)
            else:
                for j in range(peel * period, n * period):
                    body(None, j)
            for j in range(n * period, count):
                body(None, j)

        def at(i, period, j):
            return j if i is None else i * period + j

        def transpose_pe(pe, groups):
            for u, (srcs, _) in enumerate(groups):
                if u >= 8:
                    t = (tr_free_v, tr_free_a)[u % 2]
                    pe.wait_ge(t.sem, t.at((u - 8) // 2 + 1))
                for j, s in enumerate(srcs):
                    f, p = s.shape[1], s.shape[0]
                    ins = pe.transpose(ps[0:f, u % 8, j * p:(j + 1) * p], s, ident[0:p, 0:p])
                ins.then_inc(tr_ready.sem, 1)

        def transpose_out(eng, groups, which):
            t = (tr_free_v, tr_free_a)[which]
            for u, (srcs, dst) in enumerate(groups):
                if u % 2 != which:
                    continue
                eng.wait_ge(tr_ready.sem, tr_ready.at(u + 1))
                f, p = srcs[0].shape[1], srcs[0].shape[0]
                src = ps[0:f, u % 8, 0:p * len(srcs)]
                if which:
                    nc.scalar.copy(dst, src).then_inc(t.sem, 1)
                else:
                    nc.vector.tensor_copy(dst, src).then_inc(t.sem, 1)

        def transpose_close(groups):
            tr_ready.close(len(groups))
            tr_free_v.close((len(groups) + 1) // 2)
            tr_free_a.close(len(groups) // 2)

        def norm_stage(centre, ranges, src, dst, scale, shift):
            n_r, n_sq = len(ranges), squares.shape[1]
            with nc.Block() as block:
                @block.sync
                def _(sp):
                    load_slabs(sp, done[0] + NS)

                @block.tensor
                def _(pe):
                    if centre:
                        for r, (t0, n) in enumerate(ranges):
                            for k in range(KT):
                                ins = pe.matmul(ps[:, r, 0:n], ones, src[:, k, t0:t0 + n],
                                                start=(k == 0), stop=(k == KT - 1))
                            ins.then_inc(N["sum"].sem, 1)
                    for r, (t0, n) in enumerate(ranges):
                        for k in range(KT):
                            u = r * KT + k
                            pe.wait_ge(N["sq"].sem, N["sq"].at(u + 1))
                            pe.matmul(ps[:, 2 + r, 0:n], ones, squares[:, u % n_sq, 0:n],
                                      start=(k == 0), stop=(k == KT - 1)).then_inc(N["sq_used"].sem, 1)

                @block.scalar
                def _(act):
                    if centre:
                        for r, (t0, n) in enumerate(ranges):
                            act.wait_ge(N["sum"].sem, N["sum"].at(r + 1))
                            act.activation(mean[:, t0:t0 + n], ps[:, r, 0:n], ACT.Copy, scale=1.0 / D)\
                               .then_inc(N["mean"].sem, 1)
                    for r, (t0, n) in enumerate(ranges):
                        for k in range(KT):
                            u = r * KT + k
                            if centre:
                                act.wait_ge(N["centered"].sem, N["centered"].at(u + 1))
                            if u >= n_sq:
                                act.wait_ge(N["sq_used"].sem, N["sq_used"].at(u - n_sq + 1))
                            act.activation(squares[:, u % n_sq, 0:n],
                                           (dst if centre else src)[:, k, t0:t0 + n], ACT.Square)\
                               .then_inc(N["sq"].sem, 1)
                    for r, (t0, n) in enumerate(ranges):
                        act.wait_ge(N["sq_used"].sem, N["sq_used"].at((r + 1) * KT))
                        act.activation(rstd[:, t0:t0 + n], ps[:, 2 + r, 0:n], ACT.Sqrt, bias=eps_col,
                                       scale=1.0 / D).then_inc(N["std"].sem, 1)
                    for r, (t0, n) in enumerate(ranges):
                        for k in range(KT):
                            act.wait_ge(N["scaled"].sem, N["scaled"].at(r * KT + k + 1))
                            act.activation(dst[:, k, t0:t0 + n], dst[:, k, t0:t0 + n], ACT.Identity,
                                           bias=shift(k, r), scale=scale(k, r))

                @block.vector
                def _(dve):
                    if centre:
                        for r, (t0, n) in enumerate(ranges):
                            dve.wait_ge(N["mean"].sem, N["mean"].at(r + 1))
                            for k in range(KT):
                                dve.tensor_tensor(dst[:, k, t0:t0 + n], src[:, k, t0:t0 + n],
                                                  mean[:, t0:t0 + n], ALU.subtract)\
                                   .then_inc(N["centered"].sem, 1)
                    for r, (t0, n) in enumerate(ranges):
                        dve.wait_ge(N["std"].sem, N["std"].at(r + 1))
                        v_order.step(dve, dve.reciprocal(rstd[:, t0:t0 + n], rstd[:, t0:t0 + n]))
                        for k in range(KT):
                            dve.tensor_tensor(dst[:, k, t0:t0 + n], (dst if centre else src)[:, k, t0:t0 + n],
                                              rstd[:, t0:t0 + n], ALU.mult).then_inc(N["scaled"].sem, 1)
            if centre:
                N["sum"].close(n_r)
                N["mean"].close(n_r)
                N["centered"].close(n_r * KT)
            for n in ("sq", "sq_used", "scaled"):
                N[n].close(n_r * KT)
            N["std"].close(n_r)

        def modulate(norm_no, centre, src, ranges):
            sh = 24 * norm_no
            norm_stage(centre, ranges, src, hT,
                       lambda k, r: scl[:, norm_no, k, r:r + 1], lambda k, r: mod[:, sh + k, r:r + 1])

        done = [0]

        def ada_stage(which, slab0, bias_col, gain_cols):
            done[0] = slab0 + 24
            c = sil[:, which, :, :]
            acc = ps[:, 0, :]
            with nc.Block() as block:
                @block.sync
                def _(sp):
                    load_slabs(sp, done[0] + NS)

                @block.tensor
                def _(pe):
                    def slab(i, j):
                        n = slab0 + j
                        wait_slab(pe, n, i, NS)
                        for m in range(2):
                            o = at(i, NS * 4, j * 4 + m * 2)
                            dst = acc[:, o:o + 2] if i is None else acc[:, bass.ds(o, 2)]
                            for k in range(KT):
                                ins = pe.matmul(dst, ring[:, n % NS, k, m * P:(m + 1) * P], c[:, k, :],
                                                start=(k == 0), stop=(k == KT - 1))
                        ins.then_inc(mm_done, 1)
                    turns(pe, 24, NS, slab)

                @block.vector
                def _(dve):
                    dve.wait_ge(mm_done, signals[slab0 + 24])
                    v_order.step(dve, dve.tensor_tensor(
                        mod[:, :, :], acc[:, 0:96].rearrange("p (m c) -> p m c", c=2),
                        cols[:, bias_col:bias_col + 48].unsqueeze(2).to_broadcast([P, 48, 2]), ALU.add))
                    for n in range(2):
                        sc = mod[:, 8 + 24 * n:16 + 24 * n, :]
                        v_order.step(dve, dve.tensor_scalar(scl[:, n, :, :], sc, 1.0, None, ALU.add))
                        if gain_cols is not None:
                            g = cols[:, gain_cols[n]:gain_cols[n] + 8].unsqueeze(2).to_broadcast([P, 8, 2])
                            v_order.step(dve, dve.tensor_tensor(scl[:, n, :, :], scl[:, n, :, :], g, ALU.mult))

        def product_stage(slab0, n_cols, row_groups, rhs, ranges, take, which, before=None):
            n_r, n_g = len(ranges), len(row_groups)
            done[0] = slab0 + n_cols * n_g
            period = NS if n_g == 1 else 2
            per_turn = signals[slab0 + period * n_g] - signals[slab0]
            n_banks = min(8, period * 2 * n_r)
            loops = (period * n_g) % NS == 0

            def columns(eng, body):
                if loops:
                    turns(eng, n_cols, period, body)
                else:
                    for j in range(n_cols):
                        body(None, j)

            with nc.Block() as block:
                @block.sync
                def _(sp):
                    load_slabs(sp, done[0] + NS)

                @block.tensor
                def _(pe):
                    def column(i, j):
                        for g, (_, kt) in enumerate(row_groups):
                            n = slab0 + j * n_g + g
                            wait_slab(pe, n, i, period * n_g)
                            for m in range(2):
                                for r, (t0, nt) in enumerate(ranges):
                                    u = (j * 2 + m) * n_r + r
                                    free = u - n_banks + 1
                                    if g == 0 and (free >= 1 or i is not None):
                                        v = mm_free.at(free)
                                        pe.wait_ge(mm_free.sem, v if i is None else i * (period * 2 * n_r) + v)
                                    for k in range(kt):
                                        ins = pe.matmul(ps[:, u % n_banks, 0:nt],
                                                        ring[:, n % NS, k, m * P:(m + 1) * P],
                                                        rhs(g * KT + k, r), start=(g == 0 and k == 0),
                                                        stop=(g == n_g - 1 and k == kt - 1))
                                    ins.then_inc(mm_done, 1)
                    columns(pe, column)

                def taker(eng):
                    if before is not None:
                        before(eng)

                    def column(i, j):
                        for m in range(2):
                            for r, (t0, nt) in enumerate(ranges):
                                u = (j * 2 + m) * n_r + r
                                v = signals[slab0 + j * n_g + n_g - 1] + m * n_r + r + 1
                                eng.wait_ge(mm_done, v if i is None else i * per_turn + v)
                                take(at(i, 2 * period, 2 * j + m), r, ps[:, u % n_banks, 0:nt])\
                                    .then_inc(mm_free.sem, 1)
                    columns(eng, column)
                (block.scalar if which == "scalar" else block.vector)(taker)
            mm_free.close(n_cols * 2 * n_r)

        def tile_of(buf, t, n, t0=0, width=None):
            width = n if width is None else width
            if isinstance(t, int):
                return buf[:, t, t0:t0 + width]
            return buf.rearrange("p t n -> p (t n)")[:, bass.ds(t * n + t0, width)]

        def column_of(buf, c):
            return buf[:, c:c + 1] if isinstance(c, int) else buf[:, bass.ds(c, 1)]

        def units_stage(slab0, units, narrow, bias_rows):
            done[0] = slab0 + len(units)
            named("narrow")
            flat = [(n, x) for n, us in enumerate(units) for x in us]
            assert all(signals[slab0 + n + 1] - signals[slab0 + n] == len(us) for n, us in enumerate(units))
            with nc.Block() as block:
                @block.sync
                def _(sp):
                    if narrow is not None:
                        sp.dma_start(wnarrow[:, :, :], narrow.rearrange("(k p) n -> p k n", p=P))\
                          .then_inc(loaded.sem, 16)
                    load_slabs(sp, done[0] + NS)

                @block.tensor
                def _(pe):
                    if narrow is not None:
                        pe.wait_ge(loaded.sem, loaded.at(16))
                        for c in range(NCH):
                            for k in range(KT):
                                ins = pe.matmul(ps[:, 7, c * 16:(c + 1) * 16], hT[:, k, c * CH:(c + 1) * CH],
                                                wnarrow[:, k, :], start=(k == 0), stop=(k == KT - 1))
                        ins.then_inc(S["narrow"].sem, 1)
                    for u, (n, x) in enumerate(flat):
                        if u == 0 or flat[u - 1][0] != n:
                            wait_slab(pe, slab0 + n)
                        if u >= 7:
                            pe.wait_ge(mm_free.sem, mm_free.at(u - 6))
                        slab = ring[:, (slab0 + n) % NS, :, :]
                        for k in range(KT):
                            if x[0] == "tile":
                                _, m, t0, nt, _, _ = x
                                ins = pe.matmul(ps[:, u % 7, 0:nt], slab[:, k, m * P:(m + 1) * P],
                                                hT[:, k, t0:t0 + nt], start=(k == 0), stop=(k == KT - 1))
                            else:
                                _, c, c0, nt, _, _ = x
                                ins = pe.matmul(ps[:, u % 7, 0:nt], hT[:, k, c * CH:(c + 1) * CH],
                                                slab[:, k, c0:c0 + nt], start=(k == 0), stop=(k == KT - 1))
                        ins.then_inc(mm_done, 1)

                @block.vector
                def _(dve):
                    if narrow is not None:
                        dve.wait_ge(S["narrow"].sem, S["narrow"].at(1))
                        dve.tensor_tensor(small[:, 0:NCH * 16].rearrange("p (c n) -> p c n", n=16),
                                          ps[:, 7, 0:NCH * 16].rearrange("p (c n) -> p c n", n=16),
                                          bias_rows.unsqueeze(1).to_broadcast([P, NCH, 16]), ALU.add)

                @block.scalar
                def _(act):
                    for u, (n, x) in enumerate(flat):
                        act.wait_ge(mm_done, signals[slab0] + u + 1)
                        act.activation(x[4], ps[:, u % 7, 0:x[3]] if len(x[4].shape) == 2 else
                                       ps[:, u % 7, 0:x[3]].rearrange("p (h d) -> p h d", d=x[4].shape[2]),
                                       ACT.Copy, scale=x[5] or 1.0).then_inc(mm_free.sem, 1)
            mm_free.close(len(flat))
            if narrow is not None:
                loaded.close(16)
                S["narrow"].close(1)

        n_small, dve_abs, conv_marks = [0], [0, 0], [None]

        def end(name):
            if dumps and name in dumps:
                srcs = dumps[name](locals_of())
                with nc.Block() as block:
                    @block.sync
                    def _(sp):
                        for dst, src in srcs:
                            sp.dma_start(dst, src).then_inc(stored.sem, 16)
                        sp.wait_ge(stored.sem, stored.at(16 * len(srcs)))
                stored.close(16 * len(srcs))
            return stop == name

        def locals_of():
            return dict(xT=xT, hT=hT, big=big, small=small, mod=mod, scl=scl, cols=cols, COL=COL)

        COL = {}
        col_rows = []

        def param(name, rows_ap):
            COL[name] = sum(x.shape[0] for x in col_rows)
            col_rows.append(rows_ap)

        vec = lambda a: a.rearrange("(n p) -> n p", p=P)
        param("c", vec(w["c"][0]))
        param("c_ctx", vec(w["c_ctx"]))
        param("c2", vec(w["c_2"][0]))
        param("c_ctx2", vec(w["c_ctx_2"]))
        param("b_ada", vec(w["b_ada"][0]))
        param("b_ada2_0", vec(w["ada_b_2"][0]))
        param("b_ada2_1", vec(w["ada_b_2"][1]))
        for l in range(2):
            param(f"norm1_{l}", vec(w["norm1_g_2"][l]))
            param(f"norm2_{l}", vec(w["norm2_g_2"][l]))
        for n in ("ln1_g", "ln1_b", "ln2_g", "ln2_b"):
            param(n, vec(w[n][0]))
        param("conv_w", w["ssd_conv_w"][0].rearrange("t (n p) -> (t n) p", p=P))
        param("conv_b", vec(w["ssd_conv_b"][0]))
        param("ssd_norm", vec(w["ssd_norm_w"][0]))
        param("pool_scale", vec(w["pool_scale"][0]))
        param("ffn_w", w["ffn_conv_w"][0].rearrange("a b (n p) -> (a b n) p", p=P))
        param("ffn_b", vec(w["ffn_conv_b"][0]))
        param("mlstm_norm", vec(w["mlstm_norm_g_2"][0]))
        param("c_q_norm", w["c_q_norm_g_2"])
        param("c_k_norm", w["c_k_norm_g_2"])
        COL["swa_q"] = sum(x.shape[0] for x in col_rows)
        COL["swa_k"] = COL["swa_q"] + 1
        n_rows = COL["swa_k"] + 1
        assert n_rows <= 768
        n_lots = (n_rows + P - 1) // P
        tok_in = big[:, 0:NCH * D].rearrange("p (c d) -> p c d", c=NCH)
        row_in = big[:, NCH * D:NCH * D + 768].rearrange("p (g f) -> p g f", f=P)
        ctx2_in = big[:, 8192:8192 + NCTX * D].rearrange("p (c d) -> p c d", c=NCTX)
        d_in = big[0:4, 12288:12288 + P]
        DT_B, A_ROW, GATE_B, SINK = 0, 16, 32, 48

        groups = []
        for g in range(n_lots):
            n = min(P, n_rows - g * P)
            groups.append(([row_in[0:n, g, :]], cols[:, g * P:g * P + n]))
        for k in range(KT):
            groups.append(([tok_in[:, c, k * P:(k + 1) * P] for c in range(NLAT)], xT[:, k, 0:LAT]))
            groups.append(([tok_in[:, NLAT + c, k * P:(k + 1) * P] for c in range(NCTX)], xT[:, k, LAT:TOK]))
        groups.append(([d_in], dskip[:, :]))
        with nc.Block() as block:
            @block.sync
            def _(sp):
                n_loads = 0

                def load(dst, src):
                    nonlocal n_loads
                    sp.dma_start(dst, src).then_inc(loaded.sem, 16)
                    n_loads += 1
                load(mats[:, :, :], w["const_mats"].rearrange("n p q -> p n q"))
                for (name, _), ap in zip(list(COL.items()), col_rows):
                    at0, n, r = COL[name], ap.shape[0], 0
                    while r < n:
                        g, p0 = divmod(at0 + r, P)
                        m = min(n - r, P - p0)
                        load(row_in[p0:p0 + m, g, :], ap[r:r + m, :])
                        r += m
                for name, src in (("swa_q", w["swa_q_norm_g_2"]), ("swa_k", w["swa_k_norm_g_2"])):
                    g, p0 = divmod(COL[name], P)
                    for half in range(2):
                        load(row_in[p0:p0 + 1, g, half * 64:half * 64 + 64], src)
                load(tok_in[:, 0:NLAT, :], w["x"][0].rearrange("(c p) d -> p c d", p=P))
                load(tok_in[:, NLAT:NCH, :], w["ctx"][0].rearrange("(c p) d -> p c d", p=P))
                load(small[0:4, 0:2], w["ssd_d"][0].rearrange("(t h) -> t h", h=2))
                for dst, src in ((DT_B, w["ssd_dt_bias"][0].rearrange("a h -> (a h)")),
                                 (A_ROW, w["ssd_a_log"][0].rearrange("a h -> (a h)")),
                                 (GATE_B, w["ab_gate_b_2"][0]), (SINK, w["swa_sink_2"][0])):
                    load(rows[:, dst:dst + src.shape[0]], src.partition_broadcast(P))
                load_slabs(sp, NS)
                n_small[0] = n_loads
            @block.vector
            def _(dve):
                dve.wait_ge(loaded.sem, loaded.at(16 * n_small[0]))
                v_order.step(dve, dve.tensor_copy(d_in.rearrange("p (h q) -> p h q", h=2),
                                                  small[0:4, 0:2].unsqueeze(2).to_broadcast([4, 2, 64])))
                transpose_out(dve, groups, 0)

            @block.tensor
            def _(pe):
                pe.wait_ge(loaded.sem, loaded.at(16 * n_small[0]))
                pe.wait_ge(v_order.sem, 1)
                transpose_pe(pe, groups)

            @block.scalar
            def _(act):
                act.wait_ge(loaded.sem, loaded.at(16 * n_small[0]))
                a = rows[:, A_ROW:A_ROW + 16]
                a_order.step(act, act.activation(a, a, ACT.Exp))
                act.activation(a, a, ACT.Copy, scale=-1.0)
                transpose_out(act, groups, 1)
        loaded.close(16 * n_small[0])
        transpose_close(groups)
        if end("inputs"):
            return

        with nc.Block() as block:
            @block.scalar
            def _(act):
                for n, (a, b) in enumerate((("c", "c_ctx"), ("c2", "c_ctx2"))):
                    act.activation(sil[:, n, :, 0], cols[:, COL[a]:COL[a] + 8], ACT.Silu)
                    act.activation(sil[:, n, :, 1], cols[:, COL[b]:COL[b] + 8], ACT.Silu)

        ada_stage(0, W["ada"], COL["b_ada"], None)
        if end("ada"):
            return
        modulate(0, True, xT, BOTH)
        if end("mod1"):
            return
        LP, CP = LAT + 2, CTX + 2
        xbc_pad = big[:, 0:8 * (LP + CP)].rearrange("p (t n) -> p t n", t=8)
        o = 8 * (LP + CP)
        xbc = big[:, o:o + 8 * TOK].rearrange("p (t n) -> p t n", t=8)
        o += 8 * TOK
        zT = big[:, o:o + 4 * LAT].rearrange("p (t n) -> p t n", t=4)
        o += 4 * LAT
        fT = big[:, o:o + 2 * LAT].rearrange("p (t n) -> p t n", t=2)
        o += 2 * LAT
        PP = LAT + 16
        poolT = big[:, o:o + 2 * PP].rearrange("p (t n) -> p t n", t=2)
        o += 2 * PP
        x_tok = big[:, o:o + NCH * 512].rearrange("p (c n) -> p c n", c=NCH)
        o += NCH * 512
        b_tok = big[:, o:o + NCH * 256].rearrange("p (c n) -> p c n", c=NCH)
        o += NCH * 256
        yT = big[:, o:o + 4 * LAT].rearrange("p (t n) -> p t n", t=4)
        o += 4 * LAT
        assert o <= 24576

        with nc.Block() as block:
            @block.gpsimd
            def _(pool):
                for t in (xbc_pad, poolT):
                    pool.memset(t, 0.0)
        units = []
        for s in range(4):
            us = []
            for m in range(2):
                t = 2 * s + m
                us.append(("tile", m, 0, LAT, xbc_pad[:, t, 1:1 + LAT], None))
                if t < 6:
                    us.append(("tile", m, LAT, CTX, xbc_pad[:, t, LP + 1:LP + 1 + CTX], None))
            units.append(us)
        for s in range(2):
            units.append([("tile", m, 0, LAT, zT[:, 2 * s + m, :], None) for m in range(2)])
        units.append([("tile", m, 0, LAT, fT[:, m, :], None) for m in range(2)])
        units.append([("tile", m, 0, LAT, poolT[:, m, 8:8 + LAT], None) for m in range(2)])
        units_stage(W["in"], units, w["w_in"][0, :, OFF_DT:OFF_DT + 16], rows[:, DT_B:DT_B + 16])
        if end("w_in"):
            return

        n16 = NCH * 16
        sm = lambda i: small[:, i * n16:(i + 1) * n16]
        dt, dA, t_a, t_b, t_c = (sm(i) for i in range(5))
        conv_units = [(t, 0, LAT, 0) for t in range(8)] + [(t, LP, CTX, LAT) for t in range(6)]
        named("exp_ln")
        with nc.Block() as block:
            @block.vector
            def _(dve):
                v_order.step(dve, dve.scalar_tensor_tensor(t_a, dt, -1.0, dt, ALU.mult, ALU.max))
                dve_abs[0] = v_order.n
                marks = []
                for tap in range(3):
                    for u, (t, p0, n, t0) in enumerate(conv_units):
                        wcol = cols[:, COL["conv_w"] + tap * 8 + t:COL["conv_w"] + tap * 8 + t + 1]
                        src, dst = xbc_pad[:, t, p0 + tap:p0 + tap + n], xbc[:, t, t0:t0 + n]
                        if tap == 0:
                            b = cols[:, COL["conv_b"] + t:COL["conv_b"] + t + 1]
                            marks.append(v_order.mark(dve.tensor_scalar(dst, src, wcol, b, ALU.mult, ALU.add)))
                        else:
                            dve.wait_ge(v_order.sem, marks[-len(conv_units)])
                            marks.append(v_order.mark(dve.scalar_tensor_tensor(
                                dst, src, wcol, dst, ALU.mult, ALU.add)))
                conv_marks[0] = marks[-len(conv_units):]
                dve.wait_ge(S["exp_ln"].sem, S["exp_ln"].at(1))
                v_order.step(dve, dve.tensor_scalar(t_b, t_a, 1.0, None, ALU.add))
                dve_abs[1] = v_order.n
                v_order.step(dve, dve.tensor_scalar(dA, t_b, -1.0, None, ALU.add))
                dve.wait_ge(S["exp_ln"].sem, S["exp_ln"].at(2))
                v_order.step(dve, dve.tensor_scalar(t_b, dA, 0.0, None, ALU.is_equal))
                v_order.step(dve, dve.tensor_tensor(t_c, t_c, t_b, ALU.add))
                v_order.step(dve, dve.tensor_tensor(dA, dA, t_b, ALU.add))
                v_order.step(dve, dve.reciprocal(dA, dA))
                v_order.step(dve, dve.tensor_tensor(t_c, t_c, dA, ALU.mult))
                v_order.step(dve, dve.tensor_tensor(t_c, t_c, t_a, ALU.mult))
                v_order.step(dve, dve.scalar_tensor_tensor(dt, dt, 0.0, t_c, ALU.max, ALU.add))
                a_rows = rows[:, A_ROW:A_ROW + 16].unsqueeze(1).to_broadcast([P, NCH, 16])
                dve.tensor_tensor(dA.rearrange("p (c n) -> p c n", n=16), dt.rearrange("p (c n) -> p c n", n=16),
                                  a_rows, ALU.mult)

            @block.scalar
            def _(act):
                act.wait_ge(v_order.sem, dve_abs[0])
                act.activation(t_a, t_a, ACT.Exp, scale=-1.0).then_inc(S["exp_ln"].sem, 1)
                act.wait_ge(v_order.sem, dve_abs[1])
                act.activation(t_c, t_b, ACT.Ln).then_inc(S["exp_ln"].sem, 1)
                for (t, _, n, t0), m in zip(conv_units, conv_marks[0]):
                    act.wait_ge(v_order.sem, m)
                    act.activation(xbc[:, t, t0:t0 + n], xbc[:, t, t0:t0 + n], ACT.Silu)
        S["exp_ln"].close(2)
        if end("conv"):
            return
        tmp = big[:, 0:8 * (LP + CP)]
        Gs = tmp[:, 0:8 * P].rearrange("p (c g n) -> p c g n", c=NLAT, g=2)
        state = tmp[:, 1024:2048].rearrange("p (d g n) -> p d g n", d=2, g=2)
        xd = tmp[:, 2048:3072].rearrange("p (b k n) -> p b k n", b=2, k=2)
        seg = tmp[:, 3072:4096].rearrange("p (b h n) -> p b h n", b=2, h=4)
        lmat = tmp[:, 4096:5120].rearrange("p (b h n) -> p b h n", b=2, h=4)
        e_row = tmp[:, 5120:6144].rearrange("p (b h n) -> p b h n", b=2, h=4)
        c_dec = squares[:, 0:2, :].rearrange("p b (h n) -> p b h n", h=4)
        g_mask = mean[:, 0:256].rearrange("p (b n) -> p b n", b=2)
        neg_cs, e_tot, decay = t_a, t_b, t_c
        by_chunk = lambda a: a.rearrange("p (c n) -> p c n", n=16)
        groups = []
        for c in range(NCH):
            t0 = c * CH
            groups.append(([xbc[:, t, t0:t0 + CH] for t in range(4)], x_tok[:, c, :]))
            groups.append(([xbc[:, 4 + g, t0:t0 + CH] for g in range(2)], b_tok[:, c, :]))
        with nc.Block() as block:
            @block.tensor
            def _(pe):
                transpose_pe(pe, groups)

            @block.vector
            def _(dve):
                transpose_out(dve, groups, 0)

            @block.scalar
            def _(act):
                transpose_out(act, groups, 1)
        transpose_close(groups)
        named("cs", "cb", "log_decay")
        with nc.Block() as block:
            @block.tensor
            def _(pe):
                for c in range(NCH):
                    for d, tri in enumerate((U_LE, U_GE)):
                        o = c * 16 + d * 8
                        pe.matmul(ps[:, 0, o:o + 8], mats[:, tri, :], dA[:, o:o + 8], start=True, stop=True)
                pe.matmul(ps[:, 1, 0:n16], ones, dA, start=True, stop=True).then_inc(S["cs"].sem, 1)
                for c in range(NLAT):
                    for g in range(2):
                        u = c * 2 + g
                        pe.matmul(ps[:, 2 + u // 4, (u % 4) * P:(u % 4 + 1) * P],
                                  xbc[:, 4 + g, c * CH:(c + 1) * CH], xbc[:, 6 + g, c * CH:(c + 1) * CH],
                                  start=True, stop=True).then_inc(S["cb"].sem, 1)

            @block.vector
            def _(dve):
                dve.wait_ge(S["cs"].sem, S["cs"].at(1))
                v_order.step(dve, dve.tensor_scalar(neg_cs, ps[:, 0, 0:n16], -1.0, None, ALU.mult))
                dve.tensor_tensor(decay, ps[:, 1, 0:n16], neg_cs, ALU.add).then_inc(S["log_decay"].sem, 1)
                dve.memset(tmp[:, 1024:2048], 0.0)

            @block.scalar
            def _(act):
                act.wait_ge(S["log_decay"].sem, S["log_decay"].at(1))
                act.activation(e_tot, ps[:, 1, 0:n16], ACT.Exp)
                act.activation(decay, decay, ACT.Exp)
                for q in range(2):
                    act.wait_ge(S["cb"].sem, S["cb"].at(4 * (q + 1)))
                    act.activation(tmp[:, q * 512:(q + 1) * 512], ps[:, 2 + q, :], ACT.Copy)
        S["cs"].close(1)
        S["cb"].close(8)
        S["log_decay"].close(1)

        order_of = [[4, 5, 0, 1, 2, 3], [5, 4, 3, 2, 1, 0]]
        steps = [(d, order_of[d][k], g, k) for k in range(NCH) for d in range(2) for g in range(2)]
        outs = [s for s, (_, _, _, k) in enumerate(steps) if k >= NCTX]
        ups = [s for s, (_, _, _, k) in enumerate(steps) if k < NCH - 1]
        upto = lambda lst, s: sum(1 for x in lst if x < s)
        heads = lambda a, d, c, g: by_chunk(a)[:, c, d * 8 + g * 4:d * 8 + g * 4 + 4]
        R = named("xdt", "bc", "seg", "lmat", "erow", "m", "cdec", "y", "y_out", "ds", "state")
        sig = lambda ins, n: ins.then_inc(R[n].sem, 1)
        wait = lambda eng, n, v: eng.wait_ge(R[n].sem, R[n].at(v))

        with nc.Block() as block:
            @block.gpsimd
            def _(pool):
                for s, (d, c, g, k) in enumerate(steps):
                    b = s % 2
                    if s >= 2:
                        if s - 2 in ups:
                            wait(pool, "ds", upto(ups, s - 1))
                        if s - 2 in outs:
                            wait(pool, "y", upto(outs, s - 1))
                    x3 = x_tok[:, c, g * 256:(g + 1) * 256].rearrange("p (h q) -> p h q", h=4)
                    v = [xd[:, b, j, :].rearrange("p (h q) -> p h q", h=4) for j in range(2)]
                    g_order.step(pool, pool.tensor_tensor(
                        v[0], x3, heads(dt, d, c, g).unsqueeze(2).to_broadcast([P, 4, 64]), ALU.mult))
                    sig(pool.tensor_tensor(
                        v[1], v[0], heads(decay, d, c, g).unsqueeze(2).to_broadcast([P, 4, 64]), ALU.mult), "xdt")
                    if s in outs:
                        i = outs.index(s)
                        wait(pool, "erow", i + 1)
                        if i >= 2:
                            wait(pool, "y", i - 1)
                        cT = xbc[:, 6 + g, c * CH:(c + 1) * CH].unsqueeze(1).to_broadcast([P, 4, CH])
                        sig(pool.tensor_tensor(c_dec[:, i % 2, :, :], e_row[:, i % 2, :, :], cT, ALU.mult), "cdec")

            @block.tensor
            def _(pe):
                def rows_of_cs(i):
                    d, c, g, _ = steps[outs[i]]
                    if i >= 2:
                        wait(pe, "seg", i - 1)
                        wait(pe, "erow", i - 1)
                    for h in range(4):
                        col = heads(dA, d, c, g)[:, h:h + 1]
                        ins = pe.matmul(ps[:, i % 2, h * P:(h + 1) * P], col.to_broadcast([P, P]),
                                        mats[:, (U_LE, U_GE)[d], :], start=True, stop=True)
                    sig(ins, "bc")

                rows_of_cs(0)
                for s, (d, c, g, k) in enumerate(steps):
                    wait(pe, "xdt", s + 1)
                    if s in ups:
                        i = ups.index(s)
                        if i >= 2:
                            wait(pe, "state", i - 1)
                        sig(pe.matmul(ps[:, 4 + i % 2, 0:256], b_tok[:, c, g * P:(g + 1) * P], xd[:, s % 2, 1, :],
                                      start=True, stop=True), "ds")
                    if s in outs:
                        i = outs.index(s)
                        if i + 1 < len(outs):
                            rows_of_cs(i + 1)
                        wait(pe, "m", i + 1)
                        wait(pe, "cdec", i + 1)
                        wait(pe, "state", upto(ups, s - 3))
                        if i >= 2:
                            wait(pe, "y_out", i - 1)
                        for h in range(4):
                            o = ps[64 * (h % 2):64 * (h % 2) + 64, 2 + i % 2, (h // 2) * P:(h // 2 + 1) * P]
                            pe.matmul(o, xd[:, s % 2, 0, h * 64:(h + 1) * 64], lmat[:, i % 2, h, :],
                                      start=True, stop=False, skip_group_check=True)
                            ins = pe.matmul(o, state[:, d, g, h * 64:(h + 1) * 64], c_dec[:, i % 2, h, :],
                                            start=False, stop=True, skip_group_check=True)
                        sig(ins, "y")

            @block.vector
            def _(dve):
                def finish(s):
                    d, c, g, k = steps[s]
                    if s in outs:
                        i = outs.index(s)
                        wait(dve, "y", i + 1)
                        dst = yT[:, 2 * g:2 * g + 2, c * CH:(c + 1) * CH]
                        src = ps[:, 2 + i % 2, 0:2 * P].rearrange("p (t n) -> p t n", t=2)
                        if k < NCTX + NLAT // 2:
                            sig(dve.tensor_copy(dst, src), "y_out")
                        else:
                            wait(dve, "y_out", i - 1)
                            sig(dve.tensor_tensor(dst, src, dst, ALU.add), "y_out")
                    if s in ups:
                        i = ups.index(s)
                        st = state[:, d, g, :]
                        st3 = st.rearrange("p (h q) -> p h q", h=4)
                        wait(dve, "ds", i + 1)
                        if i >= 4:
                            wait(dve, "state", i - 3)
                        v_order.step(dve, dve.tensor_tensor(
                            st3, st3, heads(e_tot, d, c, g).unsqueeze(2).to_broadcast([P, 4, 64]), ALU.mult))
                        sig(dve.tensor_tensor(st, ps[:, 4 + i % 2, 0:256], st, ALU.add), "state")

                for s, (d, c, g, k) in enumerate(steps):
                    if s in outs:
                        i = outs.index(s)
                        b = i % 2
                        wait(dve, "erow", i + 1)
                        if i >= 2:
                            wait(dve, "lmat", i - 1)
                        for h in range(4):
                            ins = dve.tensor_scalar(seg[:, b, h, :], ps[:, b, h * P:(h + 1) * P],
                                                    heads(neg_cs, d, c, g)[:, h:h + 1], 0.0, ALU.add, ALU.min)
                        sig(ins, "seg")
                        if i >= 2:
                            wait(dve, "m", i - 1)
                        v_order.step(dve, dve.tensor_tensor(g_mask[:, b, :], Gs[:, c, g, :],
                                                            mats[:, (U_LE, U_GE)[d], :], ALU.mult))
                    if s >= 1:
                        finish(s - 1)
                    if s in outs:
                        wait(dve, "lmat", i + 1)
                        sig(dve.tensor_tensor(lmat[:, b, :, :], lmat[:, b, :, :],
                                              g_mask[:, b, :].unsqueeze(1).to_broadcast([P, 4, P]), ALU.mult), "m")
                finish(len(steps) - 1)

            @block.scalar
            def _(act):
                for i in range(len(outs)):
                    b = i % 2
                    wait(act, "bc", i + 1)
                    if i >= 2:
                        wait(act, "cdec", i - 1)
                    sig(act.activation(e_row[:, b, :, :].rearrange("p h n -> p (h n)"), ps[:, b, :], ACT.Exp), "erow")
                    wait(act, "seg", i + 1)
                    if i >= 2:
                        wait(act, "y", i - 1)
                    sig(act.activation(lmat[:, b, :, :], seg[:, b, :, :], ACT.Exp), "lmat")
        for n in ("bc", "seg", "lmat", "erow", "m", "cdec", "y", "y_out"):
            R[n].close(len(outs))
        R["xdt"].close(len(steps))
        R["ds"].close(len(ups))
        R["state"].close(len(ups))
        if end("ssd"):
            return

        dft = big[:, 0:4096].rearrange("p (a k n) -> p a k n", a=2, k=NLAT)
        w4 = small[:, :].rearrange("p (a n) -> p a n", a=4)
        W12 = tmp[:, 4096:4608].rearrange("p (t n) -> p t n", t=2)
        f_tok = tmp[:, 4608:5632].rearrange("p (c n) -> p c n", c=NLAT)
        cnt = x_tok.rearrange("p c n -> p (c n)")[:, 0:1024].rearrange("p (t n) -> p t n", t=2)
        sums = xbc.rearrange("p t n -> p (t n)")[:, 3072:3072 + 4 * PP].rearrange("p (t s n) -> p t s n", t=2, s=2)
        pooled = x_tok.rearrange("p c n -> p (c n)")[:, 1024:2048].rearrange("p (t n) -> p t n", t=2)
        gated = b_tok.rearrange("p c n -> p (c n)")[:, 0:1024].rearrange("p (t n) -> p t n", t=2)
        R = named("zero", "silu", "y", "sq", "var", "std", "w12", "w12_out", "ftok", "ftok_out", "dft", "pooled", "pool")
        with nc.Block() as block:
            @block.gpsimd
            def _(pool):
                sig(pool.memset(small[:, :], 0.0), "zero")
                sig(pool.memset(sums, 0.0), "zero")

            @block.sync
            def _(sp):
                wait(sp, "zero", 1)
                for a, name in enumerate(("fnet_w", "pool_w")):
                    for g in range(4):
                        h = 64 * (g % 2)
                        sp.dma_start(w4[h:h + 64, 2 * a + g // 2, h:h + 64], w[name][0, g]).then_inc(loaded.sem, 16)
                sp.dma_start(cnt, w["const_tables"][T_CNT:T_CNT + 2].rearrange("t p n -> p t n"))\
                  .then_inc(loaded.sem, 16)
                for a in range(2):
                    sp.dma_start(dft[:, a, :, :], w["const_dft"][a].rearrange("(k p) n -> p k n", p=P))\
                      .then_inc(loaded.sem, 16)

            @block.scalar
            def _(act):
                for t in range(4):
                    sig(act.activation(zT[:, t, :], zT[:, t, :], ACT.Silu), "silu")
                for t in range(4):
                    wait(act, "y", t + 1)
                    if t >= 3:
                        wait(act, "var", t - 2)
                    sig(act.activation(squares[:, t % 3, :], yT[:, t, :], ACT.Square), "sq")
                wait(act, "w12", 4)
                for t in range(2):
                    sig(act.activation(W12[:, t, :], ps[:, 2, t * 256:(t + 1) * 256], ACT.Copy), "w12_out")
                for t in range(2):
                    for c in range(NLAT):
                        u = t * NLAT + c
                        wait(act, "ftok", 2 * (u // 2 + 1))
                        if u >= NLAT:
                            wait(act, "dft", 1)
                        sig(act.activation(f_tok[:, c, :], ps[:, 3 + (u // 2) % 2, (u % 2) * 256:(u % 2 + 1) * 256],
                                           ACT.Copy), "ftok_out")
                    wait(act, "dft", t + 1)
                    act.activation(hT[:, 4 + t, 0:LAT], ps[:, 5, :], ACT.Copy).then_inc(mm_free.sem, 1)
                for t in range(2):
                    wait(act, "pool", t + 1)
                    sc = cols[:, COL["pool_scale"] + t:COL["pool_scale"] + t + 1]
                    act.activation(hT[:, 6 + t, 0:LAT], ps[:, 6 + t, :], ACT.Copy, scale=sc)
                for g in range(2):
                    wait(act, "var", 2 * g + 2)
                    sig(act.activation(rstd[:, 0:LAT] if g == 0 else mean[:, 0:LAT], ps[:, g, :], ACT.Sqrt,
                                       bias=eps_col, scale=1.0 / 256), "std")

            @block.tensor
            def _(pe):
                for t in range(4):
                    wait(pe, "sq", t + 1)
                    sig(pe.matmul(ps[:, t // 2, :], ones, squares[:, t % 3, :], start=(t % 2 == 0),
                                  stop=(t % 2 == 1)), "var")
                pe.wait_ge(loaded.sem, loaded.at(16 * 11))
                for t in range(2):
                    for a, m in enumerate((DFT_C, DFT_S)):
                        sig(pe.matmul(ps[:, 2, t * 256 + a * P:t * 256 + (a + 1) * P], mats[:, m, :], w4[:, t, :],
                                      start=True, stop=True), "w12")
                for t in range(2):
                    wait(pe, "w12_out", t + 1)
                    for c in range(NLAT):
                        u = t * NLAT + c
                        if u >= NLAT:
                            wait(pe, "ftok_out", u // 2 * 2 - 2)
                        sig(pe.matmul(ps[:, 3 + (u // 2) % 2, (u % 2) * 256:(u % 2 + 1) * 256],
                                      fT[:, t, c * CH:(c + 1) * CH], W12[:, t, :], start=True, stop=True), "ftok")
                    if t == 1:
                        pe.wait_ge(mm_free.sem, mm_free.at(1))
                    for a in range(2):
                        for c in range(NLAT):
                            wait(pe, "ftok_out", t * NLAT + c + 1)
                            ins = pe.matmul(ps[:, 5, :], f_tok[:, c, a * P:(a + 1) * P], dft[:, a, c, :],
                                            start=(a == 0 and c == 0), stop=(a == 1 and c == NLAT - 1))
                    sig(ins, "dft")
                for t in range(2):
                    wait(pe, "pooled", t + 1)
                    sig(pe.matmul(ps[:, 6 + t, :], w4[:, 2 + t, :], pooled[:, t, :], start=True, stop=True), "pool")

            @block.vector
            def _(dve):
                for t in range(4):
                    v_order.step(dve, dve.scalar_tensor_tensor(yT[:, t, :], xbc[:, t, 0:LAT], dskip[:, t:t + 1],
                                                               yT[:, t, :], ALU.mult, ALU.add))
                    wait(dve, "silu", t + 1)
                    sig(dve.tensor_tensor(yT[:, t, :], yT[:, t, :], zT[:, t, :], ALU.mult), "y")
                wait(dve, "zero", 2)
                dve.wait_ge(loaded.sem, loaded.at(16 * 11))
                for t in range(2):
                    src = poolT[:, t, :]
                    for lvl in range(4 if t else 2):
                        dst = sums[:, t, lvl % 2, :]
                        h = 1 if lvl == 0 else 2 ** (lvl - 1)
                        lo, n = 8, LAT
                        if lvl == 0:
                            a, b, e0, e1 = 1, 0, 1, PP
                        else:
                            a, b, e0, e1 = h, h, 2 ** lvl, PP - 2 ** lvl
                        v_order.step(dve, dve.tensor_tensor(dst[:, e0:e1], src[:, e0 - a:e1 - a],
                                                            src[:, e0 + b:e1 + b], ALU.add))
                        part = slice(0, 64) if lvl % 2 == 0 else slice(64, P)
                        if lvl // 2 == t:
                            v_order.step(dve, dve.tensor_tensor(pooled[part, t, :], dst[part, 8:8 + LAT],
                                                                cnt[part, t, :], ALU.mult))
                        src = dst
                    sig(dve.tensor_tensor(pooled[:, t, :], pooled[:, t, :], poolT[:, t, 8:8 + LAT],
                                          ALU.subtract), "pooled")
                for g in range(2):
                    wait(dve, "std", g + 1)
                    r = rstd[:, 0:LAT] if g == 0 else mean[:, 0:LAT]
                    v_order.step(dve, dve.reciprocal(r, r))
                    for t in (2 * g, 2 * g + 1):
                        wn = cols[:, COL["ssd_norm"] + t:COL["ssd_norm"] + t + 1]
                        dve.scalar_tensor_tensor(hT[:, t, 0:LAT], yT[:, t, :], wn, r, ALU.mult, ALU.mult)
        for n, v in (("zero", 2), ("silu", 4), ("y", 4), ("sq", 4), ("var", 4), ("std", 2), ("w12", 4), ("w12_out", 2),
                     ("ftok", 8), ("ftok_out", 8), ("dft", 2), ("pooled", 2), ("pool", 2)):
            R[n].close(v)
        loaded.close(16 * 11)
        mm_free.close(2)
        if end("mix1"):
            return

        def add_gated(gate):
            return lambda t, r, bank: nc.vector.scalar_tensor_tensor(
                tile_of(xT, t, TOK, BOTH[r][0], BOTH[r][1]), bank,
                mod[:, :, :].rearrange("p m c -> p (m c)")[:, 2 * (gate + t) + r:2 * (gate + t) + r + 1]
                if isinstance(t, int) else mod[:, :, :].rearrange("p m c -> p (m c)")[:, bass.ds(t * 2 + 2 * gate + r, 1)],
                tile_of(xT, t, TOK, BOTH[r][0], BOTH[r][1]), ALU.mult, ALU.add)

        def alpha_x(dve):
            for k in range(KT):
                v_order.step(dve, dve.tensor_scalar(xT[:, k, 0:LAT], xT[:, k, 0:LAT], ALPHA, None, ALU.mult))

        def post_norm(g, b):
            norm_stage(True, ONLY_LAT, xT, xT, lambda k, r: cols[:, COL[g] + k:COL[g] + k + 1],
                       lambda k, r: cols[:, COL[b] + k:COL[b] + k + 1])

        from_h = lambda k, r: hT[:, k, BOTH[r][0]:BOTH[r][0] + BOTH[r][1]]
        product_stage(W["out"], 4, whole, from_h, ONLY_LAT, add_gated(16), "vector", alpha_x)
        post_norm("ln1_g", "ln1_b")
        if end("x1"):
            return
        modulate(1, True, xT, ONLY_LAT)

        act_ff = big[:, 0:FT * LAT].rearrange("p (t n) -> p t n", t=FT)
        GP = (GRID_H + 2) * (GRID_W + 2)
        o = FT * LAT
        grid = big[:, o:o + 8 * GP].rearrange("p (b h w) -> p b h w", b=8, h=GRID_H + 2)
        o += 8 * GP
        conv = big[:, o:o + 8 * LAT].rearrange("p (b n) -> p b n", b=8)
        R = named("zero", "grid", "conv", "gelu", "ff")
        done[0] = W["up"] + FT
        slab0 = W["up"]
        v_base = v_order.n
        CW, TAPS = COL["ffn_w"], 9

        def wait_turn(eng, n, i, per_turn, v):
            eng.wait_ge(R[n].sem, R[n].at(v) if i is None else i * per_turn + R[n].at(v))

        with nc.Block() as block:
            @block.sync
            def _(sp):
                load_slabs(sp, done[0] + NS)

            @block.gpsimd
            def _(pool):
                sig(pool.memset(grid, 0.0), "zero")

                def step(i, j):
                    for m in range(2):
                        wait_turn(pool, "gelu", i, 4, 2 * j + m + 1)
                        u = (4 * j + m) % 8
                        sig(pool.tensor_tensor(tile_of(act_ff, at(i, 4, 2 * j + m), LAT), conv[:, u, :],
                                               conv[:, (u + 2) % 8, :], ALU.mult), "ff")
                turns(pool, FT // 2, 2, step, 1)

            @block.tensor
            def _(pe):
                def step(i, j):
                    for half in range(2):
                        n = slab0 + 2 * j + half
                        wait_slab(pe, n, i, 4)
                        for m in range(2):
                            u = 4 * j + 2 * half + m
                            if u >= 8 or i is not None:
                                v = mm_free.at(u - 7)
                                pe.wait_ge(mm_free.sem, v if i is None else i * 8 + v)
                            for k in range(KT):
                                ins = pe.matmul(ps[:, u % 8, :], ring[:, n % NS, k, m * P:(m + 1) * P],
                                                hT[:, k, 0:LAT], start=(k == 0), stop=(k == KT - 1))
                            ins.then_inc(mm_done, 1)
                turns(pe, FT // 2, 2, step, 1)

            @block.scalar
            def _(act):
                wait(act, "zero", 1)

                def step(i, j):
                    for u in range(4 * j, 4 * j + 4):
                        v = signals[slab0] + u + 1
                        act.wait_ge(mm_done, v if i is None else i * 8 + v)
                        if u >= 8 or i is not None:
                            wait_turn(act, "conv", i, 8, u - 7)
                        act.activation(grid[:, u % 8, 1:1 + GRID_H, 1:1 + GRID_W],
                                       ps[:, u % 8, :].rearrange("p (h w) -> p h w", w=GRID_W), ACT.Copy)\
                           .then_inc(mm_free.sem, 1)

                def gelus(i, j):
                    for m in range(2):
                        wait_turn(act, "conv", i, 8, 4 * j + 2 + m + 1)
                        g = conv[:, (4 * j + 2 + m) % 8, :]
                        sig(act.activation(g, g, ACT.Gelu_apprx_tanh), "gelu")
                turns(act, FT // 2, 2, lambda i, j: (step(i, j), gelus(i, j)), 1)

            @block.vector
            def _(dve):
                def step(i, j):
                    first = [0] * 4
                    for tap in range(TAPS):
                        for q in range(4):
                            u = 4 * j + q
                            tile = at(i, 4, 2 * j + q % 2)
                            if q >= 2:
                                tile = tile + FT
                            wcol = column_of(cols, tile + (CW + tap * 2 * FT))
                            b = u % 8
                            dy, dx = divmod(tap, 3)
                            src = grid[:, b, dy:dy + GRID_H, dx:dx + GRID_W]
                            dst = conv[:, b, :].rearrange("p (h w) -> p h w", w=GRID_W)
                            mine = v_base + j * 4 * (TAPS - 1) + tap * 4 + q
                            if tap == 0:
                                v = mm_free.at(u + 1)
                                dve.wait_ge(mm_free.sem, v if i is None else i * 8 + v)
                                if u >= 8 or i is not None:
                                    wait_turn(dve, "ff", i, 4, 2 * j - 2)
                                ins = dve.tensor_scalar(dst, src, wcol, column_of(cols, tile + COL["ffn_b"]),
                                                        ALU.mult, ALU.add)
                            else:
                                v = mine - 3
                                dve.wait_ge(v_order.sem, v if i is None else i * (8 * (TAPS - 1)) + v)
                                ins = dve.scalar_tensor_tensor(dst, src, wcol, dst, ALU.mult, ALU.add)
                            if tap < TAPS - 1:
                                ins.then_inc(v_order.sem, 1)
                            else:
                                sig(ins, "conv")
                turns(dve, FT // 2, 2, step, 1)
        v_order.n += (FT // 2) * 4 * (TAPS - 1)
        mm_free.close(FT * 2)
        R["zero"].close(1)
        R["conv"].close(FT * 2)
        R["gelu"].close(FT)
        R["ff"].close(FT)
        if end("ffn"):
            return
        product_stage(W["down"], 4, DOWN_ROWS, lambda k, r: act_ff[:, k, :], ONLY_LAT, add_gated(40), "vector",
                      alpha_x)
        post_norm("ln2_g", "ln2_b")
        if end("block1"):
            return
        def mlp(layer, ranges):
            n = sum(r[1] for r in ranges)
            hid = big[:, 0:MT * n].rearrange("p (t n) -> p t n", t=MT)
            slab0 = W[f"w1_{layer}"]
            n_r = len(ranges)
            done[0] = slab0 + MT // 2
            per_turn = NS * 2 * n_r

            def units(eng, body):
                def column(i, j):
                    for m in range(2):
                        for r in range(n_r):
                            body(i, j, m, r, (j * 2 + m) * n_r + r)
                turns(eng, MT // 2, NS, column)

            with nc.Block() as block:
                @block.sync
                def _(sp):
                    load_slabs(sp, done[0] + NS)

                @block.tensor
                def _(pe):
                    def unit(i, j, m, r, u):
                        if m == 0 and r == 0:
                            wait_slab(pe, slab0 + j, i, NS)
                        v = mm_free.at(u - 7)
                        pe.wait_ge(mm_free.sem, v if i is None else i * per_turn + v)
                        for k in range(KT):
                            ins = pe.matmul(ps[:, u % 8, 0:ranges[r][1]],
                                            ring[:, (slab0 + j) % NS, k, m * P:(m + 1) * P],
                                            from_h(k, r), start=(k == 0), stop=(k == KT - 1))
                        ins.then_inc(mm_done, 1)
                    units(pe, unit)

                @block.scalar
                def _(act):
                    def unit(i, j, m, r, u):
                        v = signals[slab0] + u + 1
                        act.wait_ge(mm_done, v if i is None else i * per_turn + v)
                        t0, nt = ranges[r]
                        act.activation(tile_of(hid, at(i, 2 * NS, 2 * j + m), n, t0, nt), ps[:, u % 8, 0:nt],
                                       ACT.Relu).then_inc(mm_free.sem, 1)
                    units(act, unit)

                @block.vector
                def _(dve):
                    def unit(i, j, m, r, u):
                        v = mm_free.at(u + 1)
                        dve.wait_ge(mm_free.sem, v if i is None else i * per_turn + v)
                        t0, nt = ranges[r]
                        h = tile_of(hid, at(i, 2 * NS, 2 * j + m), n, t0, nt)
                        dve.tensor_tensor(h, h, h, ALU.mult)
                    units(dve, unit)
            mm_free.close(MT * n_r)
            product_stage(W[f"w2_{layer}"], 4, MLP_ROWS,
                          lambda k, r: hid[:, k, ranges[r][0]:ranges[r][0] + ranges[r][1]], ranges,
                          add_gated(40), "vector")

        def head_norms(jobs, hd_mat, hd):
            R = named("sq", "var", "std")
            temps = [rstd[:, 0:LAT], mean[:, 0:LAT]]
            v_at = v_order.n
            with nc.Block() as block:
                @block.tensor
                def _(pe):
                    for u, (src, n, _) in enumerate(jobs):
                        pe.wait_ge(R["sq"].sem, R["sq"].at(u + 1))
                        if u >= 4:
                            pe.wait_ge(R["std"].sem, R["std"].at(u - 3))
                        pe.matmul(ps[:, u % 4, 0:n], hd_mat, squares[:, u % 3, 0:n], start=True, stop=True)\
                          .then_inc(R["var"].sem, 1)

                @block.scalar
                def _(act):
                    def root(u):
                        n = jobs[u][1]
                        act.wait_ge(R["var"].sem, R["var"].at(u + 1))
                        if u >= 2:
                            act.wait_ge(v_order.sem, v_at + 2 * (u - 1))
                        act.activation(temps[u % 2][:, 0:n], ps[:, u % 4, 0:n], ACT.Sqrt, bias=eps_col,
                                       scale=1.0 / hd).then_inc(R["std"].sem, 1)
                    for u, (src, n, _) in enumerate(jobs):
                        if u >= 3:
                            act.wait_ge(R["var"].sem, R["var"].at(u - 2))
                        act.activation(squares[:, u % 3, 0:n], src, ACT.Square).then_inc(R["sq"].sem, 1)
                        if u >= 1:
                            root(u - 1)
                    root(len(jobs) - 1)

                @block.vector
                def _(dve):
                    for u, (src, n, gain) in enumerate(jobs):
                        t = temps[u % 2][:, 0:n]
                        dve.wait_ge(R["std"].sem, R["std"].at(u + 1))
                        v_order.step(dve, dve.reciprocal(t, t))
                        v_order.mark(dve.scalar_tensor_tensor(src, src, gain, t, ALU.mult, ALU.mult))
            for n in R:
                R[n].close(len(jobs))

        def rope(tiles, rot, cos, sin):
            R = named("rot", "sin")
            with nc.Block() as block:
                @block.tensor
                def _(pe):
                    for u, t in enumerate(tiles):
                        if u >= 4:
                            pe.wait_ge(R["sin"].sem, R["sin"].at(u - 3))
                        pe.matmul(ps[:, u % 4, :], mats[:, rot, :], t, start=True, stop=True)\
                          .then_inc(R["rot"].sem, 1)

                @block.vector
                def _(dve):
                    for u, t in enumerate(tiles):
                        dve.wait_ge(R["rot"].sem, R["rot"].at(u + 1))
                        v_order.step(dve, dve.tensor_tensor(t, t, cos, ALU.mult))
                        ins = dve.tensor_tensor(squares[:, u % 3, :], ps[:, u % 4, :], sin, ALU.mult)
                        ins.then_inc(R["sin"].sem, 1)
                        dve.wait_ge(R["sin"].sem, R["sin"].at(u + 1))
                        v_order.step(dve, dve.tensor_tensor(t, t, squares[:, u % 3, :], ALU.add))
            for n in R:
                R[n].close(len(tiles))

        def attention(jobs, scale, bufs):
            sc, pt, stat = bufs
            R = named("qk", "scaled", "max", "exp", "norm", "turned", "turned_out", "pv", "pv_out")
            sig = lambda ins, n: ins.then_inc(R[n].sem, 1)
            wait = lambda eng, n, v: eng.wait_ge(R[n].sem, R[n].at(v))
            flat = ps[:, :, :].rearrange("p b n -> p (b n)")
            n_jobs = len(jobs)
            with nc.Block() as block:
                @block.tensor
                def _(pe):
                    def scores(j):
                        q, keys, _, _, _, _ = jobs[j]
                        if j >= 2:
                            wait(pe, "scaled", j - 1)
                        for k_ap, c0, _ in keys:
                            ins = pe.matmul(flat[:, (j % 2) * 1024 + c0:(j % 2) * 1024 + c0 + k_ap.shape[1]],
                                            q, k_ap, start=True, stop=True, skip_group_check=True)
                        sig(ins, "qk")

                    def turn(j):
                        width = jobs[j][2]
                        wait(pe, "norm", j + 1)
                        if j >= 1:
                            wait(pe, "turned_out", j)
                        for c in range(width // P):
                            ins = pe.transpose(flat[:, 2048 + c * P:2048 + (c + 1) * P],
                                               sc[:, j % 2, c * P:(c + 1) * P], ident)
                        sig(ins, "turned")

                    def values(j):
                        _, _, width, v, _, o = jobs[j]
                        wait(pe, "turned_out", j + 1)
                        if j >= 2:
                            wait(pe, "pv_out", j - 1)
                        p0, d = o.start_partition(), v[0].shape[1]
                        for c in range(width // P):
                            ins = pe.matmul(ps[p0:p0 + d, 6 + j % 2, 0:P], v[c], pt[:, j % 2, c * P:(c + 1) * P],
                                            start=(c == 0), stop=(c == width // P - 1))
                        sig(ins, "pv")

                    scores(0)
                    for j in range(n_jobs):
                        if j + 1 < n_jobs:
                            scores(j + 1)
                        turn(j)
                        if j >= 1:
                            values(j - 1)
                    values(n_jobs - 1)

                @block.vector
                def _(dve):
                    def top(j):
                        _, keys, width, _, sink, _ = jobs[j]
                        b = j % 2
                        wait(dve, "qk", j + 1)
                        if j >= 2:
                            wait(dve, "turned", j - 1)
                        base = b * 1024
                        at_sc = 0
                        marks = []
                        for k_ap, c0, mask in keys:
                            n = k_ap.shape[1]
                            src, dst = flat[:, base + c0:base + c0 + n], sc[:, b, at_sc:at_sc + n]
                            if mask is None:
                                ins = dve.tensor_scalar(dst, src, scale, None, ALU.mult)
                            else:
                                ins = dve.scalar_tensor_tensor(dst, src, scale, mask, ALU.mult, ALU.add)
                            at_sc += n
                            if (k_ap is keys[-1][0]):
                                sig(ins, "scaled")
                            else:
                                marks.append(v_order.mark(ins))
                        wait(dve, "scaled", j + 1)
                        if marks:
                            dve.wait_ge(v_order.sem, marks[-1])
                        m = stat[:, b, 0:1]
                        v_order.step(dve, dve.tensor_reduce(m, sc[:, b, 0:width], AX_X, ALU.max))
                        if sink is not None:
                            v_order.step(dve, dve.tensor_tensor(m, m, sink, ALU.max))
                        sig(dve.tensor_scalar(m, m, -1.0, None, ALU.mult), "max")

                    def norm(j):
                        _, _, width, _, sink, _ = jobs[j]
                        b = j % 2
                        wait(dve, "exp", j + 1)
                        den = stat[:, b, 1:2]
                        if sink is not None:
                            v_order.step(dve, dve.tensor_tensor(den, den, stat[:, b, 2:3], ALU.add))
                        v_order.step(dve, dve.reciprocal(den, den))
                        sig(dve.tensor_scalar(sc[:, b, 0:width], sc[:, b, 0:width], den, None, ALU.mult), "norm")

                    top(0)
                    for j in range(n_jobs):
                        if j + 1 < n_jobs:
                            top(j + 1)
                        norm(j)

                @block.scalar
                def _(act):
                    def expo(j):
                        _, _, width, _, sink, _ = jobs[j]
                        b = j % 2
                        wait(act, "max", j + 1)
                        if sink is not None:
                            a_order.step(act, act.activation(stat[:, b, 2:3], sink, ACT.Exp, bias=stat[:, b, 0:1]))
                        sig(act.activation(sc[:, b, 0:width], sc[:, b, 0:width], ACT.Exp, bias=stat[:, b, 0:1],
                                           accum_out=stat[:, b, 1:2]), "exp")

                    def take(j):
                        width, o = jobs[j][2], jobs[j][5]
                        wait(act, "turned", j + 1)
                        if j >= 2:
                            wait(act, "pv", j - 1)
                        sig(act.activation(pt[:, j % 2, 0:width], flat[:, 2048:2048 + width], ACT.Copy),
                            "turned_out")
                        if j >= 1:
                            give(j - 1)

                    def give(j):
                        o = jobs[j][5]
                        p0, d = o.start_partition(), o.shape[0]
                        wait(act, "pv", j + 1)
                        sig(act.activation(o, ps[p0:p0 + d, 6 + j % 2, 0:P], ACT.Copy), "pv_out")

                    expo(0)
                    for j in range(n_jobs):
                        if j + 1 < n_jobs:
                            expo(j + 1)
                        take(j)
                    give(n_jobs - 1)
            for n in R:
                R[n].close(n_jobs)

        groups = [([ctx2_in[:, c, k * P:(k + 1) * P] for c in range(NCTX)], xT[:, k, LAT:TOK]) for k in range(KT)]
        with nc.Block() as block:
            @block.sync
            def _(sp):
                sp.dma_start(ctx2_in, w["ctx_2"][0].rearrange("(c p) d -> p c d", p=P)).then_inc(loaded.sem, 16)

            @block.tensor
            def _(pe):
                pe.wait_ge(loaded.sem, loaded.at(16))
                transpose_pe(pe, groups)

            @block.vector
            def _(dve):
                transpose_out(dve, groups, 0)

            @block.scalar
            def _(act):
                transpose_out(act, groups, 1)
        loaded.close(16)
        transpose_close(groups)
        ada_stage(1, W["ada0"], COL["b_ada2_0"], (COL["norm1_0"], COL["norm2_0"]))
        modulate(0, False, xT, BOTH)
        if end("mod2"):
            return

        def part(n, pattern, **kw):
            nonlocal_o[0] += n
            assert nonlocal_o[0] <= 24576
            return big[:, nonlocal_o[0] - n:nonlocal_o[0]].rearrange(pattern, **kw)
        nonlocal_o = [0]
        qa = part(4 * TOK, "p (t n) -> p t n", t=4)
        ka = part(4 * TOK, "p (t n) -> p t n", t=4)
        va = part(NCH * 4 * 129, "p (c h e) -> p c h e", c=NCH, h=4)
        oa = part(4 * TOK, "p (t n) -> p t n", t=4)
        qb = part(4 * TOK, "p (t n) -> p t n", t=4)
        kb = part(2 * TOK, "p (t n) -> p t n", t=2)
        vb = part(NCH * P, "p (c n) -> p c n", c=NCH)
        k_tok = part(NCH * 512, "p (c n) -> p c n", c=NCH)
        free0 = nonlocal_o[0]
        units = []
        for buf, sc_ in ((qa, None), (ka, float(P) ** -0.5)):
            for s in range(2):
                units.append([("tile", m, t0, nt, buf[:, 2 * s + m, t0:t0 + nt], sc_)
                              for m in range(2) for t0, nt in BOTH])
        for s in range(2):
            units.append([("rows", c, 0, SLAB, va[:, c, 2 * s:2 * s + 2, 0:P], None) for c in range(NCH)])
        for buf in (oa, qb):
            for s in range(2):
                units.append([("tile", m, t0, nt, buf[:, 2 * s + m, t0:t0 + nt], None)
                              for m in range(2) for t0, nt in BOTH])
        units.append([("tile", 0, t0, nt, kb[:, 0, t0:t0 + nt], None) for t0, nt in BOTH] +
                     [("rows", c, P, P, vb[:, c, :], None) for c in range(NCH)])
        with nc.Block() as block:
            @block.gpsimd
            def _(pool):
                pool.memset(va, 1.0)
        units_stage(W["ab"], units, w["ab_w_in_2"][0, :, AB_G:AB_G + 16], rows[:, GATE_B:GATE_B + 16])
        if end("ab_in"):
            return

        log_f = by_chunk(dt)
        fs = lambda a: by_chunk(a).rearrange("p c (d k h) -> p c d k h", d=2, k=2)[:, :, :, 1, :]
        raw = big[0:4, free0:free0 + 4 * TOK].rearrange("p (k n) -> p k n", k=4)
        with nc.Block() as block:
            @block.vector
            def _(dve):
                v_order.step(dve, dve.scalar_tensor_tensor(t_a, dt, -1.0, dt, ALU.mult, ALU.max))
                dve_abs[0] = v_order.n
                dve.wait_ge(S["exp_ln"].sem, S["exp_ln"].at(1))
                v_order.step(dve, dve.tensor_scalar(t_b, t_a, 1.0, None, ALU.add))
                dve_abs[1] = v_order.n
                v_order.step(dve, dve.tensor_scalar(dA, t_b, -1.0, None, ALU.add))
                dve.wait_ge(S["exp_ln"].sem, S["exp_ln"].at(2))
                v_order.step(dve, dve.tensor_scalar(t_b, dA, 0.0, None, ALU.is_equal))
                v_order.step(dve, dve.tensor_tensor(t_c, t_c, t_b, ALU.add))
                v_order.step(dve, dve.tensor_tensor(dA, dA, t_b, ALU.add))
                v_order.step(dve, dve.reciprocal(dA, dA))
                v_order.step(dve, dve.tensor_tensor(t_c, t_c, dA, ALU.mult))
                v_order.step(dve, dve.tensor_tensor(t_c, t_c, t_a, ALU.mult))
                v_order.step(dve, dve.tensor_scalar(t_b, dt, 0.0, None, ALU.min))
                v_order.step(dve, dve.tensor_tensor(t_b, t_b, t_c, ALU.subtract))
                for d in range(2):
                    o = 8 * d + 4
                    v_order.step(dve, dve.tensor_copy(by_chunk(dt)[:, :, o:o + 4], by_chunk(t_b)[:, :, o:o + 4]))

            @block.scalar
            def _(act):
                act.wait_ge(v_order.sem, dve_abs[0])
                act.activation(t_a, t_a, ACT.Exp, scale=-1.0).then_inc(S["exp_ln"].sem, 1)
                act.wait_ge(v_order.sem, dve_abs[1])
                act.activation(t_c, t_b, ACT.Ln).then_inc(S["exp_ln"].sem, 1)
        S["exp_ln"].close(2)
        groups = []
        for kind in range(4):
            lat = [dt[:, c * 16 + kind * 4:c * 16 + kind * 4 + 4] for c in range(NCH)]
            groups.append((lat[0:NLAT], raw[:, kind, 0:LAT]))
            groups.append((lat[NLAT:], raw[:, kind, LAT:TOK]))
        for c in range(NCH):
            groups.append(([ka[:, h, c * CH:(c + 1) * CH] for h in range(4)], k_tok[:, c, :]))
        with nc.Block() as block:
            @block.tensor
            def _(pe):
                transpose_pe(pe, groups)

            @block.vector
            def _(dve):
                transpose_out(dve, groups, 0)

            @block.scalar
            def _(act):
                transpose_out(act, groups, 1)
        transpose_close(groups)

        row_m = squares[:, :, :].rearrange("p a n -> p (a n)")[0:4, 0:2 * TOK].rearrange("p (q n) -> p q n", q=2)
        one_row = ones[0:4, :]
        m_col = small[0:4, 480:482]
        b_row = mean[0:4, 0:CH]
        r_row = mean[0:4, CH:2 * CH]
        g_row = mean[0:4, 2 * CH:3 * CH]
        with nc.Block() as block:
            @block.vector
            def _(dve):
                v_order.step(dve, dve.memset(m_col, 0.0))
                for d in range(2):
                    for c in order_of[d]:
                        view = lambda a: a[:, ::-1] if d else a
                        cut = lambda a: view(a[:, c * CH:(c + 1) * CH])
                        last = (lambda a: a[:, 0:1]) if d else (lambda a: a[:, CH - 1:CH])
                        ii, ff = raw[:, 2 * d, :], raw[:, 2 * d + 1, :]
                        m = m_col[:, d:d + 1]
                        v_order.step(dve, dve.tensor_tensor_scan(view(b_row), one_row, cut(ff), 0.0,
                                                                 ALU.mult, ALU.add))
                        v_order.step(dve, dve.tensor_tensor(r_row, ii[:, c * CH:(c + 1) * CH], b_row, ALU.subtract))
                        v_order.step(dve, dve.tensor_tensor_scan(view(g_row), view(r_row), view(r_row), m,
                                                                 ALU.max, ALU.max))
                        v_order.step(dve, dve.tensor_scalar(ii[:, c * CH:(c + 1) * CH], g_row, -1.0, m,
                                                            ALU.mult, ALU.add))
                        v_order.step(dve, dve.tensor_tensor(ff[:, c * CH:(c + 1) * CH], b_row, g_row, ALU.add))
                        v_order.step(dve, dve.tensor_scalar(row_m[:, d, c * CH:(c + 1) * CH], r_row, m, None,
                                                            ALU.subtract))
                        v_order.step(dve, dve.tensor_copy(m, last(ff[:, c * CH:(c + 1) * CH])))
        if end("rows"):
            return

        nonlocal_o[0] = free0 + 0
        part(4 * TOK, "p (k n) -> p k n", k=4)
        wide = lambda b: b.rearrange("p h n -> p (h n)")
        c_state = [t[:, 0:4 * 129].rearrange("p (h e) -> p h e", h=4) for t in (mean, rstd)]
        hfree = hT[:, 4:8, :].rearrange("p t n -> p (t n)")
        pmat, iw, em, qs, kw, hd = (hfree[:, i * 512:(i + 1) * 512].rearrange("p (h n) -> p h n", h=4)
                                    for i in range(6))
        rp_col = small[:, 0:4]
        w_col = small[:, 4:8]
        order_m = [(d, order_of[d][k], k) for k in range(NCH) for d in range(2)]
        R = named("bc", "cols", "rp", "seg", "p_exp", "p", "em", "w", "masked", "m", "qs", "kw", "mem", "h", "iw")
        n_m = len(order_m)
        chunk4 = lambda buf, c: buf[:, :, c * CH:(c + 1) * CH]
        with nc.Block() as block:
            @block.tensor
            def _(pe):
                for s, (d, c, k) in enumerate(order_m):
                    t0 = c * CH
                    if s >= 1:
                        wait(pe, "m", s)
                        wait(pe, "em", s)
                        wait(pe, "iw", s)
                        wait(pe, "rp", s)
                        wait(pe, "w", s)
                    for h in range(4):
                        pe.matmul(ps[:, 0, h * P:(h + 1) * P], mats[0:4, SEL + h, :], raw[:, 2 * d, t0:t0 + CH],
                                  start=True, stop=True)
                        pe.matmul(ps[:, 1, h * P:(h + 1) * P], mats[0:4, SEL + h, :], raw[:, 2 * d + 1, t0:t0 + CH],
                                  start=True, stop=True)
                    sig(pe.transpose(ps[:, 7, 0:4], row_m[:, d, t0:t0 + CH], ident[0:4, 0:4]), "bc")
                    for h in range(4):
                        ins = pe.matmul(ps[:, 2, h * P:(h + 1) * P], ka[:, h, t0:t0 + CH], qa[:, h, t0:t0 + CH],
                                        start=True, stop=True)
                    sig(ins, "cols")
                    wait(pe, "m", s + 1)
                    wait(pe, "qs", s + 1)
                    if s >= 1:
                        wait(pe, "h", s)
                        wait(pe, "mem", s - 1) if s >= 2 else None
                    for h in range(4):
                        o, dn = ps[:, 3, h * P:(h + 1) * P], ps[:, 4, h * P:(h + 1) * P]
                        pe.matmul(o, va[:, c, h, 0:P], pmat[:, h, :], start=True, stop=False)
                        pe.matmul(o, c_state[d][:, h, 0:P], qs[:, h, :], start=False, stop=True)
                        pe.matmul(dn, ones, pmat[:, h, :], start=True, stop=False)
                        ins = pe.matmul(dn, c_state[d][:, h, P:P + 1].to_broadcast([P, P]), qs[:, h, :],
                                        start=False, stop=True)
                    sig(ins, "p")
                    wait(pe, "kw", s + 1)
                    if s >= 1:
                        wait(pe, "mem", s)
                    for h in range(4):
                        ins = pe.matmul(ps[:, 5 + h // 2, (h % 2) * 129:(h % 2) * 129 + 129], kw[:, h, :],
                                        va[:, c, h, :], start=True, stop=True)
                    sig(ins, "masked")

            @block.vector
            def _(dve):
                for st in c_state:
                    v_order.step(dve, dve.memset(st, 0.0))
                for s, (d, c, k) in enumerate(order_m):
                    tri = (U_LE, U_GE)[d]
                    edge = 0 if d else CH - 1
                    wait(dve, "bc", s + 1)
                    sig(dve.tensor_copy(rp_col, ps[:, 7, 0:4]), "rp")
                    wait(dve, "rp", s + 1)
                    wait(dve, "iw", s + 1)
                    last_a = ps[:, 0, :].rearrange("p (h n) -> p h n", h=4)[:, :, edge]
                    sig(dve.tensor_tensor(w_col, last_a, rp_col, ALU.add), "w")
                    for h in range(4):
                        ins = dve.tensor_scalar(pmat[:, h, :], ps[:, 0, h * P:(h + 1) * P], rp_col[:, h:h + 1], 0.0,
                                                ALU.add, ALU.min)
                    sig(ins, "seg")
                    wait(dve, "p_exp", s + 1)
                    sig(dve.tensor_tensor(qs, chunk4(qa, c), iw, ALU.mult), "qs")
                    v_order.step(dve, dve.tensor_tensor(
                        pmat, pmat, mats[:, tri, :].unsqueeze(1).to_broadcast([P, 4, P]), ALU.mult))
                    wait(dve, "cols", s + 1)
                    sig(dve.tensor_tensor(wide(pmat), wide(pmat), ps[:, 2, :], ALU.mult), "m")
                    wait(dve, "p", s + 1)
                    wait(dve, "em", s + 1)
                    v_order.step(dve, dve.tensor_tensor(wide(hd), ps[:, 4, :], wide(em), ALU.max))
                    v_order.step(dve, dve.scalar_tensor_tensor(wide(hd), ps[:, 4, :], -1.0, wide(hd),
                                                               ALU.mult, ALU.max))
                    v_order.step(dve, dve.reciprocal(wide(hd), wide(hd)))
                    dst = chunk4(hT[:, 0:4, :], c)
                    num = ps[:, 3, :].rearrange("p (h n) -> p h n", h=4)
                    seen = any(x[1] == c for x in order_m[:s])
                    if seen:
                        v_order.step(dve, dve.tensor_tensor(hd, num, hd, ALU.mult))
                        sig(dve.tensor_tensor(dst, dst, hd, ALU.add), "h")
                    else:
                        sig(dve.tensor_tensor(dst, num, hd, ALU.mult), "h")
                    wait(dve, "h", s + 1)
                    wait(dve, "masked", s + 1)
                    for h in range(4):
                        st = c_state[d][:, h, :]
                        ins = dve.scalar_tensor_tensor(st, st, iw[:, h, edge:edge + 1],
                                                       ps[:, 5 + h // 2, (h % 2) * 129:(h % 2) * 129 + 129],
                                                       ALU.mult, ALU.add)
                    sig(ins, "mem")
                    wait(dve, "mem", s + 1)

            @block.scalar
            def _(act):
                for s, (d, c, k) in enumerate(order_m):
                    wait(act, "bc", s + 1)
                    if s >= 1:
                        wait(act, "mem", s)
                    sig(act.activation(wide(iw), ps[:, 0, :], ACT.Exp), "iw")
                    sig(act.activation(wide(em), ps[:, 1, :], ACT.Exp, scale=-1.0), "em")
                    wait(act, "w", s + 1)
                    a_order.step(act, act.activation(w_col, w_col, ACT.Exp))
                    wait(act, "seg", s + 1)
                    sig(act.activation(wide(pmat), wide(pmat), ACT.Exp), "p_exp")

            @block.gpsimd
            def _(pool):
                for s, (d, c, k) in enumerate(order_m):
                    wait(pool, "p_exp", s + 1)
                    if s >= 1:
                        wait(pool, "masked", s)
                    sig(pool.tensor_tensor(kw, k_tok[:, c, :].rearrange("p (h n) -> p h n", h=4),
                                           w_col.unsqueeze(2).to_broadcast([P, 4, P]), ALU.mult), "kw")
        for n in R:
            R[n].close(n_m)
        if end("mlstm"):
            return

        jobs = [(hT[:, t, t0:t0 + n], n, cols[:, COL["mlstm_norm"] + t:COL["mlstm_norm"] + t + 1])
                for t in range(4) for t0, n in BOTH]
        with nc.Block() as block:
            @block.scalar
            def _(act):
                for t in range(4):
                    act.activation(oa[:, t, :], oa[:, t, :], ACT.Sigmoid)
        head_norms(jobs, ones, 128)
        with nc.Block() as block:
            @block.vector
            def _(dve):
                for t in range(4):
                    dve.tensor_tensor(hT[:, t, :], hT[:, t, :], oa[:, t, :], ALU.mult)

            @block.sync
            def _(sp):
                sp.dma_start(qa[:, 0:2, 0:LAT], w["const_tables"][T_CB:T_CB + 2].rearrange("t p n -> p t n"))\
                  .then_inc(loaded.sem, 16)
                sp.wait_ge(loaded.sem, loaded.at(16))
        loaded.close(16)

        jobs = [(buf[:, t, t0:t0 + n], n, cols[:, COL[g]:COL[g] + 1])
                for buf, nt, g in ((qb, 4, "swa_q"), (kb, 1, "swa_k")) for t in range(nt) for t0, n in BOTH]
        head_norms(jobs, blk64, 64)
        rope([qb[:, t, 0:LAT] for t in range(4)] + [kb[:, 0, 0:LAT]], ROT32, qa[:, 0, 0:LAT], qa[:, 1, 0:LAT])
        named("swapped")
        with nc.Block() as block:
            @block.tensor
            def _(pe):
                for r, (t0, n) in enumerate(BOTH):
                    ins = pe.matmul(ps[:, r, 0:n], mats[:, SWAP, :], kb[:, 0, t0:t0 + n], start=True, stop=True)
                ins.then_inc(S["swapped"].sem, 1)

            @block.vector
            def _(dve):
                dve.wait_ge(S["swapped"].sem, S["swapped"].at(1))
                for r, (t0, n) in enumerate(BOTH):
                    dve.tensor_copy(kb[:, 1, t0:t0 + n], ps[:, r, 0:n])
        S["swapped"].close(1)
        bufs = (ka.rearrange("p t n -> p (t n)")[:, 0:2 * TOK].rearrange("p (b n) -> p b n", b=2),
                ka.rearrange("p t n -> p (t n)")[:, 2 * TOK:4 * TOK].rearrange("p (b n) -> p b n", b=2),
                small[:, 0:16].rearrange("p (b n) -> p b n", b=2))
        jobs = []
        for h in range(B_HEADS):
            kv, half = h // (B_HEADS // 2), h % 2
            rows_h = slice(64 * half, 64 * half + 64)
            keys_t = kb[rows_h, 0 if kv == half else 1, :]
            for n in range(NCH):
                keys, v, width = [], [], 0
                if n < NLAT:
                    for kn, mask in ((n - 1, M_PREV), (n, None), (n + 1, M_NEXT)):
                        if 0 <= kn < NLAT:
                            keys.append((keys_t[:, kn * CH:(kn + 1) * CH], width,
                                         None if mask is None else mats[:, mask, :]))
                            v.append(vb[:, kn, kv * 64:(kv + 1) * 64])
                            width += CH
                keys.append((keys_t[:, LAT:TOK], 512, None))
                v += [vb[:, NLAT + i, kv * 64:(kv + 1) * 64] for i in range(NCTX)]
                width += CTX
                jobs.append((qb[rows_h, h // 2, n * CH:(n + 1) * CH], keys, width, v,
                             rows[:, SINK + h:SINK + h + 1],
                             hT[rows_h, 4 + h // 2, n * CH:(n + 1) * CH]))
        attention(jobs, 64.0 ** -0.5, bufs)
        if end("mix2"):
            return
        product_stage(W["ab_out"], 4, whole, from_h, BOTH, add_gated(16), "vector")
        modulate(1, False, xT, BOTH)
        mlp(0, BOTH)
        if end("layer0"):
            return

        ada_stage(1, W["ada1"], COL["b_ada2_1"], (COL["norm1_1"], COL["norm2_1"]))
        modulate(0, False, xT, BOTH)
        nonlocal_o[0] = 0
        qc = part(8 * LAT, "p (t n) -> p t n", t=8)
        kc = part(2 * TOK, "p (t n) -> p t n", t=2)
        vc = part(NCH * SLAB, "p (c n) -> p c n", c=NCH)
        tabs = part(2 * LAT, "p (t n) -> p t n", t=2)
        bufs = (part(2 * TOK, "p (b n) -> p b n", b=2), part(2 * TOK, "p (b n) -> p b n", b=2),
                small[:, 0:16].rearrange("p (b n) -> p b n", b=2))
        units = [[("tile", m, 0, LAT, qc[:, 2 * s + m, :], None) for m in range(2)] for s in range(4)]
        units.append([("tile", m, t0, nt, kc[:, m, t0:t0 + nt], None) for m in range(2) for t0, nt in BOTH])
        units.append([("rows", c, 0, SLAB, vc[:, c, :], None) for c in range(NCH)])
        with nc.Block() as block:
            @block.sync
            def _(sp):
                sp.dma_start(tabs, w["const_tables"][T_CC:T_CC + 2].rearrange("t p n -> p t n"))\
                  .then_inc(loaded.sem, 16)
                sp.wait_ge(loaded.sem, loaded.at(16))
        loaded.close(16)
        units_stage(W["c"], units, None, None)
        jobs = [(qc[:, t, :], LAT, cols[:, COL["c_q_norm"]:COL["c_q_norm"] + 1]) for t in range(8)] + \
               [(kc[:, t, t0:t0 + n], n, cols[:, COL["c_k_norm"]:COL["c_k_norm"] + 1])
                for t in range(2) for t0, n in BOTH]
        head_norms(jobs, ones, 128)
        rope([qc[:, t, :] for t in range(8)] + [kc[:, t, 0:LAT] for t in range(2)], ROT64,
             tabs[:, 0, :], tabs[:, 1, :])
        jobs = []
        for h in range(8):
            kv = h // 4
            for n in range(NLAT):
                keys = [(kc[:, kv, 0:LAT], 0, None), (kc[:, kv, LAT:TOK], 512, None)]
                v = [vc[:, c, kv * P:(kv + 1) * P] for c in range(NCH)]
                jobs.append((qc[:, h, n * CH:(n + 1) * CH], keys, TOK, v, None, hT[:, h, n * CH:(n + 1) * CH]))
        attention(jobs, 128.0 ** -0.5, bufs)
        if end("mix3"):
            return
        product_stage(W["c_out"], 4, whole, from_h, ONLY_LAT, add_gated(16), "vector")
        modulate(1, False, xT, ONLY_LAT)
        mlp(1, ONLY_LAT)

        y_out = big[:, 0:NLAT * D].rearrange("p (c d) -> p c d", c=NLAT)
        groups = [([xT[:, k, c * CH:(c + 1) * CH] for k in range(4 * q, 4 * q + 4)],
                   y_out[:, c, q * 512:(q + 1) * 512]) for c in range(NLAT) for q in range(2)]
        with nc.Block() as block:
            @block.tensor
            def _(pe):
                transpose_pe(pe, groups)

            @block.vector
            def _(dve):
                transpose_out(dve, groups, 0)

            @block.scalar
            def _(act):
                transpose_out(act, groups, 1)

            @block.sync
            def _(sp):
                for c in range(NLAT):
                    sp.wait_ge(tr_free_v.sem, tr_free_v.at(c + 1))
                    sp.wait_ge(tr_free_a.sem, tr_free_a.at(c + 1))
                    sp.dma_start(out[0, c * CH:(c + 1) * CH, :], y_out[:, c, :]).then_inc(stored.sem, 16)
                sp.wait_ge(stored.sem, stored.at(16 * NLAT))
        transpose_close(groups)


_INS = ["x", "c", "ctx", "c_ctx", "w_ada", "b_ada", "w_in", "ssd_conv_w", "ssd_conv_b", "ssd_dt_bias",
        "ssd_a_log", "ssd_d", "ssd_norm_w", "fnet_w", "pool_w", "pool_scale", "w_out", "ln1_g", "ln1_b",
        "ffn_w_up", "ffn_conv_w", "ffn_conv_b", "ffn_w_down", "ln2_g", "ln2_b", "c_2", "ctx_2", "c_ctx_2",
        "ada_w_2", "ada_b_2", "norm1_g_2", "norm2_g_2", "ab_w_in_2", "ab_gate_b_2", "mlstm_norm_g_2",
        "swa_q_norm_g_2", "swa_k_norm_g_2", "swa_sink_2", "ab_w_out_2", "c_w_in_2", "c_q_norm_g_2",
        "c_k_norm_g_2", "c_w_out_2", "mlp_w1_2", "mlp_w2_2"]


def kernel(**inputs):
    import concourse.bacc as bacc
    from concourse.bass_utils import run_bass_kernel_spmd

    nc = bacc.Bacc("TRN2", target_bir_lowering=False, num_devices=1)
    arrays, w = {}, {}
    data = {n: np.ascontiguousarray(inputs[n]) for n in _INS}
    data["const_mats"], data["const_tables"], data["const_dft"] = shape_constants()
    for name, a in data.items():
        arrays[f"in_{name}"] = a
        w[name] = nc.dram_tensor(f"in_{name}", a.shape, mybir.dt.from_np(a.dtype), kind="ExternalInput").ap()
    out = nc.dram_tensor("out_0", (1, LAT, D), F32, kind="ExternalOutput").ap()
    program(nc, w, out)
    r = run_bass_kernel_spmd(nc, [arrays], core_ids=[0])
    return r.results[0]["out_0"]
```

```python
from contextlib import ExitStack

import numpy as np
import concourse.bass as bass
from concourse import mybir

F32 = mybir.dt.float32
F32R = mybir.dt.float32r
ALU = mybir.AluOpType
ACT = mybir.ActivationFunctionType
AX_X = mybir.AxisListType.X

P = 128
D = 1024
KT = D // P
LAT, CTX = 512, 256
TOK = LAT + CTX
CH = 128
NLAT, NCTX = LAT // CH, CTX // CH
NCH = NLAT + NCTX
BOTH = [(0, LAT), (LAT, CTX)]
ONLY_LAT = [(0, LAT)]
GRID_W = 64
GRID_H = LAT // GRID_W
EPS = 1e-6
ALPHA = 2.0 ** 0.25

SLAB = 256
NS = 4
D_FF = 2816
FT = D_FF // P
D_FF2 = 4096
MT = D_FF2 // P
OFF_XBC, OFF_DT, OFF_FNET, OFF_POOL = 512, 1536, 1552, 1808
N_CONV = 8
A_HEADS = 4
B_HEADS = 8
AB_O, AB_G, AB_QB, AB_KB = 1536, 2048, 2064, 2576

(IDENT, ONES, BLK64, U_LE, U_GE, ROT32, ROT64, SWAP, M_PREV, M_NEXT, DFT_C, DFT_S, SEL, TINY) = range(14)
N_MATS = SEL + A_HEADS + 1
TINY = SEL + A_HEADS
T_CB, T_SB, T_CC, T_SC, T_CNT = 0, 1, 2, 3, 4
NEG = -1e30


def shape_constants():
    i = np.arange(P)
    m = np.zeros((N_MATS, P, P), np.float64)
    m[IDENT] = np.eye(P)
    m[ONES] = 1
    m[BLK64] = i[:, None] // 64 == i[None, :] // 64
    m[U_LE] = i[:, None] <= i[None, :]
    m[U_GE] = i[:, None] >= i[None, :]
    for n, half in ((ROT32, 32), (ROT64, 64)):
        for f in range(P):
            up = f % (2 * half) < half
            m[n, f + half if up else f - half, f] = -1 if up else 1
    m[SWAP] = np.roll(np.eye(P), 64, axis=0)
    m[M_PREV] = np.where(i[None, :] >= i[:, None], 0, NEG)
    m[M_NEXT] = np.where(i[None, :] <= i[:, None], 0, NEG)
    ang = 2 * np.pi * ((i[:, None] * i[None, :]) % 64) / 64
    ortho = 1 / np.sqrt(LAT * 64)
    m[DFT_C] = m[BLK64] * np.cos(ang) * ortho
    m[DFT_S] = -m[BLK64] * np.sin(ang) * ortho
    for h in range(A_HEADS):
        m[SEL + h, h] = 1
    m[TINY, :, 0] = EPS
    for q in range(4):
        m[TINY, 32 * q + np.arange(16), 1 + np.arange(16)] = 1
    t = np.zeros((6, P, LAT), np.float64)
    pos = np.arange(LAT)
    for n, head in ((T_CB, 64), (T_CC, 128)):
        pairs = head // 4
        inv = (np.float32(10000.0) ** (-np.arange(pairs, dtype=np.float32) / pairs)).astype(np.float32)
        ang = np.concatenate([(pos // GRID_W)[:, None].astype(np.float32) * inv,
                              (pos % GRID_W)[:, None].astype(np.float32) * inv], axis=1).T.astype(np.float64)
        ang = np.tile(ang, (P // (head // 2), 1))
        t[n], t[n + 1] = np.cos(ang), np.sin(ang)
    for g, win in enumerate((2, 4, 8, 16)):
        left = win // 2
        hi, lo = np.minimum(pos + win - left, LAT), np.maximum(pos - left, 0)
        t[T_CNT + g // 2, (g % 2) * 64:(g % 2) * 64 + 64] = 1.0 / (hi - lo)
    ang = 2 * np.pi * ((pos[:, None] * pos[None, :]) % LAT) / LAT
    dft = np.stack([np.cos(ang), np.sin(ang)])
    return m.astype(np.float32), t.astype(np.float32), dft.astype(np.float32)


class Tally:

    def __init__(self, sem):
        self.sem, self.base = sem, 0

    def at(self, n):
        return self.base + n

    def close(self, n):
        self.base += n


class Order:

    def __init__(self, sem):
        self.sem, self.n = sem, 0

    def mark(self, ins):
        ins.then_inc(self.sem, 1)
        self.n += 1
        return self.n

    def step(self, eng, ins):
        eng.wait_ge(self.sem, self.mark(ins))


def program(nc, w, out):
    ctx = ExitStack()
    with ctx:
        def sb(name, shape, scope=None, dtype=F32):
            return (scope or ctx).enter_context(nc.sbuf_tensor(name, shape, dtype))

        def tally(name):
            return Tally(ctx.enter_context(nc.semaphore(name)))

        def order(name):
            return Order(ctx.enter_context(nc.semaphore(name)))

        xT = sb("xT", [P, KT, TOK])
        ring = sb("ring", [P, NS, KT, SLAB])
        mean = sb("mean", [P, TOK])
        rstd = sb("rstd", [P, TOK])
        squares = sb("squares", [P, 3, LAT])
        mats = sb("mats", [P, N_MATS, P])
        cols = sb("cols", [P, 768])
        mods = sb("mods", [P, 3, 48, 2])
        scls = sb("scls", [P, 3, 2, 8, 2])
        sil = sb("sil", [P, 2, 8, 32])
        ada_rows = sb("ada_rows", [P, 2, SLAB])
        rows = sb("rows", [P, 64])
        dskip = sb("dskip", [P, 4])
        small = sb("small", [P, 512])
        wnarrow = sb("wnarrow", [P, KT, 16])
        ps = ctx.enter_context(nc.psum_tensor("ps", [P, 8, 512], F32))

        def mixer_memory(scope, name):
            return sb("hT" + name, [P, KT, TOK], scope), sb("big" + name, [P, 24576], scope)

        mixer = ctx.enter_context(ExitStack())
        hT, big = mixer_memory(mixer, "0")

        ident, ones, blk64 = mats[:, IDENT, :], mats[:, ONES, :], mats[:, BLK64, :]
        eps_col = mats[:, TINY, 0:1]
        sum_groups = mats[:, TINY, 1:17]
        cur = [0]

        slot_loaded = [ctx.enter_context(nc.semaphore(f"slot_loaded{s}")) for s in range(NS)]
        mm_done = ctx.enter_context(nc.semaphore("mm_done"))
        loaded = tally("loaded")
        stored = tally("stored")
        mm_free = tally("mm_free")
        mm_free_v = tally("mm_free_v")
        tr_ready, tr_free_v, tr_free_a = tally("tr_ready"), tally("tr_free_v"), tally("tr_free_a")
        v_order, a_order, g_order = order("v_order"), order("a_order"), order("g_order")
        N = {n: tally("norm_" + n) for n in ("sum", "mean", "centered", "sq", "sq_used", "std", "scaled", "out", "hi", "lo", "recip")}
        S = {}

        def named(*names):
            for n in names:
                if n not in S:
                    S[n] = tally(n)
            return {n: S[n] for n in names}

        stream = []
        signals = [0]

        def add_slabs(name, layer, row_groups, col_starts, n_signals):
            first = len(stream)
            for j, c in enumerate(col_starts):
                for r0, kt in row_groups:
                    stream.append((name, layer, r0, kt, c))
                    signals.append(signals[-1] + (n_signals[j] if isinstance(n_signals, list) else n_signals))
            return first

        whole = [(0, KT)]
        cols_of = lambda start, n: [start + SLAB * i for i in range(n)]
        W = {}
        W["ada"] = add_slabs("w_ada", 0, whole, cols_of(0, 24), 1)
        W["in"] = add_slabs("w_in", 0, whole, cols_of(OFF_XBC, 4) + cols_of(0, 2) + [OFF_FNET, OFF_POOL],
                            [4, 4, 4, 2, 2, 2, 2, 2])
        W["out"] = add_slabs("w_out", 0, whole, cols_of(0, 4), 2)
        W["up"] = len(stream)
        for j in range(FT // 2):
            add_slabs("ffn_w_up", 0, whole, [SLAB * j, D_FF + SLAB * j], 2)
            add_slabs("ada_w_2", 0, whole, cols_of(2 * SLAB * j, 2), 1)
        add_slabs("ada_w_2", 0, whole, cols_of(2 * SLAB * (FT // 2), 2), 1)
        DOWN_ROWS = [(0, 8), (1024, 8), (2048, 6)]
        W["down"] = add_slabs("ffn_w_down", 0, DOWN_ROWS, cols_of(0, 4), 2)
        W["ab"] = add_slabs("ab_w_in_2", 0, whole,
                            cols_of(0, 4) + cols_of(1024, 4) + cols_of(AB_QB, 2) + [AB_KB],
                            [4] * 4 + [NCH] * 2 + [4] * 2 + [4] * 2 + [2 + NCH])
        W["ab_out"] = add_slabs("ab_w_out_2", 0, whole, cols_of(0, 4), 4)
        W["mlp_0"], ada_col = len(stream), [0]
        for q in range(4):
            for j in range(4):
                add_slabs("mlp_w1_2", 0, whole, [1024 * q + SLAB * j], 4)
                for _ in range(1 if q else (2, 2, 2, 3)[j]):
                    add_slabs("ada_w_2", 1, whole, [ada_col[0]], 1)
                    ada_col[0] += SLAB
            for j in range(4):
                add_slabs("mlp_w2_2", 0, [(1024 * q, KT)], [SLAB * j], 4)
                if q == 0 and j < 3:
                    add_slabs("ada_w_2", 1, whole, [ada_col[0]], 1)
                    ada_col[0] += SLAB
        W["c"] = add_slabs("c_w_in_2", 0, whole, cols_of(0, 6), [2] * 4 + [4, NCH])
        W["c_out"] = add_slabs("c_w_out_2", 0, whole, cols_of(0, 4), 2)
        W["mlp_1"] = len(stream)
        for q in range(4):
            add_slabs("mlp_w1_2", 1, whole, cols_of(1024 * q, 4), 2)
            add_slabs("mlp_w2_2", 1, [(1024 * q, KT)], cols_of(0, 4), 2)
        issued = [0]

        def slab_source(entry, i=None, d_row=0, d_col=0):
            name, layer, r0, kt, c = entry
            if i is None:
                return w[name][layer, r0:r0 + kt * P, c:c + SLAB].rearrange("(k p) n -> p k n", p=P)
            m = w[name][layer]
            if d_row:
                m = m[bass.ds(i * d_row + r0, kt * P), :]
            else:
                m = m[r0:r0 + kt * P, :]
            m = m.rearrange("(k p) n -> p k n", p=P)
            return m[:, :, bass.ds(i * d_col + c, SLAB)] if d_col else m[:, :, c:c + SLAB]

        def load_slabs(sp, upto):
            upto = min(upto, len(stream))
            n = issued[0]

            def one(n, i=None, step=(0, 0), per_turn=0):
                if n >= NS:
                    used = signals[n - NS + 1]
                    sp.wait_ge(mm_done, used if i is None else i * per_turn + used)
                sp.dma_start(ring[:, n % NS, 0:stream[n][3], :], slab_source(stream[n], i, *step))\
                  .then_inc(slot_loaded[n % NS], 16)

            def turns_alike(n, period):
                if n < NS or n + 2 * period > upto:
                    return 1, None, 0
                steps = [(stream[n + period + s][2] - stream[n + s][2], stream[n + period + s][4] - stream[n + s][4])
                         for s in range(period)]
                per_turn = signals[n] - signals[n - NS] if period == NS else signals[n + period] - signals[n]
                reps = 1
                while n + period * (reps + 1) <= upto and all(
                        signals[n + period * reps + s - NS + 1] == signals[n + s - NS + 1] + per_turn * reps and
                        stream[n + period * reps + s] ==
                        (*stream[n + s][:2], stream[n + s][2] + dr * reps, stream[n + s][3], stream[n + s][4] + dc * reps)
                        for s, (dr, dc) in enumerate(steps)):
                    reps += 1
                return reps, steps, per_turn

            while n < upto:
                best = max((NS, 2 * NS, 3 * NS), key=lambda p: (turns_alike(n, p)[0] - 1) * p)
                reps, steps, per_turn = turns_alike(n, best)
                if reps >= 3:
                    with sp.Fori(0, reps) as i:
                        for s in range(best):
                            one(n + s, i, steps[s], per_turn)
                    n += best * reps
                else:
                    one(n)
                    n += 1
            issued[0] = n

        def wait_slab(pe, n, i=None, slabs_per_turn=0):
            v = 16 * (n // NS + 1)
            pe.wait_ge(slot_loaded[n % NS], v if i is None else i * (16 * slabs_per_turn // NS) + v)

        def turns(eng, count, period, body, peel=0):
            n = count // period
            for j in range(peel * period):
                body(None, j)
            if n - peel >= 2:
                with eng.Fori(peel, n) as i:
                    for j in range(period):
                        body(i, j)
            else:
                for j in range(peel * period, n * period):
                    body(None, j)
            for j in range(n * period, count):
                body(None, j)

        def at(i, period, j):
            return j if i is None else i * period + j

        def transpose_pe(pe, groups):
            for u, (srcs, _) in enumerate(groups):
                if u >= 8:
                    t = (tr_free_v, tr_free_a)[u % 2]
                    pe.wait_ge(t.sem, t.at((u - 8) // 2 + 1))
                for j, s in enumerate(srcs):
                    f, p = s.shape[1], s.shape[0]
                    ins = pe.transpose(ps[0:f, u % 8, j * p:(j + 1) * p], s, ident[0:p, 0:p])
                ins.then_inc(tr_ready.sem, 1)

        def transpose_out(eng, groups, which):
            t = (tr_free_v, tr_free_a)[which]
            for u, (srcs, dst) in enumerate(groups):
                if u % 2 != which:
                    continue
                eng.wait_ge(tr_ready.sem, tr_ready.at(u + 1))
                f, p = srcs[0].shape[1], srcs[0].shape[0]
                src = ps[0:f, u % 8, 0:p * len(srcs)]
                if which:
                    nc.scalar.copy(dst, src).then_inc(t.sem, 1)
                else:
                    nc.vector.tensor_copy(dst, src).then_inc(t.sem, 1)

        def transpose_close(groups):
            tr_ready.close(len(groups))
            tr_free_v.close((len(groups) + 1) // 2)
            tr_free_a.close(len(groups) // 2)

        class Norm:

            def __init__(self, centre, ranges, src, dst, scale, shift, split=None):
                self.centre, self.ranges, self.src, self.dst = centre, ranges, src, dst
                self.scale, self.shift, self.split = scale, shift, split
                self.tiles = [(r, k, *ranges[r]) for r in range(len(ranges)) for k in range(KT)]

            def where(self, u):
                r, k, t0, n = self.tiles[u]
                return self.split[2][:, u % 4, 0:n] if self.split else self.dst[:, k, t0:t0 + n]

            def pe(self, pe):
                if self.centre:
                    for r, k, t0, n in self.tiles:
                        ins = pe.matmul(ps[:, r, 0:n], ones, self.src[:, k, t0:t0 + n],
                                        start=(k == 0), stop=(k == KT - 1))
                        if k == KT - 1:
                            ins.then_inc(N["sum"].sem, 1)
                for u, (r, k, t0, n) in enumerate(self.tiles):
                    pe.wait_ge(N["sq"].sem, N["sq"].at(u + 1))
                    pe.matmul(ps[:, 2 + r, 0:n], ones, squares[:, u % 3, 0:n],
                              start=(k == 0), stop=(k == KT - 1)).then_inc(N["sq_used"].sem, 1)

            def ready(self, pe, r, k):
                t = N["lo"] if self.split else N["out"]
                pe.wait_ge(t.sem, t.at(r * KT + k + 1))

            def act(self, act):
                n_sq = 3
                if self.centre:
                    for r, (t0, n) in enumerate(self.ranges):
                        act.wait_ge(N["sum"].sem, N["sum"].at(r + 1))
                        act.activation(mean[:, t0:t0 + n], ps[:, r, 0:n], ACT.Copy, scale=1.0 / D)\
                           .then_inc(N["mean"].sem, 1)
                for u, (r, k, t0, n) in enumerate(self.tiles):
                    if self.centre:
                        act.wait_ge(N["centered"].sem, N["centered"].at(u + 1))
                    if u >= n_sq:
                        act.wait_ge(N["sq_used"].sem, N["sq_used"].at(u - n_sq + 1))
                    act.activation(squares[:, u % n_sq, 0:n],
                                   (self.dst if self.centre else self.src)[:, k, t0:t0 + n], ACT.Square)\
                       .then_inc(N["sq"].sem, 1)
                for r, (t0, n) in enumerate(self.ranges):
                    act.wait_ge(N["sq_used"].sem, N["sq_used"].at((r + 1) * KT))
                    act.activation(rstd[:, t0:t0 + n], ps[:, 2 + r, 0:n], ACT.Sqrt, bias=eps_col,
                                   scale=1.0 / D).then_inc(N["std"].sem, 1)
                for u, (r, k, t0, n) in enumerate(self.tiles):
                    act.wait_ge(N["scaled"].sem, N["scaled"].at(u + 1))
                    act.activation(self.where(u), self.where(u), ACT.Identity,
                                   bias=self.shift(k, r), scale=self.scale(k, r)).then_inc(N["out"].sem, 1)

            def dve(self, dve):
                if self.centre:
                    for r, (t0, n) in enumerate(self.ranges):
                        dve.wait_ge(N["mean"].sem, N["mean"].at(r + 1))
                        for k in range(KT):
                            dve.tensor_tensor(self.dst[:, k, t0:t0 + n], self.src[:, k, t0:t0 + n],
                                              mean[:, t0:t0 + n], ALU.subtract).then_inc(N["centered"].sem, 1)

                def scaled(u):
                    r, k, t0, n = self.tiles[u]
                    if k == 0:
                        dve.wait_ge(N["std"].sem, N["std"].at(r + 1))
                        dve.reciprocal(rstd[:, t0:t0 + n], rstd[:, t0:t0 + n]).then_inc(N["recip"].sem, 1)
                        dve.wait_ge(N["recip"].sem, N["recip"].at(r + 1))
                    if self.split and u >= 4:
                        dve.wait_ge(N["lo"].sem, N["lo"].at(u - 3))
                    dve.tensor_tensor(self.where(u), (self.dst if self.centre else self.src)[:, k, t0:t0 + n],
                                      rstd[:, t0:t0 + n], ALU.mult).then_inc(N["scaled"].sem, 1)

                for u in range(len(self.tiles) + 2):
                    if u < len(self.tiles):
                        scaled(u)
                    if self.split and u >= 2:
                        r, k, t0, n = self.tiles[u - 2]
                        dve.wait_ge(N["out"].sem, N["out"].at(u - 1))
                        dve.tensor_copy(self.split[0][:, k, t0:t0 + n], self.where(u - 2)).then_inc(N["hi"].sem, 1)

            def pool(self, pool):
                if self.split:
                    for u, (r, k, t0, n) in enumerate(self.tiles):
                        pool.wait_ge(N["hi"].sem, N["hi"].at(u + 1))
                        pool.tensor_tensor(self.split[1][:, k, t0:t0 + n], self.where(u),
                                           self.split[0][:, k, t0:t0 + n].bitcast(F32), ALU.subtract)\
                            .then_inc(N["lo"].sem, 1)

            def close(self):
                for names, n in ((("sum", "mean"), len(self.ranges) * self.centre),
                                 (("centered",), len(self.tiles) * self.centre),
                                 (("sq", "sq_used", "scaled", "out"), len(self.tiles)),
                                 (("std", "recip"), len(self.ranges)),
                                 (("hi", "lo"), len(self.tiles) * (self.split is not None))):
                    for name in names:
                        N[name].close(n)

        def norm_stage(norm):
            with nc.Block() as block:
                @block.sync
                def _(sp):
                    load_slabs(sp, done[0] + NS)
                block.tensor(norm.pe)
                block.scalar(norm.act)
                block.vector(norm.dve)
            norm.close()

        def modulated(norm_no, centre, src, dst, ranges, split=None):
            sh, lay = 24 * norm_no, cur[0]
            return Norm(centre, ranges, src, dst, lambda k, r: scls[:, lay, norm_no, k, r:r + 1],
                        lambda k, r: mods[:, lay, sh + k, r:r + 1], split)

        done = [0]

        ADA = named("ada_rows_out", "ada_tiles")

        def turn_wait(eng, t, v, i, per_turn):
            eng.wait_ge(t.sem, t.at(v) if i is None else i * per_turn + t.at(v))

        def ada_slab(pe, which, n, a, i=None, slabs=0, per_turn=0):
            wait_slab(pe, n, i, slabs)
            if a - ada_first[0] >= 2 or i is not None:
                turn_wait(pe, ADA["ada_rows_out"], a - ada_first[0] - 1, i, per_turn)
            for kk in range(2):
                for q in range(4):
                    ins = pe.matmul(ps[32 * q:32 * q + 32, 6 + a % 2, 0:SLAB], sil[:, which, 2 * q + kk, :],
                                    ring[:, n % NS, 2 * q + kk, :], start=(kk == 0), stop=(kk == 1))
            ins.then_inc(mm_done, 1)

        def ada_tiles(pe, a, i=None, per_turn=0):
            turn_wait(pe, ADA["ada_rows_out"], a - ada_first[0] + 1, i, per_turn)
            for m in range(2):
                o = at(i, 4 * per_turn, 4 * a + 2 * m)
                dst = ps[:, 5, o:o + 2] if i is None else ps[:, 5, bass.ds(o, 2)]
                ins = pe.matmul(dst, ada_rows[:, a % 2, m * P:(m + 1) * P], sum_groups[:, 0:2], start=True,
                                stop=True)
            ins.then_inc(ADA["ada_tiles"].sem, 1)

        def ada_take(act, n, a, i=None, per_turn=0, done_per_turn=0):
            v = signals[n] + 1
            act.wait_ge(mm_done, v if i is None else i * done_per_turn + v)
            if a - ada_first[0] >= 2 or i is not None:
                turn_wait(act, ADA["ada_tiles"], a - ada_first[0] - 1, i, per_turn)
            act.activation(ada_rows[:, a % 2, :], ps[:, 6 + a % 2, 0:SLAB], ACT.Copy)\
               .then_inc(ADA["ada_rows_out"].sem, 1)

        ada_first = [0]

        def ada_finish(dve, lay, first, last, bias_col, gain_cols):
            dve.wait_ge(ADA["ada_tiles"].sem, ADA["ada_tiles"].at(last - first))
            m0, m1 = 2 * first, 2 * last
            v_order.step(dve, dve.tensor_tensor(
                mods[:, lay, m0:m1, :], ps[:, 5, 2 * m0:2 * m1].rearrange("p (m c) -> p m c", c=2),
                cols[:, bias_col + m0:bias_col + m1].unsqueeze(2).to_broadcast([P, m1 - m0, 2]), ALU.add))
            for n in range(2):
                if not (m0 <= 8 + 24 * n and 16 + 24 * n <= m1):
                    continue
                v_order.step(dve, dve.tensor_scalar(scls[:, lay, n, :, :], mods[:, lay, 8 + 24 * n:16 + 24 * n, :],
                                                    1.0, None, ALU.add))
                if gain_cols is not None:
                    g = cols[:, gain_cols[n]:gain_cols[n] + 8].unsqueeze(2).to_broadcast([P, 8, 2])
                    v_order.step(dve, dve.tensor_tensor(scls[:, lay, n, :, :], scls[:, lay, n, :, :], g, ALU.mult))

        def ada_close(n):
            for t in ADA.values():
                t.close(n)

        def ada_stage(which, slab0, lay, bias_col, gain_cols):
            done[0] = slab0 + 24
            ada_first[0] = 0
            with nc.Block() as block:
                @block.sync
                def _(sp):
                    load_slabs(sp, done[0] + NS)

                @block.tensor
                def _(pe):
                    def slab(i, j):
                        ada_slab(pe, which, slab0 + j, j, i, NS, NS)
                        if j or i is not None:
                            ada_tiles(pe, j - 1, i, NS)
                    turns(pe, 24, NS, slab, 1)
                    ada_tiles(pe, 23)

                @block.scalar
                def _(act):
                    turns(act, 24, NS, lambda i, j: ada_take(act, slab0 + j, j, i, NS, NS), 1)

                @block.vector
                def _(dve):
                    ada_finish(dve, lay, 0, 24, bias_col, gain_cols)
            ada_close(24)
        def product_stage(slab0, n_cols, row_groups, rhs, ranges, take, which, before=None):
            n_r, n_g = len(ranges), len(row_groups)
            done[0] = slab0 + n_cols * n_g
            period = NS if n_g == 1 else 2
            per_turn = signals[slab0 + period * n_g] - signals[slab0]
            n_banks = min(8, period * 2 * n_r)
            loops = (period * n_g) % NS == 0

            def columns(eng, body):
                if loops:
                    turns(eng, n_cols, period, body)
                else:
                    for j in range(n_cols):
                        body(None, j)

            with nc.Block() as block:
                @block.sync
                def _(sp):
                    load_slabs(sp, done[0] + NS)

                @block.tensor
                def _(pe):
                    def column(i, j):
                        for g, (_, kt) in enumerate(row_groups):
                            n = slab0 + j * n_g + g
                            wait_slab(pe, n, i, period * n_g)
                            for m in range(2):
                                for r, (t0, nt) in enumerate(ranges):
                                    u = (j * 2 + m) * n_r + r
                                    free = u - n_banks + 1
                                    if g == 0 and (free >= 1 or i is not None):
                                        v = mm_free.at(free)
                                        pe.wait_ge(mm_free.sem, v if i is None else i * (period * 2 * n_r) + v)
                                    for k in range(kt):
                                        ins = pe.matmul(ps[:, u % n_banks, 0:nt],
                                                        ring[:, n % NS, k, m * P:(m + 1) * P],
                                                        rhs(g * KT + k, r), start=(g == 0 and k == 0),
                                                        stop=(g == n_g - 1 and k == kt - 1))
                                    ins.then_inc(mm_done, 1)
                    columns(pe, column)

                def taker(eng):
                    if before is not None:
                        before(eng)

                    def column(i, j):
                        for m in range(2):
                            for r, (t0, nt) in enumerate(ranges):
                                u = (j * 2 + m) * n_r + r
                                v = signals[slab0 + j * n_g + n_g - 1] + m * n_r + r + 1
                                eng.wait_ge(mm_done, v if i is None else i * per_turn + v)
                                take(at(i, 2 * period, 2 * j + m), r, ps[:, u % n_banks, 0:nt])\
                                    .then_inc(mm_free.sem, 1)
                    columns(eng, column)
                (block.scalar if which == "scalar" else block.vector)(taker)
            mm_free.close(n_cols * 2 * n_r)

        def tile_of(buf, t, n, t0=0, width=None):
            width = n if width is None else width
            if isinstance(t, int):
                return buf[:, t, t0:t0 + width]
            return buf.rearrange("p t n -> p (t n)")[:, bass.ds(t * n + t0, width)]

        def column_of(buf, c):
            return buf[:, c:c + 1] if isinstance(c, int) else buf[:, bass.ds(c, 1)]

        def units_stage(slab0, units, norm, narrow, bias_rows, cleared=()):
            done[0] = slab0 + len(units)
            named("narrow", "cleared")
            flat = [(n, x) for n, us in enumerate(units) for x in us]
            assert all(signals[slab0 + n + 1] - signals[slab0 + n] == len(us) for n, us in enumerate(units))
            with nc.Block() as block:
                @block.sync
                def _(sp):
                    if narrow is not None:
                        sp.dma_start(wnarrow[:, :, :], narrow.rearrange("(k p) n -> p k n", p=P))\
                          .then_inc(loaded.sem, 16)
                    load_slabs(sp, done[0] + NS)

                @block.tensor
                def _(pe):
                    def narrow_products():
                        pe.wait_ge(loaded.sem, loaded.at(16))
                        for c in range(NCH):
                            for k in range(KT):
                                ins = pe.matmul(ps[:, 7, c * 16:(c + 1) * 16], hT[:, k, c * CH:(c + 1) * CH],
                                                wnarrow[:, k, :], start=(k == 0), stop=(k == KT - 1))
                        ins.then_inc(S["narrow"].sem, 1)

                    norm.pe(pe)
                    pe.wait_ge(N["std"].sem, N["std"].at(len(norm.ranges)))
                    ready = set()
                    for u, (n, x) in enumerate(flat):
                        if u == 0 or flat[u - 1][0] != n:
                            if n == 1 and narrow is not None:
                                narrow_products()
                            wait_slab(pe, slab0 + n)
                        r = int(x[2] >= LAT if x[0] == "tile" else x[1] >= NLAT)
                        fresh = r not in ready
                        ready.add(r)
                        if u >= 7:
                            pe.wait_ge(mm_free.sem, mm_free.at(u - 6))
                        slab = ring[:, (slab0 + n) % NS, :, :]
                        for k in range(KT):
                            if fresh:
                                norm.ready(pe, r, k)
                            if x[0] == "tile":
                                _, m, t0, nt, _, _ = x
                                ins = pe.matmul(ps[:, u % 7, 0:nt], slab[:, k, m * P:(m + 1) * P],
                                                hT[:, k, t0:t0 + nt], start=(k == 0), stop=(k == KT - 1))
                            else:
                                _, c, c0, nt, _, _ = x
                                ins = pe.matmul(ps[:, u % 7, 0:nt], hT[:, k, c * CH:(c + 1) * CH],
                                                slab[:, k, c0:c0 + nt], start=(k == 0), stop=(k == KT - 1))
                        ins.then_inc(mm_done, 1)

                @block.vector
                def _(dve):
                    norm.dve(dve)
                    if narrow is not None:
                        dve.wait_ge(S["narrow"].sem, S["narrow"].at(1))
                        dve.tensor_tensor(small[:, 0:NCH * 16].rearrange("p (c n) -> p c n", n=16),
                                          ps[:, 7, 0:NCH * 16].rearrange("p (c n) -> p c n", n=16),
                                          bias_rows.unsqueeze(1).to_broadcast([P, NCH, 16]), ALU.add)

                @block.gpsimd
                def _(pool):
                    for view, value in cleared:
                        pool.memset(view, value).then_inc(S["cleared"].sem, 1)

                @block.scalar
                def _(act):
                    norm.act(act)
                    if cleared:
                        act.wait_ge(S["cleared"].sem, S["cleared"].at(len(cleared)))
                    for u, (n, x) in enumerate(flat):
                        act.wait_ge(mm_done, signals[slab0] + u + 1)
                        act.activation(x[4], ps[:, u % 7, 0:x[3]] if len(x[4].shape) == 2 else
                                       ps[:, u % 7, 0:x[3]].rearrange("p (h d) -> p h d", d=x[4].shape[2]),
                                       ACT.Copy, scale=x[5] or 1.0).then_inc(mm_free.sem, 1)
            mm_free.close(len(flat))
            norm.close()
            S["cleared"].close(len(cleared))
            if narrow is not None:
                loaded.close(16)
                S["narrow"].close(1)

        SW = named("w_hi", "w_lo")

        def val(x, i, per):
            return x if i is None else i * per + x

        def split_stage(w_parts, segments, norm, after=None, w_units=4):
            w_hi, w_lo = w_parts
            F = {"act": mm_free, "dve": mm_free_v}
            segs, half, unit, kinds = [], 0, 0, {"act": 0, "dve": 0}
            history = []
            prev_w = None
            for items, reps in segments:
                seg = {"items": [], "reps": reps, "half0": half, "ns": len(items),
                       "sig": signals[items[0][1] + len(items)] - signals[items[0][1]]}
                kinds0 = dict(kinds)
                for it in items:
                    if it[0] == "ada":
                        seg["items"].append({"ada": it[1:]})
                        continue
                    x = dict(zip(("n", "kt", "rhs", "ranges", "eng", "take", "hooks"), it[1:]))
                    x["half"], x["prev"], x["units"] = half, prev_w, []
                    half += 2
                    for m in range(2):
                        for r in range(len(x["ranges"])):
                            u = len(history)
                            x["units"].append({"m": m, "r": r, "bank": u % w_units, "idx": kinds[x["eng"]],
                                               "reuses": history[u - w_units] if u >= w_units else None})
                            history.append((x["eng"], kinds[x["eng"]]))
                            kinds[x["eng"]] += 1
                    prev_w = x
                    seg["items"].append(x)
                seg["halves"] = half - seg["half0"]
                seg["kinds"] = {k: kinds[k] - kinds0[k] for k in kinds}
                seg["adas"] = sum(1 for it in items if it[0] == "ada")
                for t in range(reps - 1):
                    assert (seg["halves"] and len(items) % NS == 0)
                    half += seg["halves"]
                    for k in kinds:
                        kinds[k] += seg["kinds"][k]
                if reps > 1:
                    n_u = sum(len(x["units"]) for x in seg["items"] if "n" in x)
                    assert n_u % w_units == 0
                    history = history + [(k, v + seg["kinds"][k] * (reps - 1)) for k, v in history[-n_u:]]
                    prev_w = dict(prev_w, n=prev_w["n"] + seg["ns"] * (reps - 1))
                segs.append(seg)
            done[0] = segments[0][0][0][1] + sum(len(items) * reps for items, reps in segments)

            def run(eng, body):
                for s, seg in enumerate(segs):
                    if seg["reps"] > 1:
                        with eng.Fori(0, seg["reps"]) as i:
                            body(s, seg, i)
                    else:
                        body(s, seg, None)

            def next_w(s, seg, pos, i):
                for x in seg["items"][pos + 1:]:
                    if "n" in x:
                        return x, i, seg
                first = next(x for x in seg["items"] if "n" in x)
                if i is not None:
                    return first, i + 1, seg
                if s + 1 < len(segs):
                    nxt = segs[s + 1]
                    return next(x for x in nxt["items"] if "n" in x), (None if nxt["reps"] == 1 else 0), nxt
                return None

            with nc.Block() as block:
                @block.sync
                def _(sp):
                    load_slabs(sp, done[0] + NS)

                def high(act, x, i, seg, m):
                    if m == 0:
                        wait_slab(act, x["n"], i, seg["ns"])
                    if x["prev"] is not None:
                        v = signals[x["prev"]["n"]] + (m + 1) * len(x["prev"]["ranges"])
                        act.wait_ge(mm_done, val(v, i, seg["sig"]))
                    act.activation(w_hi[m][:, 0:x["kt"], :], ring[:, x["n"] % NS, 0:x["kt"], m * P:(m + 1) * P],
                                   ACT.Copy).then_inc(SW["w_hi"].sem, 1)

                def low(pool, x, i, seg, m):
                    turn_wait(pool, SW["w_hi"], x["half"] + m + 1, i, seg["halves"])
                    pool.tensor_tensor(w_lo[m][:, 0:x["kt"], :],
                                       ring[:, x["n"] % NS, 0:x["kt"], m * P:(m + 1) * P],
                                       w_hi[m][:, 0:x["kt"], :].bitcast(F32), ALU.subtract)\
                        .then_inc(SW["w_lo"].sem, 1)

                def takes(eng, name, x, i, seg, m):
                    for un in x["units"]:
                        if un["m"] == m and x["eng"] == name:
                            v = signals[x["n"]] + m * len(x["ranges"]) + un["r"] + 1
                            eng.wait_ge(mm_done, val(v, i, seg["sig"]))
                            bank = ps[:, un["bank"], 0:x["ranges"][un["r"]][1]]
                            x["take"](i, m, un["r"], bank, un).then_inc(F[name].sem, 1)

                @block.tensor
                def _(pe):
                    norm.pe(pe)

                    def body(s, seg, i):
                        late = []
                        for x in seg["items"]:
                            if "ada" in x:
                                n, which, a = x["ada"]
                                ada_slab(pe, which, n, a, i, seg["ns"], seg["adas"])
                                late.append(a)
                                if len(late) > 2:
                                    ada_tiles(pe, late.pop(0), i, seg["adas"])
                                continue
                            H, L, k0 = x["rhs"]
                            for un in x["units"]:
                                m, r = un["m"], un["r"]
                                t0, nt = x["ranges"][r]
                                if r == 0:
                                    turn_wait(pe, SW["w_lo"], x["half"] + m + 1, i, seg["halves"])
                                if un["reuses"] is not None:
                                    k_, v = un["reuses"]
                                    turn_wait(pe, F[k_], v + 1, i, seg["kinds"][k_])
                                for k in range(x["kt"]):
                                    if "k" in x["hooks"]:
                                        x["hooks"]["k"](pe, i, k, r)
                                    h, l = H[:, k0 + k, t0:t0 + nt], L[:, k0 + k, t0:t0 + nt]
                                    o = ps[:, un["bank"], 0:nt]
                                    pe.matmul(o, w_hi[m][:, k, :], h, start=(k == 0), stop=False)
                                    pe.matmul(o, w_hi[m][:, k, :], l, start=False, stop=False)
                                    ins = pe.matmul(o, w_lo[m][:, k, :], h, start=False, stop=(k == x["kt"] - 1))
                                ins.then_inc(mm_done, 1)
                                while late:
                                    ada_tiles(pe, late.pop(0), i, seg["adas"])
                        assert not late
                    run(pe, body)

                @block.scalar
                def _(act):
                    x = next(x for x in segs[0]["items"] if "n" in x)
                    for m in range(2):
                        high(act, x, None, segs[0], m)
                    norm.act(act)

                    def body(s, seg, i):
                        for pos, x in enumerate(seg["items"]):
                            if "ada" in x:
                                ada_take(act, x["ada"][0], x["ada"][2], i, seg["adas"], seg["sig"])
                                continue
                            nxt = next_w(s, seg, pos, i)
                            for m in range(2):
                                if nxt is not None:
                                    high(act, *nxt, m)
                                takes(act, "act", x, i, seg, m)
                    run(act, body)

                @block.gpsimd
                def _(pool):
                    x = next(x for x in segs[0]["items"] if "n" in x)
                    for m in range(2):
                        low(pool, x, None, segs[0], m)
                    norm.pool(pool)

                    def body(s, seg, i):
                        for pos, x in enumerate(seg["items"]):
                            if "ada" in x:
                                continue
                            nxt = next_w(s, seg, pos, i)
                            for m in range(2):
                                if nxt is not None:
                                    low(pool, *nxt, m)
                                if "pool_half" in x["hooks"]:
                                    x["hooks"]["pool_half"](pool, i, m)
                    run(pool, body)

                @block.vector
                def _(dve):
                    norm.dve(dve)

                    def body(s, seg, i):
                        for x in seg["items"]:
                            if "ada" in x:
                                continue
                            for m in range(2):
                                takes(dve, "dve", x, i, seg, m)
                                if "dve_half" in x["hooks"]:
                                    x["hooks"]["dve_half"](dve, i, m)
                    run(dve, body)
                    if after is not None:
                        after(dve)
            for name in ("w_hi", "w_lo"):
                SW[name].close(half)
            for k, t in F.items():
                t.close(kinds[k])
            norm.close()

        n_small, dve_abs, conv_marks = [0], [0, 0], [None]

        COL = {}
        col_rows = []

        def param(name, rows_ap):
            COL[name] = sum(x.shape[0] for x in col_rows)
            col_rows.append(rows_ap)

        vec = lambda a: a.rearrange("(n p) -> n p", p=P)
        param("c", vec(w["c"][0]))
        param("c_ctx", vec(w["c_ctx"]))
        param("c2", vec(w["c_2"][0]))
        param("c_ctx2", vec(w["c_ctx_2"]))
        param("b_ada", vec(w["b_ada"][0]))
        param("b_ada2_0", vec(w["ada_b_2"][0]))
        param("b_ada2_1", vec(w["ada_b_2"][1]))
        for l in range(2):
            param(f"norm1_{l}", vec(w["norm1_g_2"][l]))
            param(f"norm2_{l}", vec(w["norm2_g_2"][l]))
        for n in ("ln1_g", "ln1_b", "ln2_g", "ln2_b"):
            param(n, vec(w[n][0]))
        param("conv_w", w["ssd_conv_w"][0].rearrange("t (n p) -> (t n) p", p=P))
        param("conv_b", vec(w["ssd_conv_b"][0]))
        param("ssd_norm", vec(w["ssd_norm_w"][0]))
        param("pool_scale", vec(w["pool_scale"][0]))
        param("ffn_w", w["ffn_conv_w"][0].rearrange("a b (n p) -> (a b n) p", p=P))
        param("ffn_b", vec(w["ffn_conv_b"][0]))
        param("mlstm_norm", vec(w["mlstm_norm_g_2"][0]))
        param("c_q_norm", w["c_q_norm_g_2"])
        param("c_k_norm", w["c_k_norm_g_2"])
        COL["swa_q"] = sum(x.shape[0] for x in col_rows)
        COL["swa_k"] = COL["swa_q"] + 1
        n_rows = COL["swa_k"] + 1
        assert n_rows <= 768
        n_lots = (n_rows + P - 1) // P
        tok_in = big[:, 0:NCH * D].rearrange("p (c d) -> p c d", c=NCH)
        row_in = big[:, NCH * D:NCH * D + 768].rearrange("p (g f) -> p g f", f=P)
        ctx2_in = big[:, 8192:8192 + NCTX * D].rearrange("p (c d) -> p c d", c=NCTX)
        d_in = big[0:4, 12288:12288 + P]
        DT_B, A_ROW, GATE_B, SINK = 0, 16, 32, 48

        groups = []
        for g in range(n_lots):
            n = min(P, n_rows - g * P)
            groups.append(([row_in[0:n, g, :]], cols[:, g * P:g * P + n]))
        for k in range(KT):
            groups.append(([tok_in[:, c, k * P:(k + 1) * P] for c in range(NLAT)], xT[:, k, 0:LAT]))
            groups.append(([tok_in[:, NLAT + c, k * P:(k + 1) * P] for c in range(NCTX)], xT[:, k, LAT:TOK]))
        groups.append(([d_in], dskip[:, :]))
        with nc.Block() as block:
            @block.sync
            def _(sp):
                n_loads = 0

                def load(dst, src):
                    nonlocal n_loads
                    sp.dma_start(dst, src).then_inc(loaded.sem, 16)
                    n_loads += 1
                load(mats[:, :, :], w["const_mats"].rearrange("n p q -> p n q"))
                for (name, _), ap in zip(list(COL.items()), col_rows):
                    at0, n, r = COL[name], ap.shape[0], 0
                    while r < n:
                        g, p0 = divmod(at0 + r, P)
                        m = min(n - r, P - p0)
                        load(row_in[p0:p0 + m, g, :], ap[r:r + m, :])
                        r += m
                for name, src in (("swa_q", w["swa_q_norm_g_2"]), ("swa_k", w["swa_k_norm_g_2"])):
                    g, p0 = divmod(COL[name], P)
                    for half in range(2):
                        load(row_in[p0:p0 + 1, g, half * 64:half * 64 + 64], src)
                load(tok_in[:, 0:NLAT, :], w["x"][0].rearrange("(c p) d -> p c d", p=P))
                load(tok_in[:, NLAT:NCH, :], w["ctx"][0].rearrange("(c p) d -> p c d", p=P))
                load(small[0:4, 0:2], w["ssd_d"][0].rearrange("(t h) -> t h", h=2))
                for dst, src in ((DT_B, w["ssd_dt_bias"][0].rearrange("a h -> (a h)")),
                                 (A_ROW, w["ssd_a_log"][0].rearrange("a h -> (a h)")),
                                 (GATE_B, w["ab_gate_b_2"][0]), (SINK, w["swa_sink_2"][0])):
                    load(rows[:, dst:dst + src.shape[0]], src.partition_broadcast(P))
                load_slabs(sp, NS)
                n_small[0] = n_loads
            @block.vector
            def _(dve):
                dve.wait_ge(loaded.sem, loaded.at(16 * n_small[0]))
                v_order.step(dve, dve.tensor_copy(d_in.rearrange("p (h q) -> p h q", h=2),
                                                  small[0:4, 0:2].unsqueeze(2).to_broadcast([4, 2, 64])))
                transpose_out(dve, groups, 0)

            @block.tensor
            def _(pe):
                pe.wait_ge(loaded.sem, loaded.at(16 * n_small[0]))
                pe.wait_ge(v_order.sem, 1)
                transpose_pe(pe, groups)

            @block.scalar
            def _(act):
                act.wait_ge(loaded.sem, loaded.at(16 * n_small[0]))
                a = rows[:, A_ROW:A_ROW + 16]
                a_order.step(act, act.activation(a, a, ACT.Exp))
                act.activation(a, a, ACT.Copy, scale=-1.0)
                transpose_out(act, groups, 1)
        loaded.close(16 * n_small[0])
        transpose_close(groups)

        named("cleared")
        with nc.Block() as block:
            @block.vector
            def _(dve):
                dve.memset(sil[:, :, :, :], 0.0).then_inc(S["cleared"].sem, 1)

            @block.scalar
            def _(act):
                act.wait_ge(S["cleared"].sem, S["cleared"].at(1))
                for n, (a, b) in enumerate((("c", "c_ctx"), ("c2", "c_ctx2"))):
                    act.activation(sil[:, n, :, 0], cols[:, COL[a]:COL[a] + 8], ACT.Silu)
                    act.activation(sil[:, n, :, 1], cols[:, COL[b]:COL[b] + 8], ACT.Silu)

        S["cleared"].close(1)
        ada_stage(0, W["ada"], 0, COL["b_ada"], None)
        LP, CP = LAT + 2, CTX + 2
        xbc_pad = big[:, 0:8 * (LP + CP)].rearrange("p (t n) -> p t n", t=8)
        o = 8 * (LP + CP)
        xbc = big[:, o:o + 8 * TOK].rearrange("p (t n) -> p t n", t=8)
        o += 8 * TOK
        zT = big[:, o:o + 4 * LAT].rearrange("p (t n) -> p t n", t=4)
        o += 4 * LAT
        fT = big[:, o:o + 2 * LAT].rearrange("p (t n) -> p t n", t=2)
        o += 2 * LAT
        PP = LAT + 16
        poolT = big[:, o:o + 2 * PP].rearrange("p (t n) -> p t n", t=2)
        o += 2 * PP
        x_tok = big[:, o:o + NCH * 512].rearrange("p (c n) -> p c n", c=NCH)
        o += NCH * 512
        b_tok = big[:, o:o + NCH * 256].rearrange("p (c n) -> p c n", c=NCH)
        o += NCH * 256
        yT = big[:, o:o + 4 * LAT].rearrange("p (t n) -> p t n", t=4)
        o += 4 * LAT
        assert o <= 24576

        units = []
        for s in range(4):
            us = []
            for m in range(2):
                t = 2 * s + m
                us.append(("tile", m, 0, LAT, xbc_pad[:, t, 1:1 + LAT], None))
                if t < 6:
                    us.append(("tile", m, LAT, CTX, xbc_pad[:, t, LP + 1:LP + 1 + CTX], None))
            units.append(us)
        for s in range(2):
            units.append([("tile", m, 0, LAT, zT[:, 2 * s + m, :], None) for m in range(2)])
        units.append([("tile", m, 0, LAT, fT[:, m, :], None) for m in range(2)])
        units.append([("tile", m, 0, LAT, poolT[:, m, 8:8 + LAT], None) for m in range(2)])
        units_stage(W["in"], units, modulated(0, True, xT, hT, BOTH), w["w_in"][0, :, OFF_DT:OFF_DT + 16],
                    rows[:, DT_B:DT_B + 16], [(xbc_pad, 0.0), (poolT, 0.0)])

        n16 = NCH * 16
        sm = lambda i: small[:, i * n16:(i + 1) * n16]
        dt, dA, t_a, t_b, t_c = (sm(i) for i in range(5))
        conv_units = [(t, 0, LAT, 0) for t in range(8)] + [(t, LP, CTX, LAT) for t in range(6)]
        named("exp_ln")
        with nc.Block() as block:
            @block.vector
            def _(dve):
                v_order.step(dve, dve.scalar_tensor_tensor(t_a, dt, -1.0, dt, ALU.mult, ALU.max))
                dve_abs[0] = v_order.n
                marks = []
                for tap in range(3):
                    for u, (t, p0, n, t0) in enumerate(conv_units):
                        wcol = cols[:, COL["conv_w"] + tap * 8 + t:COL["conv_w"] + tap * 8 + t + 1]
                        src, dst = xbc_pad[:, t, p0 + tap:p0 + tap + n], xbc[:, t, t0:t0 + n]
                        if tap == 0:
                            b = cols[:, COL["conv_b"] + t:COL["conv_b"] + t + 1]
                            marks.append(v_order.mark(dve.tensor_scalar(dst, src, wcol, b, ALU.mult, ALU.add)))
                        else:
                            dve.wait_ge(v_order.sem, marks[-len(conv_units)])
                            marks.append(v_order.mark(dve.scalar_tensor_tensor(
                                dst, src, wcol, dst, ALU.mult, ALU.add)))
                conv_marks[0] = marks[-len(conv_units):]
                dve.wait_ge(S["exp_ln"].sem, S["exp_ln"].at(1))
                v_order.step(dve, dve.tensor_scalar(t_b, t_a, 1.0, None, ALU.add))
                dve_abs[1] = v_order.n
                v_order.step(dve, dve.tensor_scalar(dA, t_b, -1.0, None, ALU.add))
                dve.wait_ge(S["exp_ln"].sem, S["exp_ln"].at(2))
                v_order.step(dve, dve.tensor_scalar(t_b, dA, 0.0, None, ALU.is_equal))
                v_order.step(dve, dve.tensor_tensor(t_c, t_c, t_b, ALU.add))
                v_order.step(dve, dve.tensor_tensor(dA, dA, t_b, ALU.add))
                v_order.step(dve, dve.reciprocal(dA, dA))
                v_order.step(dve, dve.tensor_tensor(t_c, t_c, dA, ALU.mult))
                v_order.step(dve, dve.tensor_tensor(t_c, t_c, t_a, ALU.mult))
                v_order.step(dve, dve.scalar_tensor_tensor(dt, dt, 0.0, t_c, ALU.max, ALU.add))
                a_rows = rows[:, A_ROW:A_ROW + 16].unsqueeze(1).to_broadcast([P, NCH, 16])
                dve.tensor_tensor(dA.rearrange("p (c n) -> p c n", n=16), dt.rearrange("p (c n) -> p c n", n=16),
                                  a_rows, ALU.mult)

            @block.scalar
            def _(act):
                act.wait_ge(v_order.sem, dve_abs[0])
                act.activation(t_a, t_a, ACT.Exp, scale=-1.0).then_inc(S["exp_ln"].sem, 1)
                act.wait_ge(v_order.sem, dve_abs[1])
                act.activation(t_c, t_b, ACT.Ln).then_inc(S["exp_ln"].sem, 1)
                for (t, _, n, t0), m in zip(conv_units, conv_marks[0]):
                    act.wait_ge(v_order.sem, m)
                    act.activation(xbc[:, t, t0:t0 + n], xbc[:, t, t0:t0 + n], ACT.Silu)
        S["exp_ln"].close(2)
        tmp = big[:, 0:8 * (LP + CP)]
        Gs = tmp[:, 0:8 * P].rearrange("p (c g n) -> p c g n", c=NLAT, g=2)
        state = tmp[:, 1024:2048].rearrange("p (d g n) -> p d g n", d=2, g=2)
        xd = tmp[:, 2048:3072].rearrange("p (b k n) -> p b k n", b=2, k=2)
        seg = tmp[:, 3072:4096].rearrange("p (b h n) -> p b h n", b=2, h=4)
        lmat = tmp[:, 4096:5120].rearrange("p (b h n) -> p b h n", b=2, h=4)
        e_row = tmp[:, 5120:6144].rearrange("p (b h n) -> p b h n", b=2, h=4)
        c_dec = squares[:, 0:2, :].rearrange("p b (h n) -> p b h n", h=4)
        g_mask = mean[:, 0:256].rearrange("p (b n) -> p b n", b=2)
        neg_cs, e_tot, decay = t_a, t_b, t_c
        by_chunk = lambda a: a.rearrange("p (c n) -> p c n", n=16)
        groups = []
        for c in range(NCH):
            t0 = c * CH
            groups.append(([xbc[:, t, t0:t0 + CH] for t in range(4)], x_tok[:, c, :]))
            groups.append(([xbc[:, 4 + g, t0:t0 + CH] for g in range(2)], b_tok[:, c, :]))
        with nc.Block() as block:
            @block.tensor
            def _(pe):
                transpose_pe(pe, groups)

            @block.vector
            def _(dve):
                transpose_out(dve, groups, 0)

            @block.scalar
            def _(act):
                transpose_out(act, groups, 1)
        transpose_close(groups)
        named("cs", "cb", "log_decay")
        with nc.Block() as block:
            @block.tensor
            def _(pe):
                for c in range(NCH):
                    for d, tri in enumerate((U_LE, U_GE)):
                        o = c * 16 + d * 8
                        pe.matmul(ps[:, 0, o:o + 8], mats[:, tri, :], dA[:, o:o + 8], start=True, stop=True)
                pe.matmul(ps[:, 1, 0:n16], ones, dA, start=True, stop=True).then_inc(S["cs"].sem, 1)
                for c in range(NLAT):
                    for g in range(2):
                        u = c * 2 + g
                        pe.matmul(ps[:, 2 + u // 4, (u % 4) * P:(u % 4 + 1) * P],
                                  xbc[:, 4 + g, c * CH:(c + 1) * CH], xbc[:, 6 + g, c * CH:(c + 1) * CH],
                                  start=True, stop=True).then_inc(S["cb"].sem, 1)

            @block.vector
            def _(dve):
                dve.wait_ge(S["cs"].sem, S["cs"].at(1))
                v_order.step(dve, dve.tensor_scalar(neg_cs, ps[:, 0, 0:n16], -1.0, None, ALU.mult))
                dve.tensor_tensor(decay, ps[:, 1, 0:n16], neg_cs, ALU.add).then_inc(S["log_decay"].sem, 1)
                dve.memset(tmp[:, 1024:2048], 0.0)

            @block.scalar
            def _(act):
                act.wait_ge(S["log_decay"].sem, S["log_decay"].at(1))
                act.activation(e_tot, ps[:, 1, 0:n16], ACT.Exp)
                act.activation(decay, decay, ACT.Exp)
                for q in range(2):
                    act.wait_ge(S["cb"].sem, S["cb"].at(4 * (q + 1)))
                    act.activation(tmp[:, q * 512:(q + 1) * 512], ps[:, 2 + q, :], ACT.Copy)
        S["cs"].close(1)
        S["cb"].close(8)
        S["log_decay"].close(1)

        order_of = [[4, 5, 0, 1, 2, 3], [5, 4, 3, 2, 1, 0]]
        steps = [(d, order_of[d][k], g, k) for k in range(NCH) for d in range(2) for g in range(2)]
        outs = [s for s, (_, _, _, k) in enumerate(steps) if k >= NCTX]
        ups = [s for s, (_, _, _, k) in enumerate(steps) if k < NCH - 1]
        upto = lambda lst, s: sum(1 for x in lst if x < s)
        heads = lambda a, d, c, g: by_chunk(a)[:, c, d * 8 + g * 4:d * 8 + g * 4 + 4]
        R = named("xdt", "bc", "seg", "lmat", "erow", "m", "cdec", "y", "y_out", "ds", "state")
        sig = lambda ins, n: ins.then_inc(R[n].sem, 1)
        wait = lambda eng, n, v: eng.wait_ge(R[n].sem, R[n].at(v))

        with nc.Block() as block:
            @block.gpsimd
            def _(pool):
                for s, (d, c, g, k) in enumerate(steps):
                    b = s % 2
                    if s >= 2:
                        if s - 2 in ups:
                            wait(pool, "ds", upto(ups, s - 1))
                        if s - 2 in outs:
                            wait(pool, "y", upto(outs, s - 1))
                    x3 = x_tok[:, c, g * 256:(g + 1) * 256].rearrange("p (h q) -> p h q", h=4)
                    v = [xd[:, b, j, :].rearrange("p (h q) -> p h q", h=4) for j in range(2)]
                    g_order.step(pool, pool.tensor_tensor(
                        v[0], x3, heads(dt, d, c, g).unsqueeze(2).to_broadcast([P, 4, 64]), ALU.mult))
                    sig(pool.tensor_tensor(
                        v[1], v[0], heads(decay, d, c, g).unsqueeze(2).to_broadcast([P, 4, 64]), ALU.mult), "xdt")
                    if s in outs:
                        i = outs.index(s)
                        wait(pool, "erow", i + 1)
                        if i >= 2:
                            wait(pool, "y", i - 1)
                        cT = xbc[:, 6 + g, c * CH:(c + 1) * CH].unsqueeze(1).to_broadcast([P, 4, CH])
                        sig(pool.tensor_tensor(c_dec[:, i % 2, :, :], e_row[:, i % 2, :, :], cT, ALU.mult), "cdec")

            @block.tensor
            def _(pe):
                def rows_of_cs(i):
                    d, c, g, _ = steps[outs[i]]
                    if i >= 2:
                        wait(pe, "seg", i - 1)
                        wait(pe, "erow", i - 1)
                    for h in range(4):
                        col = heads(dA, d, c, g)[:, h:h + 1]
                        ins = pe.matmul(ps[:, i % 2, h * P:(h + 1) * P], col.to_broadcast([P, P]),
                                        mats[:, (U_LE, U_GE)[d], :], start=True, stop=True)
                    sig(ins, "bc")

                rows_of_cs(0)
                for s, (d, c, g, k) in enumerate(steps):
                    wait(pe, "xdt", s + 1)
                    if s in ups:
                        i = ups.index(s)
                        if i >= 2:
                            wait(pe, "state", i - 1)
                        sig(pe.matmul(ps[:, 4 + i % 2, 0:256], b_tok[:, c, g * P:(g + 1) * P], xd[:, s % 2, 1, :],
                                      start=True, stop=True), "ds")
                    if s in outs:
                        i = outs.index(s)
                        if i + 1 < len(outs):
                            rows_of_cs(i + 1)
                        wait(pe, "m", i + 1)
                        wait(pe, "cdec", i + 1)
                        wait(pe, "state", upto(ups, s - 3))
                        if i >= 2:
                            wait(pe, "y_out", i - 1)
                        for h in range(4):
                            o = ps[64 * (h % 2):64 * (h % 2) + 64, 2 + i % 2, (h // 2) * P:(h // 2 + 1) * P]
                            pe.matmul(o, xd[:, s % 2, 0, h * 64:(h + 1) * 64], lmat[:, i % 2, h, :],
                                      start=True, stop=False, skip_group_check=True)
                            ins = pe.matmul(o, state[:, d, g, h * 64:(h + 1) * 64], c_dec[:, i % 2, h, :],
                                            start=False, stop=True, skip_group_check=True)
                        sig(ins, "y")

            @block.vector
            def _(dve):
                def finish(s):
                    d, c, g, k = steps[s]
                    if s in outs:
                        i = outs.index(s)
                        wait(dve, "y", i + 1)
                        dst = yT[:, 2 * g:2 * g + 2, c * CH:(c + 1) * CH]
                        src = ps[:, 2 + i % 2, 0:2 * P].rearrange("p (t n) -> p t n", t=2)
                        if k < NCTX + NLAT // 2:
                            sig(dve.tensor_copy(dst, src), "y_out")
                        else:
                            wait(dve, "y_out", i - 1)
                            sig(dve.tensor_tensor(dst, src, dst, ALU.add), "y_out")
                    if s in ups:
                        i = ups.index(s)
                        st = state[:, d, g, :]
                        st3 = st.rearrange("p (h q) -> p h q", h=4)
                        wait(dve, "ds", i + 1)
                        if i >= 4:
                            wait(dve, "state", i - 3)
                        v_order.step(dve, dve.tensor_tensor(
                            st3, st3, heads(e_tot, d, c, g).unsqueeze(2).to_broadcast([P, 4, 64]), ALU.mult))
                        sig(dve.tensor_tensor(st, ps[:, 4 + i % 2, 0:256], st, ALU.add), "state")

                for s, (d, c, g, k) in enumerate(steps):
                    if s in outs:
                        i = outs.index(s)
                        b = i % 2
                        wait(dve, "erow", i + 1)
                        if i >= 2:
                            wait(dve, "lmat", i - 1)
                        for h in range(4):
                            ins = dve.tensor_scalar(seg[:, b, h, :], ps[:, b, h * P:(h + 1) * P],
                                                    heads(neg_cs, d, c, g)[:, h:h + 1], 0.0, ALU.add, ALU.min)
                        sig(ins, "seg")
                        if i >= 2:
                            wait(dve, "m", i - 1)
                        v_order.step(dve, dve.tensor_tensor(g_mask[:, b, :], Gs[:, c, g, :],
                                                            mats[:, (U_LE, U_GE)[d], :], ALU.mult))
                    if s >= 1:
                        finish(s - 1)
                    if s in outs:
                        wait(dve, "lmat", i + 1)
                        sig(dve.tensor_tensor(lmat[:, b, :, :], lmat[:, b, :, :],
                                              g_mask[:, b, :].unsqueeze(1).to_broadcast([P, 4, P]), ALU.mult), "m")
                finish(len(steps) - 1)

            @block.scalar
            def _(act):
                for i in range(len(outs)):
                    b = i % 2
                    wait(act, "bc", i + 1)
                    if i >= 2:
                        wait(act, "cdec", i - 1)
                    sig(act.activation(e_row[:, b, :, :].rearrange("p h n -> p (h n)"), ps[:, b, :], ACT.Exp), "erow")
                    wait(act, "seg", i + 1)
                    if i >= 2:
                        wait(act, "y", i - 1)
                    sig(act.activation(lmat[:, b, :, :], seg[:, b, :, :], ACT.Exp), "lmat")
        for n in ("bc", "seg", "lmat", "erow", "m", "cdec", "y", "y_out"):
            R[n].close(len(outs))
        R["xdt"].close(len(steps))
        R["ds"].close(len(ups))
        R["state"].close(len(ups))

        dft = big[:, 0:4096].rearrange("p (a k n) -> p a k n", a=2, k=NLAT)
        w4 = small[:, :].rearrange("p (a n) -> p a n", a=4)
        W12 = tmp[:, 4096:4608].rearrange("p (t n) -> p t n", t=2)
        f_tok = tmp[:, 4608:5632].rearrange("p (c n) -> p c n", c=NLAT)
        cnt = x_tok.rearrange("p c n -> p (c n)")[:, 0:1024].rearrange("p (t n) -> p t n", t=2)
        sums = xbc.rearrange("p t n -> p (t n)")[:, 3072:3072 + 4 * PP].rearrange("p (t s n) -> p t s n", t=2, s=2)
        pooled = x_tok.rearrange("p c n -> p (c n)")[:, 1024:2048].rearrange("p (t n) -> p t n", t=2)
        gated = b_tok.rearrange("p c n -> p (c n)")[:, 0:1024].rearrange("p (t n) -> p t n", t=2)
        R = named("zero", "silu", "y", "sq", "var", "std", "w12", "w12_out", "ftok", "ftok_out", "dft", "pooled", "pool")
        with nc.Block() as block:
            @block.gpsimd
            def _(pool):
                sig(pool.memset(small[:, :], 0.0), "zero")
                sig(pool.memset(sums, 0.0), "zero")

            @block.sync
            def _(sp):
                wait(sp, "zero", 1)
                for a, name in enumerate(("fnet_w", "pool_w")):
                    for g in range(4):
                        h = 64 * (g % 2)
                        sp.dma_start(w4[h:h + 64, 2 * a + g // 2, h:h + 64], w[name][0, g]).then_inc(loaded.sem, 16)
                sp.dma_start(cnt, w["const_tables"][T_CNT:T_CNT + 2].rearrange("t p n -> p t n"))\
                  .then_inc(loaded.sem, 16)
                for a in range(2):
                    sp.dma_start(dft[:, a, :, :], w["const_dft"][a].rearrange("(k p) n -> p k n", p=P))\
                      .then_inc(loaded.sem, 16)

            @block.scalar
            def _(act):
                for t in range(4):
                    sig(act.activation(zT[:, t, :], zT[:, t, :], ACT.Silu), "silu")
                for t in range(4):
                    wait(act, "y", t + 1)
                    if t >= 3:
                        wait(act, "var", t - 2)
                    sig(act.activation(squares[:, t % 3, :], yT[:, t, :], ACT.Square), "sq")
                wait(act, "w12", 4)
                for t in range(2):
                    sig(act.activation(W12[:, t, :], ps[:, 2, t * 256:(t + 1) * 256], ACT.Copy), "w12_out")
                for t in range(2):
                    for c in range(NLAT):
                        u = t * NLAT + c
                        wait(act, "ftok", 2 * (u // 2 + 1))
                        if u >= NLAT:
                            wait(act, "dft", 1)
                        sig(act.activation(f_tok[:, c, :], ps[:, 3 + (u // 2) % 2, (u % 2) * 256:(u % 2 + 1) * 256],
                                           ACT.Copy), "ftok_out")
                    wait(act, "dft", t + 1)
                    act.activation(hT[:, 4 + t, 0:LAT], ps[:, 5, :], ACT.Copy).then_inc(mm_free.sem, 1)
                for t in range(2):
                    wait(act, "pool", t + 1)
                    sc = cols[:, COL["pool_scale"] + t:COL["pool_scale"] + t + 1]
                    act.activation(hT[:, 6 + t, 0:LAT], ps[:, 6 + t, :], ACT.Copy, scale=sc)
                for g in range(2):
                    wait(act, "var", 2 * g + 2)
                    sig(act.activation(rstd[:, 0:LAT] if g == 0 else mean[:, 0:LAT], ps[:, g, :], ACT.Sqrt,
                                       bias=eps_col, scale=1.0 / 256), "std")

            @block.tensor
            def _(pe):
                for t in range(4):
                    wait(pe, "sq", t + 1)
                    sig(pe.matmul(ps[:, t // 2, :], ones, squares[:, t % 3, :], start=(t % 2 == 0),
                                  stop=(t % 2 == 1)), "var")
                pe.wait_ge(loaded.sem, loaded.at(16 * 11))
                for t in range(2):
                    for a, m in enumerate((DFT_C, DFT_S)):
                        sig(pe.matmul(ps[:, 2, t * 256 + a * P:t * 256 + (a + 1) * P], mats[:, m, :], w4[:, t, :],
                                      start=True, stop=True), "w12")
                for t in range(2):
                    wait(pe, "w12_out", t + 1)
                    for c in range(NLAT):
                        u = t * NLAT + c
                        if u >= NLAT:
                            wait(pe, "ftok_out", u // 2 * 2 - 2)
                        sig(pe.matmul(ps[:, 3 + (u // 2) % 2, (u % 2) * 256:(u % 2 + 1) * 256],
                                      fT[:, t, c * CH:(c + 1) * CH], W12[:, t, :], start=True, stop=True), "ftok")
                    if t == 1:
                        pe.wait_ge(mm_free.sem, mm_free.at(1))
                    for a in range(2):
                        for c in range(NLAT):
                            wait(pe, "ftok_out", t * NLAT + c + 1)
                            ins = pe.matmul(ps[:, 5, :], f_tok[:, c, a * P:(a + 1) * P], dft[:, a, c, :],
                                            start=(a == 0 and c == 0), stop=(a == 1 and c == NLAT - 1))
                    sig(ins, "dft")
                for t in range(2):
                    wait(pe, "pooled", t + 1)
                    sig(pe.matmul(ps[:, 6 + t, :], w4[:, 2 + t, :], pooled[:, t, :], start=True, stop=True), "pool")

            @block.vector
            def _(dve):
                for t in range(4):
                    v_order.step(dve, dve.scalar_tensor_tensor(yT[:, t, :], xbc[:, t, 0:LAT], dskip[:, t:t + 1],
                                                               yT[:, t, :], ALU.mult, ALU.add))
                    wait(dve, "silu", t + 1)
                    sig(dve.tensor_tensor(yT[:, t, :], yT[:, t, :], zT[:, t, :], ALU.mult), "y")
                wait(dve, "zero", 2)
                dve.wait_ge(loaded.sem, loaded.at(16 * 11))
                for t in range(2):
                    src = poolT[:, t, :]
                    for lvl in range(4 if t else 2):
                        dst = sums[:, t, lvl % 2, :]
                        h = 1 if lvl == 0 else 2 ** (lvl - 1)
                        lo, n = 8, LAT
                        if lvl == 0:
                            a, b, e0, e1 = 1, 0, 1, PP
                        else:
                            a, b, e0, e1 = h, h, 2 ** lvl, PP - 2 ** lvl
                        v_order.step(dve, dve.tensor_tensor(dst[:, e0:e1], src[:, e0 - a:e1 - a],
                                                            src[:, e0 + b:e1 + b], ALU.add))
                        part = slice(0, 64) if lvl % 2 == 0 else slice(64, P)
                        if lvl // 2 == t:
                            v_order.step(dve, dve.tensor_tensor(pooled[part, t, :], dst[part, 8:8 + LAT],
                                                                cnt[part, t, :], ALU.mult))
                        src = dst
                    sig(dve.tensor_tensor(pooled[:, t, :], pooled[:, t, :], poolT[:, t, 8:8 + LAT],
                                          ALU.subtract), "pooled")
                for g in range(2):
                    wait(dve, "std", g + 1)
                    r = rstd[:, 0:LAT] if g == 0 else mean[:, 0:LAT]
                    v_order.step(dve, dve.reciprocal(r, r))
                    for t in (2 * g, 2 * g + 1):
                        wn = cols[:, COL["ssd_norm"] + t:COL["ssd_norm"] + t + 1]
                        dve.scalar_tensor_tensor(hT[:, t, 0:LAT], yT[:, t, :], wn, r, ALU.mult, ALU.mult)
        for n, v in (("zero", 2), ("silu", 4), ("y", 4), ("sq", 4), ("var", 4), ("std", 2), ("w12", 4), ("w12_out", 2),
                     ("ftok", 8), ("ftok_out", 8), ("dft", 2), ("pooled", 2), ("pool", 2)):
            R[n].close(v)
        loaded.close(16 * 11)
        mm_free.close(2)

        def add_gated(gate):
            lay = cur[0]

            def take(t, r, bank):
                x = tile_of(xT, t, TOK, BOTH[r][0], BOTH[r][1])
                gates = mods[:, lay, :, :].rearrange("p m c -> p (m c)")
                return nc.vector.scalar_tensor_tensor(x, bank, column_of(gates, t * 2 + 2 * gate + r), x,
                                                      ALU.mult, ALU.add)
            return take

        def alpha_x(dve):
            for k in range(KT):
                v_order.step(dve, dve.tensor_scalar(xT[:, k, 0:LAT], xT[:, k, 0:LAT], ALPHA, None, ALU.mult))

        def post_norm(g, b):
            norm_stage(Norm(True, ONLY_LAT, xT, xT, lambda k, r: cols[:, COL[g] + k:COL[g] + k + 1],
                            lambda k, r: cols[:, COL[b] + k:COL[b] + k + 1]))

        from_h = lambda k, r: hT[:, k, BOTH[r][0]:BOTH[r][0] + BOTH[r][1]]
        product_stage(W["out"], 4, whole, from_h, ONLY_LAT, add_gated(16), "vector", alpha_x)
        post_norm("ln1_g", "ln1_b")
        norm = modulated(1, True, xT, hT, ONLY_LAT)

        act_ff = big[:, 0:FT * LAT].rearrange("p (t n) -> p t n", t=FT)
        GP = (GRID_H + 2) * (GRID_W + 2)
        o = FT * LAT
        grid = big[:, o:o + 8 * GP].rearrange("p (b h w) -> p b h w", b=8, h=GRID_H + 2)
        o += 8 * GP
        conv = big[:, o:o + 8 * LAT].rearrange("p (b n) -> p b n", b=8)
        R = named("zero", "grid", "conv", "gelu", "ff")
        done[0] = W["up"] + FT + 24
        ada_first[0] = 0
        slab0 = W["up"]
        v_base = v_order.n
        CW, TAPS = COL["ffn_w"], 9

        def wait_turn(eng, n, i, per_turn, v):
            eng.wait_ge(R[n].sem, R[n].at(v) if i is None else i * per_turn + R[n].at(v))

        ADA_TURN, DONE_TURN = 4, signals[slab0 + 8] - signals[slab0]
        with nc.Block() as block:
            @block.sync
            def _(sp):
                load_slabs(sp, done[0] + NS)

            @block.gpsimd
            def _(pool):
                sig(pool.memset(grid, 0.0), "zero")

                def step(i, j):
                    for m in range(2):
                        wait_turn(pool, "gelu", i, 4, 2 * j + m + 1)
                        u = (4 * j + m) % 8
                        sig(pool.tensor_tensor(tile_of(act_ff, at(i, 4, 2 * j + m), LAT), conv[:, u, :],
                                               conv[:, (u + 2) % 8, :], ALU.mult), "ff")
                turns(pool, FT // 2, 2, step, 1)

            @block.tensor
            def _(pe):
                norm.pe(pe)

                def step(i, j):
                    for half in range(2):
                        n = slab0 + 4 * j + half
                        wait_slab(pe, n, i, 8)
                        for m in range(2):
                            u = 4 * j + 2 * half + m
                            if u >= 4 or i is not None:
                                v = mm_free.at(u - 3)
                                pe.wait_ge(mm_free.sem, v if i is None else i * 8 + v)
                            for k in range(KT):
                                if u == 0 and i is None:
                                    norm.ready(pe, 0, k)
                                ins = pe.matmul(ps[:, u % 4, :], ring[:, n % NS, k, m * P:(m + 1) * P],
                                                hT[:, k, 0:LAT], start=(k == 0), stop=(k == KT - 1))
                            ins.then_inc(mm_done, 1)
                            if half == 0 and m == 0 and (j or i is not None):
                                for a in (2 * j - 2, 2 * j - 1):
                                    ada_tiles(pe, a, i, ADA_TURN)
                    for half in range(2):
                        ada_slab(pe, 1, slab0 + 4 * j + 2 + half, 2 * j + half, i, 8, ADA_TURN)
                turns(pe, FT // 2, 2, step, 1)
                for a in (22, 23):
                    ada_tiles(pe, a - 2)
                    ada_slab(pe, 1, slab0 + FT + a, a)
                for a in (22, 23):
                    ada_tiles(pe, a)

            @block.scalar
            def _(act):
                norm.act(act)
                wait(act, "zero", 1)

                def step(i, j):
                    for u in range(4 * j, 4 * j + 4):
                        v = signals[slab0 + 4 * j] + u % 4 + 1
                        act.wait_ge(mm_done, v if i is None else i * DONE_TURN + v)
                        if u >= 8 or i is not None:
                            wait_turn(act, "conv", i, 8, u - 7)
                        act.activation(grid[:, u % 8, 1:1 + GRID_H, 1:1 + GRID_W],
                                       ps[:, u % 4, :].rearrange("p (h w) -> p h w", w=GRID_W), ACT.Copy)\
                           .then_inc(mm_free.sem, 1)

                def gelus(i, j):
                    for m in range(2):
                        wait_turn(act, "conv", i, 8, 4 * j + 2 + m + 1)
                        g = conv[:, (4 * j + 2 + m) % 8, :]
                        sig(act.activation(g, g, ACT.Gelu_apprx_tanh), "gelu")

                def adas(i, j):
                    for a in (2 * j, 2 * j + 1):
                        ada_take(act, slab0 + 2 * j + 2 + a, a, i, ADA_TURN, DONE_TURN)
                turns(act, FT // 2, 2, lambda i, j: (step(i, j), adas(i, j), gelus(i, j)), 1)
                for a in (22, 23):
                    ada_take(act, slab0 + FT + a, a)

            @block.vector
            def _(dve):
                norm.dve(dve)

                def step(i, j):
                    first = [0] * 4
                    for tap in range(TAPS):
                        for q in range(4):
                            u = 4 * j + q
                            tile = at(i, 4, 2 * j + q % 2)
                            if q >= 2:
                                tile = tile + FT
                            wcol = column_of(cols, tile + (CW + tap * 2 * FT))
                            b = u % 8
                            dy, dx = divmod(tap, 3)
                            src = grid[:, b, dy:dy + GRID_H, dx:dx + GRID_W]
                            dst = conv[:, b, :].rearrange("p (h w) -> p h w", w=GRID_W)
                            mine = v_base + j * 4 * (TAPS - 1) + tap * 4 + q
                            if tap == 0:
                                v = mm_free.at(u + 1)
                                dve.wait_ge(mm_free.sem, v if i is None else i * 8 + v)
                                if u >= 8 or i is not None:
                                    wait_turn(dve, "ff", i, 4, 2 * j - 2)
                                ins = dve.tensor_scalar(dst, src, wcol, column_of(cols, tile + COL["ffn_b"]),
                                                        ALU.mult, ALU.add)
                            else:
                                v = mine - 3
                                dve.wait_ge(v_order.sem, v if i is None else i * (8 * (TAPS - 1)) + v)
                                ins = dve.scalar_tensor_tensor(dst, src, wcol, dst, ALU.mult, ALU.add)
                            if tap < TAPS - 1:
                                ins.then_inc(v_order.sem, 1)
                            else:
                                sig(ins, "conv")
                turns(dve, FT // 2, 2, step, 1)
        v_order.n += (FT // 2) * 4 * (TAPS - 1)
        with nc.Block() as block:
            @block.vector
            def _(dve):
                ada_finish(dve, 1, 0, 24, COL["b_ada2_0"], (COL["norm1_0"], COL["norm2_0"]))
        ada_close(24)
        mm_free.close(FT * 2)
        norm.close()
        R["zero"].close(1)
        R["conv"].close(FT * 2)
        R["gelu"].close(FT)
        R["ff"].close(FT)
        product_stage(W["down"], 4, DOWN_ROWS, lambda k, r: act_ff[:, k, :], ONLY_LAT, add_gated(40), "vector",
                      alpha_x)
        post_norm("ln2_g", "ln2_b")
        def mlp_stage(layer, ranges):
            with ExitStack() as scope:
                def parts(name, tiles, n):
                    return [sb(f"{name}_{p}{layer}", [P, tiles, n], scope, F32R) for p in ("hi", "lo")]
                n_tok = sum(r[1] for r in ranges)
                h_parts, m_parts = parts("h", KT, n_tok), parts("hidden", KT, n_tok)
                w_parts = list(zip(parts("w0", KT, P), parts("w1", KT, P)))
                norm = modulated(1, False, xT, None, ranges, (*h_parts, sb(f"h{layer}", [P, 4, LAT], scope)))
                mlp(layer, ranges, norm, h_parts, m_parts, w_parts)

        def mlp(layer, ranges, norm, h_parts, m_parts, w_parts):
            (h_hi, h_lo), (m_hi, m_lo) = h_parts, m_parts
            n_r = len(ranges)
            R = named("m_hi", "m_lo")
            gated = add_gated(40)
            first = W[f"mlp_{layer}"]
            n_u, per_q = 2 * n_r, 8 * n_r
            relus = [squares[:, b, :] for b in range(3)] + [rstd[:, 0:LAT]]
            v_at = v_order.n
            ada_first[0] = 0

            def hidden(q, j, last_w2):
                def relu(i, m, r, bank, un):
                    u = q * per_q + j * n_u + m * n_r + r
                    if u >= 4:
                        turn_wait(nc.scalar, R["m_lo"], u - 3, i, per_q)
                    return nc.scalar.activation(relus[u % 4][:, 0:ranges[r][1]], bank, ACT.Relu)

                def high(dve, i, m):
                    if q and j == 0 and m == 0:
                        v = signals[last_w2]
                        dve.wait_ge(mm_done, val(v, i, signals[last_w2] - signals[last_w2 - (8 if layer else 12)]))
                    for r, (t0, nt) in enumerate(ranges):
                        u = q * per_q + j * n_u + m * n_r + r
                        sq = relus[u % 4][:, 0:nt]
                        turn_wait(dve, mm_free, u + 1, i, per_q)
                        dve.tensor_tensor(sq, sq, sq, ALU.mult).then_inc(v_order.sem, 1)
                        dve.wait_ge(v_order.sem, val(v_at + u + 1, i, per_q))
                        dve.tensor_copy(m_hi[:, 2 * j + m, t0:t0 + nt], sq).then_inc(R["m_hi"].sem, 1)

                def low(pool, i, m):
                    for r, (t0, nt) in enumerate(ranges):
                        u = q * per_q + j * n_u + m * n_r + r
                        turn_wait(pool, R["m_hi"], u + 1, i, per_q)
                        pool.tensor_tensor(m_lo[:, 2 * j + m, t0:t0 + nt], relus[u % 4][:, 0:nt],
                                           m_hi[:, 2 * j + m, t0:t0 + nt].bitcast(F32), ALU.subtract)\
                            .then_inc(R["m_lo"].sem, 1)
                hooks = {"dve_half": high, "pool_half": low}
                if q == 0 and j == 0:
                    hooks["k"] = lambda pe, i, k, r: norm.ready(pe, r, k)
                return relu, hooks

            def back(q, j):
                def take(i, m, r, bank, un):
                    if q:
                        turn_wait(nc.vector, mm_free_v, un["idx"] - per_q + 1, i, per_q)
                    return gated(2 * j + m, r, bank)

                def operand(pe, i, k, r):
                    turn_wait(pe, R["m_lo"], q * per_q + k * n_r + r + 1, i, per_q)
                return take, ({"k": operand} if j == 0 else {})

            segments, n, ada_no = [], first, 0
            for q in range(4):
                items, last_w2 = [], n
                for j in range(4):
                    take, hooks = hidden(q, j, last_w2)
                    items.append(("w", n, KT, (h_hi, h_lo, 0), ranges, "act", take, hooks))
                    n += 1
                    if layer == 0:
                        k = 1 if q else (2, 2, 2, 3)[j]
                        items += [("ada", n + x, 1, ada_no + x) for x in range(k)]
                        n, ada_no = n + k, ada_no + k
                for j in range(4):
                    take, hooks = back(q, j)
                    items.append(("w", n, KT, (m_hi, m_lo, 0), ranges, "dve", take, hooks))
                    n += 1
                    if layer == 0 and q == 0 and j < 3:
                        items.append(("ada", n, 1, ada_no))
                        n, ada_no = n + 1, ada_no + 1
                segments.append((items, 1))
            segments = [segments[0], (segments[1][0], 2), segments[3]]
            after = None
            if layer == 0:
                after = lambda dve: ada_finish(dve, 2, 0, 24, COL["b_ada2_1"], (COL["norm1_1"], COL["norm2_1"]))
            v_order.n += 4 * per_q
            split_stage(w_parts, segments, norm, after)
            R["m_hi"].close(4 * per_q)
            R["m_lo"].close(4 * per_q)
            if layer == 0:
                ada_close(24)

        def head_norms(jobs, hd_mat, hd):
            R = named("sq", "var", "std")
            temps = [rstd[:, 0:LAT], mean[:, 0:LAT]]
            v_at = v_order.n
            with nc.Block() as block:
                @block.tensor
                def _(pe):
                    for u, (src, n, _) in enumerate(jobs):
                        pe.wait_ge(R["sq"].sem, R["sq"].at(u + 1))
                        if u >= 4:
                            pe.wait_ge(R["std"].sem, R["std"].at(u - 3))
                        pe.matmul(ps[:, u % 4, 0:n], hd_mat, squares[:, u % 3, 0:n], start=True, stop=True)\
                          .then_inc(R["var"].sem, 1)

                @block.scalar
                def _(act):
                    def root(u):
                        n = jobs[u][1]
                        act.wait_ge(R["var"].sem, R["var"].at(u + 1))
                        if u >= 2:
                            act.wait_ge(v_order.sem, v_at + 2 * (u - 1))
                        act.activation(temps[u % 2][:, 0:n], ps[:, u % 4, 0:n], ACT.Sqrt, bias=eps_col,
                                       scale=1.0 / hd).then_inc(R["std"].sem, 1)
                    for u, (src, n, _) in enumerate(jobs):
                        if u >= 3:
                            act.wait_ge(R["var"].sem, R["var"].at(u - 2))
                        act.activation(squares[:, u % 3, 0:n], src, ACT.Square).then_inc(R["sq"].sem, 1)
                        if u >= 1:
                            root(u - 1)
                    root(len(jobs) - 1)

                @block.vector
                def _(dve):
                    for u, (src, n, gain) in enumerate(jobs):
                        t = temps[u % 2][:, 0:n]
                        dve.wait_ge(R["std"].sem, R["std"].at(u + 1))
                        v_order.step(dve, dve.reciprocal(t, t))
                        v_order.mark(dve.scalar_tensor_tensor(src, src, gain, t, ALU.mult, ALU.mult))
            for n in R:
                R[n].close(len(jobs))

        def rope(tiles, rot, cos, sin):
            R = named("rot", "sin")
            with nc.Block() as block:
                @block.tensor
                def _(pe):
                    for u, t in enumerate(tiles):
                        if u >= 4:
                            pe.wait_ge(R["sin"].sem, R["sin"].at(u - 3))
                        pe.matmul(ps[:, u % 4, :], mats[:, rot, :], t, start=True, stop=True)\
                          .then_inc(R["rot"].sem, 1)

                @block.vector
                def _(dve):
                    for u, t in enumerate(tiles):
                        dve.wait_ge(R["rot"].sem, R["rot"].at(u + 1))
                        v_order.step(dve, dve.tensor_tensor(t, t, cos, ALU.mult))
                        ins = dve.tensor_tensor(squares[:, u % 3, :], ps[:, u % 4, :], sin, ALU.mult)
                        ins.then_inc(R["sin"].sem, 1)
                        dve.wait_ge(R["sin"].sem, R["sin"].at(u + 1))
                        v_order.step(dve, dve.tensor_tensor(t, t, squares[:, u % 3, :], ALU.add))
            for n in R:
                R[n].close(len(tiles))

        def attention(jobs, scale, bufs):
            sc, pt, stat = bufs
            R = named("qk", "top", "max", "exp", "norm", "turned", "turned_out", "pv", "pv_out")
            sig = lambda ins, n: ins.then_inc(R[n].sem, 1)
            wait = lambda eng, n, v: eng.wait_ge(R[n].sem, R[n].at(v))
            flat = ps[:, :, :].rearrange("p b n -> p (b n)")
            n_jobs = len(jobs)
            with nc.Block() as block:
                @block.tensor
                def _(pe):
                    def scores(j):
                        q, keys, _, _, _, _ = jobs[j]
                        if j >= 2:
                            wait(pe, "exp", j - 1)
                        for k_ap, c0, mask in keys:
                            dst = flat[:, (j % 2) * 1024 + c0:(j % 2) * 1024 + c0 + k_ap.shape[1]]
                            ins = pe.matmul(dst, q, k_ap, start=True, stop=mask is None)
                            if mask is not None:
                                ins = pe.matmul(dst, ident, mask, start=False, stop=True)
                        sig(ins, "qk")

                    def turn(j):
                        width = jobs[j][2]
                        wait(pe, "norm", j + 1)
                        if j >= 1:
                            wait(pe, "turned_out", j)
                        for c in range(width // P):
                            ins = pe.transpose(flat[:, 2048 + c * P:2048 + (c + 1) * P],
                                               sc[:, j % 2, c * P:(c + 1) * P], ident)
                        sig(ins, "turned")

                    def values(j):
                        _, _, width, v, _, o = jobs[j]
                        wait(pe, "turned_out", j + 1)
                        if j >= 2:
                            wait(pe, "pv_out", j - 1)
                        p0, d = o.start_partition(), v[0].shape[1]
                        for c in range(width // P):
                            ins = pe.matmul(ps[p0:p0 + d, 6 + j % 2, 0:P], v[c], pt[:, j % 2, c * P:(c + 1) * P],
                                            start=(c == 0), stop=(c == width // P - 1))
                        sig(ins, "pv")

                    scores(0)
                    scores(1)
                    for j in range(n_jobs):
                        turn(j)
                        if j + 2 < n_jobs:
                            scores(j + 2)
                        if j >= 1:
                            values(j - 1)
                    values(n_jobs - 1)

                @block.vector
                def _(dve):
                    def top(j):
                        _, _, width, _, sink, _ = jobs[j]
                        b = j % 2
                        m, t = stat[:, b, 0:1], stat[:, b, 3:4]
                        wait(dve, "qk", j + 1)
                        sig(dve.tensor_reduce(t, flat[:, b * 1024:b * 1024 + width], AX_X, ALU.max), "top")
                        wait(dve, "top", j + 1)
                        if j >= 2:
                            wait(dve, "exp", j - 1)
                        if sink is None:
                            sig(dve.tensor_scalar(m, t, -scale, None, ALU.mult), "max")
                        else:
                            v_order.step(dve, dve.scalar_tensor_tensor(t, t, scale, sink, ALU.mult, ALU.max))
                            sig(dve.tensor_scalar(m, t, -1.0, None, ALU.mult), "max")

                    def norm(j):
                        _, _, width, _, sink, _ = jobs[j]
                        b = j % 2
                        wait(dve, "exp", j + 1)
                        den = stat[:, b, 1:2]
                        if sink is not None:
                            v_order.step(dve, dve.tensor_tensor(den, den, stat[:, b, 2:3], ALU.add))
                        v_order.step(dve, dve.reciprocal(den, den))
                        sig(dve.tensor_scalar(sc[:, b, 0:width], sc[:, b, 0:width], den, None, ALU.mult), "norm")

                    top(0)
                    for j in range(n_jobs):
                        if j + 1 < n_jobs:
                            top(j + 1)
                        norm(j)

                @block.scalar
                def _(act):
                    def expo(j):
                        _, _, width, _, sink, _ = jobs[j]
                        b = j % 2
                        wait(act, "max", j + 1)
                        if j >= 2:
                            wait(act, "turned", j - 1)
                        if sink is not None:
                            a_order.step(act, act.activation(stat[:, b, 2:3], sink, ACT.Exp, bias=stat[:, b, 0:1]))
                        sig(act.activation(sc[:, b, 0:width], flat[:, b * 1024:b * 1024 + width], ACT.Exp,
                                           bias=stat[:, b, 0:1], scale=scale, accum_out=stat[:, b, 1:2]), "exp")

                    def take(j):
                        width = jobs[j][2]
                        wait(act, "turned", j + 1)
                        if j >= 2:
                            wait(act, "pv", j - 1)
                        sig(act.activation(pt[:, j % 2, 0:width], flat[:, 2048:2048 + width], ACT.Copy),
                            "turned_out")

                    def give(j):
                        o = jobs[j][5]
                        p0, d = o.start_partition(), o.shape[0]
                        wait(act, "pv", j + 1)
                        sig(act.activation(o, ps[p0:p0 + d, 6 + j % 2, 0:P], ACT.Copy), "pv_out")

                    expo(0)
                    for j in range(n_jobs):
                        if j + 1 < n_jobs:
                            expo(j + 1)
                        take(j)
                        if j >= 1:
                            give(j - 1)
                    give(n_jobs - 1)
            for n in R:
                R[n].close(n_jobs)

        groups = [([ctx2_in[:, c, k * P:(k + 1) * P] for c in range(NCTX)], xT[:, k, LAT:TOK]) for k in range(KT)]
        with nc.Block() as block:
            @block.sync
            def _(sp):
                sp.dma_start(ctx2_in, w["ctx_2"][0].rearrange("(c p) d -> p c d", p=P)).then_inc(loaded.sem, 16)

            @block.tensor
            def _(pe):
                pe.wait_ge(loaded.sem, loaded.at(16))
                transpose_pe(pe, groups)

            @block.vector
            def _(dve):
                transpose_out(dve, groups, 0)

            @block.scalar
            def _(act):
                transpose_out(act, groups, 1)
        loaded.close(16)
        transpose_close(groups)
        cur[0] = 1

        def part(n, pattern, **kw):
            nonlocal_o[0] += n
            assert nonlocal_o[0] <= 24576
            return big[:, nonlocal_o[0] - n:nonlocal_o[0]].rearrange(pattern, **kw)
        nonlocal_o = [0]
        qa = part(4 * TOK, "p (t n) -> p t n", t=4)
        ka = part(4 * TOK, "p (t n) -> p t n", t=4)
        va = part(NCH * 4 * 129, "p (c h e) -> p c h e", c=NCH, h=4)
        oa = part(4 * TOK, "p (t n) -> p t n", t=4)
        qb = part(4 * TOK, "p (t n) -> p t n", t=4)
        kb = part(2 * TOK, "p (t n) -> p t n", t=2)
        vb = part(NCH * P, "p (c n) -> p c n", c=NCH)
        k_tok = part(NCH * 512, "p (c n) -> p c n", c=NCH)
        free0 = nonlocal_o[0]
        units = []
        for buf, sc_ in ((qa, None), (ka, float(P) ** -0.5)):
            for s in range(2):
                units.append([("tile", m, t0, nt, buf[:, 2 * s + m, t0:t0 + nt], sc_)
                              for m in range(2) for t0, nt in BOTH])
        for s in range(2):
            units.append([("rows", c, 0, SLAB, va[:, c, 2 * s:2 * s + 2, 0:P], None) for c in range(NCH)])
        for buf in (oa, qb):
            for s in range(2):
                units.append([("tile", m, t0, nt, buf[:, 2 * s + m, t0:t0 + nt], None)
                              for m in range(2) for t0, nt in BOTH])
        units.append([("tile", 0, t0, nt, kb[:, 0, t0:t0 + nt], None) for t0, nt in BOTH] +
                     [("rows", c, P, P, vb[:, c, :], None) for c in range(NCH)])
        units_stage(W["ab"], units, modulated(0, False, xT, hT, BOTH), w["ab_w_in_2"][0, :, AB_G:AB_G + 16],
                    rows[:, GATE_B:GATE_B + 16], [(va, 1.0)])

        log_f = by_chunk(dt)
        fs = lambda a: by_chunk(a).rearrange("p c (d k h) -> p c d k h", d=2, k=2)[:, :, :, 1, :]
        raw = big[0:4, free0:free0 + 4 * TOK].rearrange("p (k n) -> p k n", k=4)
        with nc.Block() as block:
            @block.vector
            def _(dve):
                v_order.step(dve, dve.scalar_tensor_tensor(t_a, dt, -1.0, dt, ALU.mult, ALU.max))
                dve_abs[0] = v_order.n
                dve.wait_ge(S["exp_ln"].sem, S["exp_ln"].at(1))
                v_order.step(dve, dve.tensor_scalar(t_b, t_a, 1.0, None, ALU.add))
                dve_abs[1] = v_order.n
                v_order.step(dve, dve.tensor_scalar(dA, t_b, -1.0, None, ALU.add))
                dve.wait_ge(S["exp_ln"].sem, S["exp_ln"].at(2))
                v_order.step(dve, dve.tensor_scalar(t_b, dA, 0.0, None, ALU.is_equal))
                v_order.step(dve, dve.tensor_tensor(t_c, t_c, t_b, ALU.add))
                v_order.step(dve, dve.tensor_tensor(dA, dA, t_b, ALU.add))
                v_order.step(dve, dve.reciprocal(dA, dA))
                v_order.step(dve, dve.tensor_tensor(t_c, t_c, dA, ALU.mult))
                v_order.step(dve, dve.tensor_tensor(t_c, t_c, t_a, ALU.mult))
                v_order.step(dve, dve.tensor_scalar(t_b, dt, 0.0, None, ALU.min))
                v_order.step(dve, dve.tensor_tensor(t_b, t_b, t_c, ALU.subtract))
                for d in range(2):
                    o = 8 * d + 4
                    v_order.step(dve, dve.tensor_copy(by_chunk(dt)[:, :, o:o + 4], by_chunk(t_b)[:, :, o:o + 4]))

            @block.scalar
            def _(act):
                act.wait_ge(v_order.sem, dve_abs[0])
                act.activation(t_a, t_a, ACT.Exp, scale=-1.0).then_inc(S["exp_ln"].sem, 1)
                act.wait_ge(v_order.sem, dve_abs[1])
                act.activation(t_c, t_b, ACT.Ln).then_inc(S["exp_ln"].sem, 1)
        S["exp_ln"].close(2)
        groups = []
        for kind in range(4):
            lat = [dt[:, c * 16 + kind * 4:c * 16 + kind * 4 + 4] for c in range(NCH)]
            groups.append((lat[0:NLAT], raw[:, kind, 0:LAT]))
            groups.append((lat[NLAT:], raw[:, kind, LAT:TOK]))
        for c in range(NCH):
            groups.append(([ka[:, h, c * CH:(c + 1) * CH] for h in range(4)], k_tok[:, c, :]))
        with nc.Block() as block:
            @block.tensor
            def _(pe):
                transpose_pe(pe, groups)

            @block.vector
            def _(dve):
                transpose_out(dve, groups, 0)

            @block.scalar
            def _(act):
                transpose_out(act, groups, 1)
        transpose_close(groups)

        row_m = squares[:, :, :].rearrange("p a n -> p (a n)")[0:4, 0:2 * TOK].rearrange("p (q n) -> p q n", q=2)
        one_row = ones[0:4, :]
        m_col = small[0:4, 480:482]
        b_row = mean[0:4, 0:CH]
        r_row = mean[0:4, CH:2 * CH]
        g_row = mean[0:4, 2 * CH:3 * CH]
        with nc.Block() as block:
            @block.vector
            def _(dve):
                v_order.step(dve, dve.memset(m_col, 0.0))
                for d in range(2):
                    for c in order_of[d]:
                        view = lambda a: a[:, ::-1] if d else a
                        cut = lambda a: view(a[:, c * CH:(c + 1) * CH])
                        last = (lambda a: a[:, 0:1]) if d else (lambda a: a[:, CH - 1:CH])
                        ii, ff = raw[:, 2 * d, :], raw[:, 2 * d + 1, :]
                        m = m_col[:, d:d + 1]
                        v_order.step(dve, dve.tensor_tensor_scan(view(b_row), one_row, cut(ff), 0.0,
                                                                 ALU.mult, ALU.add))
                        v_order.step(dve, dve.tensor_tensor(r_row, ii[:, c * CH:(c + 1) * CH], b_row, ALU.subtract))
                        v_order.step(dve, dve.tensor_tensor_scan(view(g_row), view(r_row), view(r_row), m,
                                                                 ALU.max, ALU.max))
                        v_order.step(dve, dve.tensor_scalar(ii[:, c * CH:(c + 1) * CH], g_row, -1.0, m,
                                                            ALU.mult, ALU.add))
                        v_order.step(dve, dve.tensor_tensor(ff[:, c * CH:(c + 1) * CH], b_row, g_row, ALU.add))
                        v_order.step(dve, dve.tensor_scalar(row_m[:, d, c * CH:(c + 1) * CH], r_row, m, None,
                                                            ALU.subtract))
                        v_order.step(dve, dve.tensor_copy(m, last(ff[:, c * CH:(c + 1) * CH])))

        nonlocal_o[0] = free0 + 0
        part(4 * TOK, "p (k n) -> p k n", k=4)
        wide = lambda b: b.rearrange("p h n -> p (h n)")
        c_state = [t[:, 0:4 * 129].rearrange("p (h e) -> p h e", h=4) for t in (mean, rstd)]
        hfree = hT[:, 4:8, :].rearrange("p t n -> p (t n)")
        pmat0, pmat1, iw0, em0, kw, qs0 = (hfree[:, i * 512:(i + 1) * 512].rearrange("p (h n) -> p h n", h=4)
                                           for i in range(6))
        pmats, iws = (pmat0, pmat1), (iw0, part(512, "p (h n) -> p h n", h=4))
        ems = (em0, ada_rows[:, :, :].rearrange("p b (h n) -> p (b h) n", n=P))
        qss = ((qs0[:, 0:2, :], qs0[:, 2:4, :]),
               (mats[:, DFT_C:DFT_S + 1, :], sil[:, 0, :, :].rearrange("p k n -> p (k n)")
                .rearrange("p (h n) -> p h n", h=2)))
        rp_cols = (small[:, 0:4], small[:, 8:12])
        w_cols = (small[:, 4:8], small[:, 12:16])
        order_m = [(d, order_of[d][k], k) for k in range(NCH) for d in range(2)]
        R = named("bc", "cols", "rp", "seg", "p_exp", "p", "em", "w", "masked", "m", "qs", "kw", "mem", "h", "iw", "w_exp")
        n_m = len(order_m)
        chunk4 = lambda buf, c: buf[:, :, c * CH:(c + 1) * CH]
        with nc.Block() as block:
            @block.tensor
            def _(pe):
                def front(s):
                    d, c, k = order_m[s]
                    t0 = c * CH
                    if s >= 1:
                        wait(pe, "m", s)
                        wait(pe, "em", s)
                        wait(pe, "iw", s)
                        wait(pe, "rp", s)
                        wait(pe, "w", s)
                    for h in range(4):
                        pe.matmul(ps[:, 0, h * P:(h + 1) * P], mats[0:4, SEL + h, :], raw[:, 2 * d, t0:t0 + CH],
                                  start=True, stop=True)
                        pe.matmul(ps[:, 1, h * P:(h + 1) * P], mats[0:4, SEL + h, :], raw[:, 2 * d + 1, t0:t0 + CH],
                                  start=True, stop=True)
                    sig(pe.transpose(ps[:, 7, 0:4], row_m[:, d, t0:t0 + CH], ident[0:4, 0:4]), "bc")
                    for h in range(4):
                        ins = pe.matmul(ps[:, 2, h * P:(h + 1) * P], ka[:, h, t0:t0 + CH], qa[:, h, t0:t0 + CH],
                                        start=True, stop=True)
                    sig(ins, "cols")

                front(0)
                for s, (d, c, k) in enumerate(order_m):
                    if s + 1 < n_m:
                        front(s + 1)
                    wait(pe, "m", s + 1)
                    wait(pe, "qs", s + 1)
                    if s >= 1:
                        wait(pe, "h", s)
                    if s >= 2:
                        wait(pe, "mem", s - 1)
                    pmat = pmats[s % 2]
                    for h in range(4):
                        q = qss[s % 2][h // 2][:, h % 2, :]
                        o, dn = ps[:, 3, h * P:(h + 1) * P], ps[:, 4, h * P:(h + 1) * P]
                        pe.matmul(o, va[:, c, h, 0:P], pmat[:, h, :], start=True, stop=False)
                        pe.matmul(o, c_state[d][:, h, 0:P], q, start=False, stop=True)
                        pe.matmul(dn, ones, pmat[:, h, :], start=True, stop=False)
                        ins = pe.matmul(dn, c_state[d][:, h, P:P + 1].to_broadcast([P, P]), q,
                                        start=False, stop=True)
                    sig(ins, "p")
                    wait(pe, "kw", s + 1)
                    if s >= 1:
                        wait(pe, "mem", s)
                    for h in range(4):
                        ins = pe.matmul(ps[:, 5 + h // 2, (h % 2) * 129:(h % 2) * 129 + 129], kw[:, h, :],
                                        va[:, c, h, :], start=True, stop=True)
                    sig(ins, "masked")

            @block.vector
            def _(dve):
                for st in c_state:
                    v_order.step(dve, dve.memset(st, 0.0))

                def front(s):
                    d, c, k = order_m[s]
                    rp_col, w_col, pmat = rp_cols[s % 2], w_cols[s % 2], pmats[s % 2]
                    tri = (U_LE, U_GE)[d]
                    edge = 0 if d else CH - 1
                    wait(dve, "bc", s + 1)
                    sig(dve.tensor_copy(rp_col, ps[:, 7, 0:4]), "rp")
                    wait(dve, "rp", s + 1)
                    wait(dve, "iw", s + 1)
                    if s >= 2:
                        wait(dve, "kw", s - 1)
                    last_a = ps[:, 0, :].rearrange("p (h n) -> p h n", h=4)[:, :, edge]
                    sig(dve.tensor_tensor(w_col, last_a, rp_col, ALU.add), "w")
                    for h in range(4):
                        ins = dve.tensor_scalar(pmat[:, h, :], ps[:, 0, h * P:(h + 1) * P], rp_col[:, h:h + 1], 0.0,
                                                ALU.add, ALU.min)
                    sig(ins, "seg")
                    for half in range(2):
                        ins = dve.tensor_tensor(qss[s % 2][half], qa[:, 2 * half:2 * half + 2, c * CH:(c + 1) * CH],
                                                iws[s % 2][:, 2 * half:2 * half + 2, :], ALU.mult)
                    sig(ins, "qs")
                    wait(dve, "p_exp", s + 1)
                    v_order.step(dve, dve.tensor_tensor(
                        pmat, pmat, mats[:, tri, :].unsqueeze(1).to_broadcast([P, 4, P]), ALU.mult))
                    wait(dve, "cols", s + 1)
                    sig(dve.tensor_tensor(wide(pmat), wide(pmat), ps[:, 2, :], ALU.mult), "m")

                front(0)
                for s, (d, c, k) in enumerate(order_m):
                    if s + 1 < n_m:
                        front(s + 1)
                    edge = 0 if d else CH - 1
                    em, iw = ems[s % 2], iws[s % 2]
                    wait(dve, "p", s + 1)
                    wait(dve, "em", s + 1)
                    den = ps[:, 4, :].rearrange("p (h n) -> p h n", h=4)
                    v_order.step(dve, dve.tensor_tensor(em, den, em, ALU.max))
                    v_order.step(dve, dve.scalar_tensor_tensor(em, den, -1.0, em, ALU.mult, ALU.max))
                    v_order.step(dve, dve.reciprocal(em, em))
                    dst = chunk4(hT[:, 0:4, :], c)
                    num = ps[:, 3, :].rearrange("p (h n) -> p h n", h=4)
                    if any(x[1] == c for x in order_m[:s]):
                        v_order.step(dve, dve.tensor_tensor(em, num, em, ALU.mult))
                        sig(dve.tensor_tensor(dst, dst, em, ALU.add), "h")
                    else:
                        sig(dve.tensor_tensor(dst, num, em, ALU.mult), "h")
                    wait(dve, "h", s + 1)
                    wait(dve, "masked", s + 1)
                    for h in range(4):
                        st = c_state[d][:, h, :]
                        ins = dve.scalar_tensor_tensor(st, st, iw[:, h, edge:edge + 1],
                                                       ps[:, 5 + h // 2, (h % 2) * 129:(h % 2) * 129 + 129],
                                                       ALU.mult, ALU.add)
                    sig(ins, "mem")
                    wait(dve, "mem", s + 1)

            @block.scalar
            def _(act):
                for s, (d, c, k) in enumerate(order_m):
                    w_col, pmat = w_cols[s % 2], pmats[s % 2]
                    wait(act, "bc", s + 1)
                    if s >= 2:
                        wait(act, "mem", s - 1)
                        wait(act, "qs", s - 1)
                    sig(act.activation(iws[s % 2], ps[:, 0, :].rearrange("p (h n) -> p h n", h=4), ACT.Exp), "iw")
                    sig(act.activation(ems[s % 2], ps[:, 1, :].rearrange("p (h n) -> p h n", h=4), ACT.Exp,
                                       scale=-1.0), "em")
                    wait(act, "seg", s + 1)
                    sig(act.activation(wide(pmat), wide(pmat), ACT.Exp), "p_exp")
                    sig(act.activation(w_col, w_col, ACT.Exp), "w_exp")

            @block.gpsimd
            def _(pool):
                for s, (d, c, k) in enumerate(order_m):
                    wait(pool, "w_exp", s + 1)
                    if s >= 1:
                        wait(pool, "masked", s)
                    sig(pool.tensor_tensor(kw, k_tok[:, c, :].rearrange("p (h n) -> p h n", h=4),
                                           w_cols[s % 2].unsqueeze(2).to_broadcast([P, 4, P]), ALU.mult), "kw")
        for n in R:
            R[n].close(n_m)

        jobs = [(hT[:, t, t0:t0 + n], n, cols[:, COL["mlstm_norm"] + t:COL["mlstm_norm"] + t + 1])
                for t in range(4) for t0, n in BOTH]
        with nc.Block() as block:
            @block.scalar
            def _(act):
                for t in range(4):
                    act.activation(oa[:, t, :], oa[:, t, :], ACT.Sigmoid)
        head_norms(jobs, ones, 128)
        with nc.Block() as block:
            @block.vector
            def _(dve):
                for t in range(4):
                    dve.tensor_tensor(hT[:, t, :], hT[:, t, :], oa[:, t, :], ALU.mult)

            @block.sync
            def _(sp):
                sp.dma_start(qa[:, 0:2, 0:LAT], w["const_tables"][T_CB:T_CB + 2].rearrange("t p n -> p t n"))\
                  .then_inc(loaded.sem, 16)
                sp.wait_ge(loaded.sem, loaded.at(16))
        loaded.close(16)

        jobs = [(buf[:, t, t0:t0 + n], n, cols[:, COL[g]:COL[g] + 1])
                for buf, nt, g in ((qb, 4, "swa_q"), (kb, 1, "swa_k")) for t in range(nt) for t0, n in BOTH]
        head_norms(jobs, blk64, 64)
        rope([qb[:, t, 0:LAT] for t in range(4)] + [kb[:, 0, 0:LAT]], ROT32, qa[:, 0, 0:LAT], qa[:, 1, 0:LAT])
        named("swapped")
        with nc.Block() as block:
            @block.tensor
            def _(pe):
                for r, (t0, n) in enumerate(BOTH):
                    ins = pe.matmul(ps[:, r, 0:n], mats[:, SWAP, :], kb[:, 0, t0:t0 + n], start=True, stop=True)
                ins.then_inc(S["swapped"].sem, 1)

            @block.vector
            def _(dve):
                dve.wait_ge(S["swapped"].sem, S["swapped"].at(1))
                for r, (t0, n) in enumerate(BOTH):
                    dve.tensor_copy(kb[:, 1, t0:t0 + n], ps[:, r, 0:n])
        S["swapped"].close(1)
        bufs = (ka.rearrange("p t n -> p (t n)")[:, 0:2 * TOK].rearrange("p (b n) -> p b n", b=2),
                ka.rearrange("p t n -> p (t n)")[:, 2 * TOK:4 * TOK].rearrange("p (b n) -> p b n", b=2),
                small[:, 0:16].rearrange("p (b n) -> p b n", b=2))
        jobs = []
        for h in range(B_HEADS):
            kv, half = h // (B_HEADS // 2), h % 2
            rows_h = slice(64 * half, 64 * half + 64)
            keys_t = kb[rows_h, 0 if kv == half else 1, :]
            for n in range(NCH):
                keys, v, width = [], [], 0
                if n < NLAT:
                    for kn, mask in ((n - 1, M_PREV), (n, None), (n + 1, M_NEXT)):
                        if 0 <= kn < NLAT:
                            keys.append((keys_t[:, kn * CH:(kn + 1) * CH], width,
                                         None if mask is None else mats[:, mask, :]))
                            v.append(vb[:, kn, kv * 64:(kv + 1) * 64])
                            width += CH
                if width + CTX > 512 > width:
                    cut = 512 - width
                    keys += [(keys_t[:, LAT:LAT + cut], width, None), (keys_t[:, LAT + cut:TOK], 512, None)]
                else:
                    keys.append((keys_t[:, LAT:TOK], width, None))
                v += [vb[:, NLAT + i, kv * 64:(kv + 1) * 64] for i in range(NCTX)]
                width += CTX
                jobs.append((qb[rows_h, h // 2, n * CH:(n + 1) * CH], keys, width, v,
                             rows[:, SINK + h:SINK + h + 1],
                             hT[rows_h, 4 + h // 2, n * CH:(n + 1) * CH]))
        attention(jobs, 64.0 ** -0.5, bufs)
        product_stage(W["ab_out"], 4, whole, from_h, BOTH, add_gated(16), "vector")
        mixer.close()
        mlp_stage(0, BOTH)
        hT, big = mixer_memory(mixer, "1")

        cur[0] = 2
        nonlocal_o[0] = 0
        qc = part(8 * LAT, "p (t n) -> p t n", t=8)
        kc = part(2 * TOK, "p (t n) -> p t n", t=2)
        vc = part(NCH * SLAB, "p (c n) -> p c n", c=NCH)
        tabs = part(2 * LAT, "p (t n) -> p t n", t=2)
        bufs = (part(2 * TOK, "p (b n) -> p b n", b=2), part(2 * TOK, "p (b n) -> p b n", b=2),
                small[:, 0:16].rearrange("p (b n) -> p b n", b=2))
        units = [[("tile", m, 0, LAT, qc[:, 2 * s + m, :], None) for m in range(2)] for s in range(4)]
        units.append([("tile", m, t0, nt, kc[:, m, t0:t0 + nt], None) for m in range(2) for t0, nt in BOTH])
        units.append([("rows", c, 0, SLAB, vc[:, c, :], None) for c in range(NCH)])
        with nc.Block() as block:
            @block.sync
            def _(sp):
                sp.dma_start(tabs, w["const_tables"][T_CC:T_CC + 2].rearrange("t p n -> p t n"))\
                  .then_inc(loaded.sem, 16)
                sp.wait_ge(loaded.sem, loaded.at(16))
        loaded.close(16)
        units_stage(W["c"], units, modulated(0, False, xT, hT, BOTH), None, None)
        jobs = [(qc[:, t, :], LAT, cols[:, COL["c_q_norm"]:COL["c_q_norm"] + 1]) for t in range(8)] + \
               [(kc[:, t, t0:t0 + n], n, cols[:, COL["c_k_norm"]:COL["c_k_norm"] + 1])
                for t in range(2) for t0, n in BOTH]
        head_norms(jobs, ones, 128)
        rope([qc[:, t, :] for t in range(8)] + [kc[:, t, 0:LAT] for t in range(2)], ROT64,
             tabs[:, 0, :], tabs[:, 1, :])
        jobs = []
        for h in range(8):
            kv = h // 4
            for n in range(NLAT):
                keys = [(kc[:, kv, 0:LAT], 0, None), (kc[:, kv, LAT:TOK], 512, None)]
                v = [vc[:, c, kv * P:(kv + 1) * P] for c in range(NCH)]
                jobs.append((qc[:, h, n * CH:(n + 1) * CH], keys, TOK, v, None, hT[:, h, n * CH:(n + 1) * CH]))
        attention(jobs, 128.0 ** -0.5, bufs)
        product_stage(W["c_out"], 4, whole, from_h, ONLY_LAT, add_gated(16), "vector")
        mixer.close()
        mlp_stage(1, ONLY_LAT)

        y_out = sb("y_out", [P, NLAT, D])
        groups = [([xT[:, k, c * CH:(c + 1) * CH] for k in range(4 * q, 4 * q + 4)],
                   y_out[:, c, q * 512:(q + 1) * 512]) for c in range(NLAT) for q in range(2)]
        with nc.Block() as block:
            @block.tensor
            def _(pe):
                transpose_pe(pe, groups)

            @block.vector
            def _(dve):
                transpose_out(dve, groups, 0)

            @block.scalar
            def _(act):
                transpose_out(act, groups, 1)

            @block.sync
            def _(sp):
                for c in range(NLAT):
                    sp.wait_ge(tr_free_v.sem, tr_free_v.at(c + 1))
                    sp.wait_ge(tr_free_a.sem, tr_free_a.at(c + 1))
                    sp.dma_start(out[0, c * CH:(c + 1) * CH, :], y_out[:, c, :]).then_inc(stored.sem, 16)
                sp.wait_ge(stored.sem, stored.at(16 * NLAT))
        transpose_close(groups)


_INS = ["x", "c", "ctx", "c_ctx", "w_ada", "b_ada", "w_in", "ssd_conv_w", "ssd_conv_b", "ssd_dt_bias",
        "ssd_a_log", "ssd_d", "ssd_norm_w", "fnet_w", "pool_w", "pool_scale", "w_out", "ln1_g", "ln1_b",
        "ffn_w_up", "ffn_conv_w", "ffn_conv_b", "ffn_w_down", "ln2_g", "ln2_b", "c_2", "ctx_2", "c_ctx_2",
        "ada_w_2", "ada_b_2", "norm1_g_2", "norm2_g_2", "ab_w_in_2", "ab_gate_b_2", "mlstm_norm_g_2",
        "swa_q_norm_g_2", "swa_k_norm_g_2", "swa_sink_2", "ab_w_out_2", "c_w_in_2", "c_q_norm_g_2",
        "c_k_norm_g_2", "c_w_out_2", "mlp_w1_2", "mlp_w2_2"]


def kernel(**inputs):
    import concourse.bacc as bacc
    from concourse.bass_utils import run_bass_kernel_spmd

    nc = bacc.Bacc("TRN2", target_bir_lowering=False, num_devices=1)
    arrays, w = {}, {}
    data = {n: np.ascontiguousarray(inputs[n]) for n in _INS}
    data["const_mats"], data["const_tables"], data["const_dft"] = shape_constants()
    for name, a in data.items():
        arrays[f"in_{name}"] = a
        w[name] = nc.dram_tensor(f"in_{name}", a.shape, mybir.dt.from_np(a.dtype), kind="ExternalInput").ap()
    out = nc.dram_tensor("out_0", (1, LAT, D), F32, kind="ExternalOutput").ap()
    program(nc, w, out)
    r = run_bass_kernel_spmd(nc, [arrays], core_ids=[0])
    return r.results[0]["out_0"]
```

```python
from contextlib import ExitStack

import numpy as np
import concourse.bass as bass
from concourse import mybir

F32 = mybir.dt.float32
F32R = mybir.dt.float32r
ALU = mybir.AluOpType
ACT = mybir.ActivationFunctionType
AX_X = mybir.AxisListType.X

P = 128
D = 1024
KT = D // P
LAT, CTX = 512, 256
TOK = LAT + CTX
CH = 128
NLAT, NCTX = LAT // CH, CTX // CH
NCH = NLAT + NCTX
BOTH = [(0, LAT), (LAT, CTX)]
ONLY_LAT = [(0, LAT)]
GRID_W = 64
GRID_H = LAT // GRID_W
EPS = 1e-6
ALPHA = 2.0 ** 0.25

SLAB = 256
NS = 4
D_FF = 2816
FT = D_FF // P
D_FF2 = 4096
MT = D_FF2 // P
OFF_XBC, OFF_DT, OFF_FNET, OFF_POOL = 512, 1536, 1552, 1808
N_CONV = 8
A_HEADS = 4
B_HEADS = 8
AB_O, AB_G, AB_QB, AB_KB = 1536, 2048, 2064, 2576

(IDENT, ONES, BLK64, U_LE, U_GE, ROT32, ROT64, SWAP, M_PREV, M_NEXT, DFT_C, DFT_S, SEL, TINY) = range(14)
N_MATS = SEL + A_HEADS + 1
TINY = SEL + A_HEADS
T_CB, T_SB, T_CC, T_SC, T_CNT = 0, 1, 2, 3, 4
NEG = -1e30


def shape_constants():
    i = np.arange(P)
    m = np.zeros((N_MATS, P, P), np.float64)
    m[IDENT] = np.eye(P)
    m[ONES] = 1
    m[BLK64] = i[:, None] // 64 == i[None, :] // 64
    m[U_LE] = i[:, None] <= i[None, :]
    m[U_GE] = i[:, None] >= i[None, :]
    for n, half in ((ROT32, 32), (ROT64, 64)):
        for f in range(P):
            up = f % (2 * half) < half
            m[n, f + half if up else f - half, f] = -1 if up else 1
    m[SWAP] = np.roll(np.eye(P), 64, axis=0)
    m[M_PREV] = np.where(i[None, :] >= i[:, None], 0, NEG)
    m[M_NEXT] = np.where(i[None, :] <= i[:, None], 0, NEG)
    ang = 2 * np.pi * ((i[:, None] * i[None, :]) % 64) / 64
    ortho = 1 / np.sqrt(LAT * 64)
    m[DFT_C] = m[BLK64] * np.cos(ang) * ortho
    m[DFT_S] = -m[BLK64] * np.sin(ang) * ortho
    for h in range(A_HEADS):
        m[SEL + h, h] = 1
    m[TINY, :, 0] = EPS
    for q in range(4):
        m[TINY, 32 * q + np.arange(16), 1 + np.arange(16)] = 1
    t = np.zeros((6, P, LAT), np.float64)
    pos = np.arange(LAT)
    for n, head in ((T_CB, 64), (T_CC, 128)):
        pairs = head // 4
        inv = (np.float32(10000.0) ** (-np.arange(pairs, dtype=np.float32) / pairs)).astype(np.float32)
        ang = np.concatenate([(pos // GRID_W)[:, None].astype(np.float32) * inv,
                              (pos % GRID_W)[:, None].astype(np.float32) * inv], axis=1).T.astype(np.float64)
        ang = np.tile(ang, (P // (head // 2), 1))
        t[n], t[n + 1] = np.cos(ang), np.sin(ang)
    for g, win in enumerate((2, 4, 8, 16)):
        left = win // 2
        hi, lo = np.minimum(pos + win - left, LAT), np.maximum(pos - left, 0)
        t[T_CNT + g // 2, (g % 2) * 64:(g % 2) * 64 + 64] = 1.0 / (hi - lo)
    ang = 2 * np.pi * ((pos[:, None] * pos[None, :]) % LAT) / LAT
    dft = np.stack([np.cos(ang), np.sin(ang)])
    return m.astype(np.float32), t.astype(np.float32), dft.astype(np.float32)


class Tally:

    def __init__(self, sem):
        self.sem, self.base = sem, 0

    def at(self, n):
        return self.base + n

    def close(self, n):
        self.base += n


class Order:

    def __init__(self, sem):
        self.sem, self.n = sem, 0

    def mark(self, ins):
        ins.then_inc(self.sem, 1)
        self.n += 1
        return self.n

    def step(self, eng, ins):
        eng.wait_ge(self.sem, self.mark(ins))


def program(nc, w, out):
    ctx = ExitStack()
    with ctx:
        def sb(name, shape, scope=None, dtype=F32):
            return (scope or ctx).enter_context(nc.sbuf_tensor(name, shape, dtype))

        def tally(name):
            return Tally(ctx.enter_context(nc.semaphore(name)))

        def order(name):
            return Order(ctx.enter_context(nc.semaphore(name)))

        xT = sb("xT", [P, KT, TOK])
        ring = sb("ring", [P, NS, KT, SLAB])
        mean = sb("mean", [P, TOK])
        rstd = sb("rstd", [P, TOK])
        squares = sb("squares", [P, 3, LAT])
        mats = sb("mats", [P, N_MATS, P])
        cols = sb("cols", [P, 768])
        mods = sb("mods", [P, 3, 48, 2])
        scls = sb("scls", [P, 3, 2, 8, 2])
        sil = sb("sil", [P, 2, 8, 32])
        ada_rows = sb("ada_rows", [P, 2, SLAB])
        rows = sb("rows", [P, 64])
        dskip = sb("dskip", [P, 4])
        small = sb("small", [P, 512])
        wnarrow = sb("wnarrow", [P, KT, 16])
        ps = ctx.enter_context(nc.psum_tensor("ps", [P, 8, 512], F32))

        mixer, stage = ctx.enter_context(ExitStack()), ctx.enter_context(ExitStack())

        def own_memory(name):
            return sb("big" + name, [P, 24576], stage)

        hT, big = sb("hT0", [P, KT, TOK], mixer), own_memory("0")

        ident, ones, blk64 = mats[:, IDENT, :], mats[:, ONES, :], mats[:, BLK64, :]
        eps_col = mats[:, TINY, 0:1]
        sum_groups = mats[:, TINY, 1:17]
        cur = [0]

        slot_loaded = [ctx.enter_context(nc.semaphore(f"slot_loaded{s}")) for s in range(NS)]
        mm_done = ctx.enter_context(nc.semaphore("mm_done"))
        loaded = tally("loaded")
        stored = tally("stored")
        mm_free = tally("mm_free")
        mm_free_v = tally("mm_free_v")
        tr_ready, tr_free_v, tr_free_a = tally("tr_ready"), tally("tr_free_v"), tally("tr_free_a")
        v_order, a_order, g_order = order("v_order"), order("a_order"), order("g_order")
        N = {n: tally("norm_" + n) for n in ("sum", "mean", "centered", "sq", "sq_used", "std", "scaled", "out", "hi", "lo", "lo_v", "recip")}
        S = {}

        def named(*names):
            for n in names:
                if n not in S:
                    S[n] = tally(n)
            return {n: S[n] for n in names}

        stream = []
        signals = [0]

        def add_slabs(name, layer, row_groups, col_starts, n_signals):
            first = len(stream)
            for j, c in enumerate(col_starts):
                for r0, kt in row_groups:
                    stream.append((name, layer, r0, kt, c))
                    signals.append(signals[-1] + (n_signals[j] if isinstance(n_signals, list) else n_signals))
            return first

        whole = [(0, KT)]
        cols_of = lambda start, n: [start + SLAB * i for i in range(n)]
        W = {}
        W["ada"] = add_slabs("w_ada", 0, whole, cols_of(0, 8), 1)
        W["in"] = len(stream)
        for n, (c, s) in enumerate(zip(cols_of(OFF_XBC, 4) + cols_of(0, 2) + [OFF_FNET, OFF_POOL],
                                       [4, 4, 4, 2, 2, 2, 2, 2])):
            add_slabs("w_in", 0, whole, [c], s)
            add_slabs("w_ada", 0, whole, cols_of(SLAB * (8 + 2 * n), 2), 1)
        W["out"] = add_slabs("w_out", 0, whole, cols_of(0, 4), 2)
        W["up"] = len(stream)
        for j in range(FT // 2):
            add_slabs("ffn_w_up", 0, whole, [SLAB * j], 2)
            add_slabs("ada_w_2", 0, whole, cols_of(2 * SLAB * j, 2 if j < FT // 2 - 1 else 4), 1)
            add_slabs("ffn_w_up", 0, whole, [D_FF + SLAB * j], 2)
        DOWN_ROWS = [(0, 8), (1024, 8), (2048, 6)]
        W["down"] = len(stream)
        for rows_kt in DOWN_ROWS:
            add_slabs("ffn_w_down", 0, [rows_kt], cols_of(0, 4), 2)
        W["ab"] = add_slabs("ab_w_in_2", 0, whole,
                            cols_of(0, 4) + cols_of(1024, 4) + cols_of(AB_QB, 2) + [AB_KB],
                            [4] * 4 + [NCH] * 2 + [4] * 2 + [4] * 2 + [2 + NCH])
        W["ab_out"] = add_slabs("ab_w_out_2", 0, whole, cols_of(0, 4), 4)
        W["mlp_0"], ada_col = len(stream), [0]
        for q in range(4):
            for j in range(4):
                add_slabs("mlp_w1_2", 0, whole, [1024 * q + SLAB * j], 4)
                for _ in range(1 if q else (2, 2, 2, 3)[j]):
                    add_slabs("ada_w_2", 1, whole, [ada_col[0]], 1)
                    ada_col[0] += SLAB
            for j in range(4):
                add_slabs("mlp_w2_2", 0, [(1024 * q, KT)], [SLAB * j], 4)
                if q == 0 and j < 3:
                    add_slabs("ada_w_2", 1, whole, [ada_col[0]], 1)
                    ada_col[0] += SLAB
        W["c"] = add_slabs("c_w_in_2", 0, whole, cols_of(0, 6), [2] * 4 + [4, NCH])
        W["c_out"] = add_slabs("c_w_out_2", 0, whole, cols_of(0, 4), 2)
        W["mlp_1"] = len(stream)
        for q in range(4):
            add_slabs("mlp_w1_2", 1, whole, cols_of(1024 * q, 4), 2)
            add_slabs("mlp_w2_2", 1, [(1024 * q, KT)], cols_of(0, 4), 2)
        issued = [0]

        def slab_source(entry, i=None, d_row=0, d_col=0):
            name, layer, r0, kt, c = entry
            if i is None:
                return w[name][layer, r0:r0 + kt * P, c:c + SLAB].rearrange("(k p) n -> p k n", p=P)
            m = w[name][layer]
            if d_row:
                m = m[bass.ds(i * d_row + r0, kt * P), :]
            else:
                m = m[r0:r0 + kt * P, :]
            m = m.rearrange("(k p) n -> p k n", p=P)
            return m[:, :, bass.ds(i * d_col + c, SLAB)] if d_col else m[:, :, c:c + SLAB]

        def load_slabs(sp, upto):
            upto = min(upto, len(stream))
            n = issued[0]

            def one(n, i=None, step=(0, 0), per_turn=0):
                if n >= NS:
                    used = signals[n - NS + 1]
                    sp.wait_ge(mm_done, used if i is None else i * per_turn + used)
                sp.dma_start(ring[:, n % NS, 0:stream[n][3], :], slab_source(stream[n], i, *step))\
                  .then_inc(slot_loaded[n % NS], 16)

            def turns_alike(n, period):
                if n < NS or n + 2 * period > upto:
                    return 1, None, 0
                steps = [(stream[n + period + s][2] - stream[n + s][2], stream[n + period + s][4] - stream[n + s][4])
                         for s in range(period)]
                per_turn = signals[n] - signals[n - NS] if period == NS else signals[n + period] - signals[n]
                reps = 1
                while n + period * (reps + 1) <= upto and all(
                        signals[n + period * reps + s - NS + 1] == signals[n + s - NS + 1] + per_turn * reps and
                        stream[n + period * reps + s] ==
                        (*stream[n + s][:2], stream[n + s][2] + dr * reps, stream[n + s][3], stream[n + s][4] + dc * reps)
                        for s, (dr, dc) in enumerate(steps)):
                    reps += 1
                return reps, steps, per_turn

            while n < upto:
                best = max((NS, 2 * NS, 3 * NS), key=lambda p: (turns_alike(n, p)[0] - 1) * p)
                reps, steps, per_turn = turns_alike(n, best)
                if reps >= 3:
                    with sp.Fori(0, reps) as i:
                        for s in range(best):
                            one(n + s, i, steps[s], per_turn)
                    n += best * reps
                else:
                    one(n)
                    n += 1
            issued[0] = n

        def wait_slab(pe, n, i=None, slabs_per_turn=0):
            v = 16 * (n // NS + 1)
            pe.wait_ge(slot_loaded[n % NS], v if i is None else i * (16 * slabs_per_turn // NS) + v)

        def turns(eng, count, period, body, peel=0):
            n = count // period
            for j in range(peel * period):
                body(None, j)
            if n - peel >= 2:
                with eng.Fori(peel, n) as i:
                    for j in range(period):
                        body(i, j)
            else:
                for j in range(peel * period, n * period):
                    body(None, j)
            for j in range(n * period, count):
                body(None, j)

        def at(i, period, j):
            return j if i is None else i * period + j

        def transpose_pe(pe, groups):
            for u, (srcs, _) in enumerate(groups):
                if u >= 8:
                    t = (tr_free_v, tr_free_a)[u % 2]
                    pe.wait_ge(t.sem, t.at((u - 8) // 2 + 1))
                for j, s in enumerate(srcs):
                    f, p = s.shape[1], s.shape[0]
                    ins = pe.transpose(ps[0:f, u % 8, j * p:(j + 1) * p], s, ident[0:p, 0:p])
                ins.then_inc(tr_ready.sem, 1)

        def transpose_out(eng, groups, which):
            t = (tr_free_v, tr_free_a)[which]
            for u, (srcs, dst) in enumerate(groups):
                if u % 2 != which:
                    continue
                eng.wait_ge(tr_ready.sem, tr_ready.at(u + 1))
                f, p = srcs[0].shape[1], srcs[0].shape[0]
                src = ps[0:f, u % 8, 0:p * len(srcs)]
                if which:
                    nc.scalar.copy(dst, src).then_inc(t.sem, 1)
                else:
                    nc.vector.tensor_copy(dst, src).then_inc(t.sem, 1)

        def transpose_close(groups):
            tr_ready.close(len(groups))
            tr_free_v.close((len(groups) + 1) // 2)
            tr_free_a.close(len(groups) // 2)

        class Norm:

            def __init__(self, centre, ranges, src, dst, scale, shift, split=None):
                self.centre, self.ranges, self.src, self.dst = centre, ranges, src, dst
                self.scale, self.shift, self.split = scale, shift, split
                self.tiles = [(r, k, *ranges[r]) for r in range(len(ranges)) for k in range(KT)]

            def where(self, u):
                r, k, t0, n = self.tiles[u]
                return self.split[2][:, u % 4, 0:n] if self.split else self.dst[:, k, t0:t0 + n]

            def pe(self, pe):
                if self.centre:
                    for r, k, t0, n in self.tiles:
                        ins = pe.matmul(ps[:, r, 0:n], ones, self.src[:, k, t0:t0 + n],
                                        start=(k == 0), stop=(k == KT - 1))
                        if k == KT - 1:
                            ins.then_inc(N["sum"].sem, 1)
                for u, (r, k, t0, n) in enumerate(self.tiles):
                    pe.wait_ge(N["sq"].sem, N["sq"].at(u + 1))
                    pe.matmul(ps[:, 2 + r, 0:n], ones, squares[:, u % 3, 0:n],
                              start=(k == 0), stop=(k == KT - 1)).then_inc(N["sq_used"].sem, 1)

            def ready(self, pe, r, k):
                t = N["lo"] if self.split else N["out"]
                pe.wait_ge(t.sem, t.at(r * KT + k + 1))

            def act(self, act):
                n_sq = 3
                if self.centre:
                    for r, (t0, n) in enumerate(self.ranges):
                        act.wait_ge(N["sum"].sem, N["sum"].at(r + 1))
                        act.activation(mean[:, t0:t0 + n], ps[:, r, 0:n], ACT.Copy, scale=1.0 / D)\
                           .then_inc(N["mean"].sem, 1)
                for u, (r, k, t0, n) in enumerate(self.tiles):
                    if self.centre:
                        act.wait_ge(N["centered"].sem, N["centered"].at(u + 1))
                    if u >= n_sq:
                        act.wait_ge(N["sq_used"].sem, N["sq_used"].at(u - n_sq + 1))
                    act.activation(squares[:, u % n_sq, 0:n],
                                   self.where(u) if self.centre else self.src[:, k, t0:t0 + n], ACT.Square)\
                       .then_inc(N["sq"].sem, 1)
                for r, (t0, n) in enumerate(self.ranges):
                    act.wait_ge(N["sq_used"].sem, N["sq_used"].at((r + 1) * KT))
                    act.activation(rstd[:, t0:t0 + n], ps[:, 2 + r, 0:n], ACT.Sqrt, bias=eps_col,
                                   scale=1.0 / D).then_inc(N["std"].sem, 1)
                for u, (r, k, t0, n) in enumerate(self.tiles):
                    act.wait_ge(N["scaled"].sem, N["scaled"].at(u + 1))
                    act.activation(self.where(u), self.where(u), ACT.Identity,
                                   bias=self.shift(k, r), scale=self.scale(k, r)).then_inc(N["out"].sem, 1)

            def centred(self, dve, u):
                _, k, t0, n = self.tiles[u]
                dve.tensor_tensor(self.where(u), self.src[:, k, t0:t0 + n], mean[:, t0:t0 + n], ALU.subtract)\
                   .then_inc(N["centered"].sem, 1)

            def dve(self, dve):
                if self.centre:
                    for u, (r, k, _, _) in enumerate(self.tiles):
                        if k == 0:
                            dve.wait_ge(N["mean"].sem, N["mean"].at(r + 1))
                        if self.split and u >= 4:
                            dve.wait_ge(N["sq"].sem, N["sq"].at(u - 3))
                        self.centred(dve, u)

                def scaled(u):
                    r, k, t0, n = self.tiles[u]
                    if k == 0:
                        dve.wait_ge(N["std"].sem, N["std"].at(r + 1))
                        dve.reciprocal(rstd[:, t0:t0 + n], rstd[:, t0:t0 + n]).then_inc(N["recip"].sem, 1)
                        dve.wait_ge(N["recip"].sem, N["recip"].at(r + 1))
                    if self.split and u >= 4:
                        dve.wait_ge(N["lo"].sem, N["lo"].at(u - 3))
                    src = self.src[:, k, t0:t0 + n]
                    if self.centre:
                        src = self.where(u)
                        if self.split:
                            self.centred(dve, u)
                            dve.wait_ge(N["centered"].sem, N["centered"].at(len(self.tiles) + u + 1))
                    dve.tensor_tensor(self.where(u), src, rstd[:, t0:t0 + n], ALU.mult)\
                       .then_inc(N["scaled"].sem, 1)

                for u in range(len(self.tiles) + 2):
                    if u < len(self.tiles):
                        scaled(u)
                    if self.split and u >= 2:
                        r, k, t0, n = self.tiles[u - 2]
                        dve.wait_ge(N["out"].sem, N["out"].at(u - 1))
                        dve.tensor_copy(self.split[0][:, k, t0:t0 + n], self.where(u - 2)).then_inc(N["hi"].sem, 1)

            def pool(self, pool):
                if self.split:
                    for u, (r, k, t0, n) in enumerate(self.tiles):
                        pool.wait_ge(N["hi"].sem, N["hi"].at(u + 1))
                        pool.tensor_tensor(self.split[1][:, k, t0:t0 + n], self.where(u),
                                           self.split[0][:, k, t0:t0 + n].bitcast(F32), ALU.subtract)\
                            .then_inc(N["lo"].sem, 1)

            def close(self):
                for names, n in ((("sum", "mean"), len(self.ranges) * self.centre),
                                 (("centered",), len(self.tiles) * self.centre * (2 if self.split else 1)),
                                 (("sq", "sq_used", "scaled", "out"), len(self.tiles)),
                                 (("std", "recip"), len(self.ranges)),
                                 (("hi", "lo"), len(self.tiles) * (self.split is not None))):
                    for name in names:
                        N[name].close(n)

        class Halves:

            def __init__(self, ranges, hi, lo, more):
                self.ranges, self.hi, self.lo, self.more = ranges, hi, lo, more
                self.tiles = [(k, *ranges[r]) for r in range(len(ranges)) for k in range(KT)]

            def low(self, eng, u):
                k, t0, n = self.tiles[u]
                return eng.tensor_tensor(self.lo[:, k, t0:t0 + n], hT[:, k, t0:t0 + n],
                                         self.hi[:, k, t0:t0 + n].bitcast(F32), ALU.subtract)

            def pe(self, pe):
                pass

            def act(self, act):
                pass

            def ready(self, pe, r, k):
                u = r * KT + k
                t = (N["lo"], N["lo_v"])[u % 2]
                pe.wait_ge(t.sem, t.at(u // 2 + 1))

            def dve(self, dve):
                for u, (k, t0, n) in enumerate(self.tiles):
                    dve.tensor_copy(self.hi[:, k, t0:t0 + n], hT[:, k, t0:t0 + n]).then_inc(N["hi"].sem, 1)
                    if u % 2:
                        dve.wait_ge(N["hi"].sem, N["hi"].at(u + 1))
                        self.low(dve, u).then_inc(N["lo_v"].sem, 1)
                if self.more is not None:
                    self.more(dve)

            def pool(self, pool):
                for u in range(0, len(self.tiles), 2):
                    pool.wait_ge(N["hi"].sem, N["hi"].at(u + 1))
                    self.low(pool, u).then_inc(N["lo"].sem, 1)

            def close(self):
                N["hi"].close(len(self.tiles))
                for name in ("lo", "lo_v"):
                    N[name].close(len(self.tiles) // 2)

        def norm_stage(norm):
            with nc.Block() as block:
                @block.sync
                def _(sp):
                    load_slabs(sp, done[0] + NS)
                block.tensor(norm.pe)
                block.scalar(norm.act)
                block.vector(norm.dve)
            norm.close()

        def modulated(norm_no, centre, src, dst, ranges, split=None):
            sh, lay = 24 * norm_no, cur[0]
            return Norm(centre, ranges, src, dst, lambda k, r: scls[:, lay, norm_no, k, r:r + 1],
                        lambda k, r: mods[:, lay, sh + k, r:r + 1], split)

        done = [0]

        ADA = named("ada_rows_out", "ada_tiles")

        def turn_wait(eng, t, v, i, per_turn):
            eng.wait_ge(t.sem, t.at(v) if i is None else i * per_turn + t.at(v))

        def ada_slab(pe, which, n, a, i=None, slabs=0, per_turn=0):
            wait_slab(pe, n, i, slabs)
            if a - ada_first[0] >= 2 or i is not None:
                turn_wait(pe, ADA["ada_rows_out"], a - ada_first[0] - 1, i, per_turn)
            for kk in range(2):
                for q in range(4):
                    ins = pe.matmul(ps[32 * q:32 * q + 32, 6 + a % 2, 0:SLAB], sil[:, which, 2 * q + kk, :],
                                    ring[:, n % NS, 2 * q + kk, :], start=(kk == 0), stop=(kk == 1))
            ins.then_inc(mm_done, 1)

        def ada_tiles(pe, a, i=None, per_turn=0):
            turn_wait(pe, ADA["ada_rows_out"], a - ada_first[0] + 1, i, per_turn)
            for m in range(2):
                o = at(i, 4 * per_turn, 4 * a + 2 * m)
                dst = ps[:, 5, o:o + 2] if i is None else ps[:, 5, bass.ds(o, 2)]
                ins = pe.matmul(dst, ada_rows[:, a % 2, m * P:(m + 1) * P], sum_groups[:, 0:2], start=True,
                                stop=True)
            ins.then_inc(ADA["ada_tiles"].sem, 1)

        def ada_take(act, n, a, i=None, per_turn=0, done_per_turn=0):
            v = signals[n] + 1
            act.wait_ge(mm_done, v if i is None else i * done_per_turn + v)
            if a - ada_first[0] >= 2 or i is not None:
                turn_wait(act, ADA["ada_tiles"], a - ada_first[0] - 1, i, per_turn)
            act.activation(ada_rows[:, a % 2, :], ps[:, 6 + a % 2, 0:SLAB], ACT.Copy)\
               .then_inc(ADA["ada_rows_out"].sem, 1)

        ada_first = [0]

        def ada_finish(dve, lay, first, last, bias_col, gain_cols):
            dve.wait_ge(ADA["ada_tiles"].sem, ADA["ada_tiles"].at(last - first))
            m0, m1 = 2 * first, 2 * last
            v_order.step(dve, dve.tensor_tensor(
                mods[:, lay, m0:m1, :], ps[:, 5, 2 * m0:2 * m1].rearrange("p (m c) -> p m c", c=2),
                cols[:, bias_col + m0:bias_col + m1].unsqueeze(2).to_broadcast([P, m1 - m0, 2]), ALU.add))
            for n in range(2):
                if not (m0 <= 8 + 24 * n and 16 + 24 * n <= m1):
                    continue
                v_order.step(dve, dve.tensor_scalar(scls[:, lay, n, :, :], mods[:, lay, 8 + 24 * n:16 + 24 * n, :],
                                                    1.0, None, ALU.add))
                if gain_cols is not None:
                    g = cols[:, gain_cols[n]:gain_cols[n] + 8].unsqueeze(2).to_broadcast([P, 8, 2])
                    v_order.step(dve, dve.tensor_tensor(scls[:, lay, n, :, :], scls[:, lay, n, :, :], g, ALU.mult))

        def ada_close(n):
            for t in ADA.values():
                t.close(n)

        def ada_stage(which, slab0, count, lay, bias_col, gain_cols):
            done[0] = slab0 + count
            ada_first[0] = 0
            with nc.Block() as block:
                @block.sync
                def _(sp):
                    load_slabs(sp, done[0] + NS)

                @block.tensor
                def _(pe):
                    def slab(i, j):
                        ada_slab(pe, which, slab0 + j, j, i, NS, NS)
                        if j or i is not None:
                            ada_tiles(pe, j - 1, i, NS)
                    turns(pe, count, NS, slab, 1)
                    ada_tiles(pe, count - 1)

                @block.scalar
                def _(act):
                    turns(act, count, NS, lambda i, j: ada_take(act, slab0 + j, j, i, NS, NS), 1)

                @block.vector
                def _(dve):
                    ada_finish(dve, lay, 0, count, bias_col, gain_cols)
            ada_close(count)

        def tile_of(buf, t, n, t0=0, width=None):
            width = n if width is None else width
            if isinstance(t, int):
                return buf[:, t, t0:t0 + width]
            return buf.rearrange("p t n -> p (t n)")[:, bass.ds(t * n + t0, width)]

        def column_of(buf, c):
            return buf[:, c:c + 1] if isinstance(c, int) else buf[:, bass.ds(c, 1)]

        def units_stage(slab0, units, norm, narrow, bias_rows, cleared=(), ada=None,
                        on_dve=None, on_act=None, head_jobs=(), head_mat=None, head=P):
            jobs_of = [[] for _ in units]
            for n, js in enumerate(head_jobs):
                for job in js:
                    jobs_of[n].append((sum(len(x) for x in jobs_of), job))
            n_jobs = sum(len(x) for x in jobs_of)
            H = named("head_sq", "head_var", "head_std", "head_recip", "head_normed")
            temps = [rstd[:, 0:LAT], mean[:, 0:LAT]]
            head_wait = lambda eng, name, v: eng.wait_ge(H[name].sem, H[name].at(v))

            def head_sums(pe, n):
                for u, (src, m, _) in jobs_of[n]:
                    head_wait(pe, "head_sq", u + 1)
                    if u >= 2:
                        head_wait(pe, "head_std", u - 1)
                    pe.matmul(ps[:, 5 + u % 2, 0:m], head_mat, squares[:, u % 3, 0:m], start=True, stop=True)\
                      .then_inc(H["head_var"].sem, 1)

            def head_squares(act, n, stored):
                if jobs_of[n]:
                    act.wait_ge(mm_free.sem, mm_free.at(stored))
                for u, (src, m, _) in jobs_of[n]:
                    if u >= 3:
                        head_wait(act, "head_var", u - 2)
                    act.activation(squares[:, u % 3, 0:m], src, ACT.Square).then_inc(H["head_sq"].sem, 1)

            def head_roots(act, n):
                for u, (src, m, _) in jobs_of[n]:
                    head_wait(act, "head_var", u + 1)
                    if u >= 2:
                        head_wait(act, "head_normed", u - 1)
                    act.activation(temps[u % 2][:, 0:m], ps[:, 5 + u % 2, 0:m], ACT.Sqrt, bias=eps_col,
                                   scale=1.0 / head).then_inc(H["head_std"].sem, 1)

            def head_norm(dve):
                for u, (src, m, gain) in (x for js in jobs_of for x in js):
                    t = temps[u % 2][:, 0:m]
                    head_wait(dve, "head_std", u + 1)
                    dve.reciprocal(t, t).then_inc(H["head_recip"].sem, 1)
                    head_wait(dve, "head_recip", u + 1)
                    dve.scalar_tensor_tensor(src, src, gain, t, ALU.mult, ALU.mult)\
                       .then_inc(H["head_normed"].sem, 1)

            stride = 3 if ada else 1
            slab_of = lambda n: slab0 + stride * n
            last_unit = lambda u: u + 1 == len(flat) or flat[u + 1][0] != flat[u][0]
            done[0] = slab0 + stride * len(units)
            ada_first[0] = ada[3] if ada else 0
            named("narrow", "cleared")
            flat = [(n, x) for n, us in enumerate(units) for x in us]
            assert all(signals[slab_of(n) + 1] - signals[slab_of(n)] == len(us) for n, us in enumerate(units))
            with nc.Block() as block:
                @block.sync
                def _(sp):
                    if narrow is not None:
                        sp.dma_start(wnarrow[:, :, :], narrow.rearrange("(k p) n -> p k n", p=P))\
                          .then_inc(loaded.sem, 16)
                    load_slabs(sp, done[0] + NS)

                @block.tensor
                def _(pe):
                    def narrow_products():
                        pe.wait_ge(loaded.sem, loaded.at(16))
                        for c in range(NCH):
                            for k in range(KT):
                                ins = pe.matmul(ps[:, 4, c * 16:(c + 1) * 16], hT[:, k, c * CH:(c + 1) * CH],
                                                wnarrow[:, k, :], start=(k == 0), stop=(k == KT - 1))
                        ins.then_inc(S["narrow"].sem, 1)

                    norm.pe(pe)
                    pe.wait_ge(N["std"].sem, N["std"].at(len(norm.ranges)))
                    ready = set()
                    for u, (n, x) in enumerate(flat):
                        fresh_slab = u == 0 or flat[u - 1][0] != n
                        if fresh_slab:
                            if n == 1 and narrow is not None:
                                narrow_products()
                            wait_slab(pe, slab_of(n))
                        r = int(x[2] >= LAT if x[0] == "tile" else x[1] >= NLAT)
                        fresh = r not in ready
                        ready.add(r)
                        if u >= 4:
                            pe.wait_ge(mm_free.sem, mm_free.at(u - 3))
                        slab = ring[:, slab_of(n) % NS, :, :]
                        for k in range(KT):
                            if fresh:
                                norm.ready(pe, r, k)
                            if x[0] == "tile":
                                _, m, t0, nt, _, _ = x
                                ins = pe.matmul(ps[:, u % 4, 0:nt], slab[:, k, m * P:(m + 1) * P],
                                                hT[:, k, t0:t0 + nt], start=(k == 0), stop=(k == KT - 1))
                            else:
                                _, c, c0, nt, _, _ = x
                                ins = pe.matmul(ps[:, u % 4, 0:nt], hT[:, k, c * CH:(c + 1) * CH],
                                                slab[:, k, c0:c0 + nt], start=(k == 0), stop=(k == KT - 1))
                        ins.then_inc(mm_done, 1)
                        if ada and fresh_slab and n:
                            for a in (2 * n - 2, 2 * n - 1):
                                ada_tiles(pe, ada[3] + a)
                        if fresh_slab and n:
                            head_sums(pe, n - 1)
                        if ada and last_unit(u):
                            for a in (0, 1):
                                ada_slab(pe, ada[0], slab_of(n) + 1 + a, ada[3] + 2 * n + a)
                    if ada:
                        for a in (2 * len(units) - 2, 2 * len(units) - 1):
                            ada_tiles(pe, ada[3] + a)

                @block.vector
                def _(dve):
                    norm.dve(dve)
                    if narrow is not None:
                        dve.wait_ge(S["narrow"].sem, S["narrow"].at(1))
                        dve.tensor_tensor(small[:, 0:NCH * 16].rearrange("p (c n) -> p c n", n=16),
                                          ps[:, 4, 0:NCH * 16].rearrange("p (c n) -> p c n", n=16),
                                          bias_rows.unsqueeze(1).to_broadcast([P, NCH, 16]), ALU.add)
                    head_norm(dve)
                    if on_dve is not None:
                        on_dve(dve)
                    if ada:
                        ada_finish(dve, ada[1], ada[3], ada[3] + 2 * len(units), ada[2], None)

                @block.gpsimd
                def _(pool):
                    for view, value in cleared:
                        pool.memset(view, value).then_inc(S["cleared"].sem, 1)

                @block.scalar
                def _(act):
                    norm.act(act)
                    if cleared:
                        act.wait_ge(S["cleared"].sem, S["cleared"].at(len(cleared)))
                    for u, (n, x) in enumerate(flat):
                        m = u - next(v for v, y in enumerate(flat) if y[0] == n)
                        if on_act is not None and n == len(units) - 2 and m == 0:
                            on_act(act)
                        act.wait_ge(mm_done, signals[slab_of(n)] + m + 1)
                        act.activation(x[4], ps[:, u % 4, 0:x[3]] if len(x[4].shape) == 2 else
                                       ps[:, u % 4, 0:x[3]].rearrange("p (h d) -> p h d", d=x[4].shape[2]),
                                       ACT.Copy, scale=x[5] or 1.0).then_inc(mm_free.sem, 1)
                        if m == 0 and n:
                            head_roots(act, n - 1)
                        if last_unit(u):
                            head_squares(act, n, u + 1)
                        if ada and last_unit(u):
                            for a in (0, 1):
                                ada_take(act, slab_of(n) + 1 + a, ada[3] + 2 * n + a)
            mm_free.close(len(flat))
            norm.close()
            for x in H.values():
                x.close(n_jobs)
            if ada:
                ada_close(2 * len(units))
            S["cleared"].close(len(cleared))
            if narrow is not None:
                loaded.close(16)
                S["narrow"].close(1)

        SW = named("w_hi", "w_lo")

        def val(x, i, per):
            return x if i is None else i * per + x

        def split_stage(w_parts, segments, norm, after=None, w_units=4, after_of={}, until=0):
            w_hi, w_lo = w_parts
            F = {"act": mm_free, "dve": mm_free_v}
            segs, half, unit, kinds = [], 0, 0, {"act": 0, "dve": 0}
            history = []
            prev_w = None
            for items, reps in segments:
                seg = {"items": [], "reps": reps, "half0": half, "ns": len(items),
                       "sig": signals[items[0][1] + len(items)] - signals[items[0][1]]}
                kinds0 = dict(kinds)
                for it in items:
                    if it[0] == "ada":
                        seg["items"].append({"ada": it[1:]})
                        continue
                    x = dict(zip(("n", "kt", "rhs", "ranges", "eng", "take", "hooks"), it[1:]))
                    x["half"], x["prev"], x["units"] = half, prev_w, []
                    half += 2
                    for m in range(2):
                        for r in range(len(x["ranges"])):
                            u = len(history)
                            x["units"].append({"m": m, "r": r, "bank": u % w_units, "idx": kinds[x["eng"]],
                                               "reuses": history[u - w_units] if u >= w_units else None})
                            history.append((x["eng"], kinds[x["eng"]]))
                            kinds[x["eng"]] += 1
                    prev_w = x
                    seg["items"].append(x)
                seg["halves"] = half - seg["half0"]
                seg["kinds"] = {k: kinds[k] - kinds0[k] for k in kinds}
                seg["adas"] = sum(1 for it in items if it[0] == "ada")
                for t in range(reps - 1):
                    assert (seg["halves"] and len(items) % NS == 0)
                    half += seg["halves"]
                    for k in kinds:
                        kinds[k] += seg["kinds"][k]
                if reps > 1:
                    n_u = sum(len(x["units"]) for x in seg["items"] if "n" in x)
                    assert n_u % w_units == 0
                    history = history + [(k, v + seg["kinds"][k] * (reps - 1)) for k, v in history[-n_u:]]
                    prev_w = dict(prev_w, n=prev_w["n"] + seg["ns"] * (reps - 1))
                segs.append(seg)
            done[0] = max(until, segments[0][0][0][1] + sum(len(items) * reps for items, reps in segments))

            def run(eng, body):
                for s, seg in enumerate(segs):
                    if seg["reps"] > 1:
                        with eng.Fori(0, seg["reps"]) as i:
                            body(s, seg, i)
                    else:
                        body(s, seg, None)

            def next_w(s, seg, pos, i):
                for x in seg["items"][pos + 1:]:
                    if "n" in x:
                        return x, i, seg
                first = next(x for x in seg["items"] if "n" in x)
                if i is not None:
                    return first, i + 1, seg
                if s + 1 < len(segs):
                    nxt = segs[s + 1]
                    return next(x for x in nxt["items"] if "n" in x), (None if nxt["reps"] == 1 else 0), nxt
                return None

            with nc.Block() as block:
                @block.sync
                def _(sp):
                    load_slabs(sp, done[0] + NS)

                def high(act, x, i, seg, m):
                    if m == 0:
                        wait_slab(act, x["n"], i, seg["ns"])
                    if x["prev"] is not None:
                        v = signals[x["prev"]["n"]] + (m + 1) * len(x["prev"]["ranges"])
                        act.wait_ge(mm_done, val(v, i, seg["sig"]))
                    act.activation(w_hi[m][:, 0:x["kt"], :], ring[:, x["n"] % NS, 0:x["kt"], m * P:(m + 1) * P],
                                   ACT.Copy).then_inc(SW["w_hi"].sem, 1)

                def low(pool, x, i, seg, m):
                    turn_wait(pool, SW["w_hi"], x["half"] + m + 1, i, seg["halves"])
                    pool.tensor_tensor(w_lo[m][:, 0:x["kt"], :],
                                       ring[:, x["n"] % NS, 0:x["kt"], m * P:(m + 1) * P],
                                       w_hi[m][:, 0:x["kt"], :].bitcast(F32), ALU.subtract)\
                        .then_inc(SW["w_lo"].sem, 1)

                def takes(eng, name, x, i, seg, m):
                    for un in x["units"]:
                        if un["m"] == m and x["eng"] == name:
                            v = signals[x["n"]] + m * len(x["ranges"]) + un["r"] + 1
                            eng.wait_ge(mm_done, val(v, i, seg["sig"]))
                            bank = ps[:, un["bank"], 0:x["ranges"][un["r"]][1]]
                            x["take"](i, m, un["r"], bank, un).then_inc(F[name].sem, 1)

                @block.tensor
                def _(pe):
                    norm.pe(pe)

                    def body(s, seg, i):
                        late = []
                        for x in seg["items"]:
                            if "ada" in x:
                                n, which, a = x["ada"]
                                ada_slab(pe, which, n, a, i, seg["ns"], seg["adas"])
                                late.append(a)
                                if len(late) > 2:
                                    ada_tiles(pe, late.pop(0), i, seg["adas"])
                                continue
                            H, L, k0 = x["rhs"]
                            for un in x["units"]:
                                m, r = un["m"], un["r"]
                                t0, nt = x["ranges"][r]
                                if r == 0:
                                    turn_wait(pe, SW["w_lo"], x["half"] + m + 1, i, seg["halves"])
                                if un["reuses"] is not None:
                                    k_, v = un["reuses"]
                                    turn_wait(pe, F[k_], v + 1, i, seg["kinds"][k_])
                                for k in range(x["kt"]):
                                    if "k" in x["hooks"]:
                                        x["hooks"]["k"](pe, i, k, r)
                                    h, l = H[:, k0 + k, t0:t0 + nt], L[:, k0 + k, t0:t0 + nt]
                                    o = ps[:, un["bank"], 0:nt]
                                    pe.matmul(o, w_hi[m][:, k, :], h, start=(k == 0), stop=False)
                                    pe.matmul(o, w_hi[m][:, k, :], l, start=False, stop=False)
                                    ins = pe.matmul(o, w_lo[m][:, k, :], h, start=False, stop=(k == x["kt"] - 1))
                                ins.then_inc(mm_done, 1)
                                while late:
                                    ada_tiles(pe, late.pop(0), i, seg["adas"])
                        assert not late
                    run(pe, body)
                    if "pe" in after_of:
                        after_of["pe"](pe)

                @block.scalar
                def _(act):
                    x = next(x for x in segs[0]["items"] if "n" in x)
                    for m in range(2):
                        high(act, x, None, segs[0], m)
                    norm.act(act)

                    def body(s, seg, i):
                        for pos, x in enumerate(seg["items"]):
                            if "ada" in x:
                                ada_take(act, x["ada"][0], x["ada"][2], i, seg["adas"], seg["sig"])
                                continue
                            nxt = next_w(s, seg, pos, i)
                            for m in range(2):
                                if nxt is not None:
                                    high(act, *nxt, m)
                                if "act_half" in x["hooks"]:
                                    x["hooks"]["act_half"](act, i, m)
                                takes(act, "act", x, i, seg, m)
                    run(act, body)
                    if "act" in after_of:
                        after_of["act"](act)

                @block.gpsimd
                def _(pool):
                    x = next(x for x in segs[0]["items"] if "n" in x)
                    for m in range(2):
                        low(pool, x, None, segs[0], m)
                    norm.pool(pool)
                    if "pool_start" in after_of:
                        after_of["pool_start"](pool)

                    def body(s, seg, i):
                        for pos, x in enumerate(seg["items"]):
                            if "ada" in x:
                                continue
                            nxt = next_w(s, seg, pos, i)
                            for m in range(2):
                                if nxt is not None:
                                    low(pool, *nxt, m)
                                if "pool_half" in x["hooks"]:
                                    x["hooks"]["pool_half"](pool, i, m)
                    run(pool, body)
                    if "pool" in after_of:
                        after_of["pool"](pool)

                @block.vector
                def _(dve):
                    norm.dve(dve)

                    def body(s, seg, i):
                        for x in seg["items"]:
                            if "ada" in x:
                                continue
                            for m in range(2):
                                takes(dve, "dve", x, i, seg, m)
                                if "dve_half" in x["hooks"]:
                                    x["hooks"]["dve_half"](dve, i, m)
                    run(dve, body)
                    if after is not None:
                        after(dve)
            for name in ("w_hi", "w_lo"):
                SW[name].close(half)
            for k, t in F.items():
                t.close(kinds[k])
            norm.close()

        n_small, dve_abs = [0], [0, 0]

        COL = {}
        col_rows = []

        def param(name, rows_ap):
            COL[name] = sum(x.shape[0] for x in col_rows)
            col_rows.append(rows_ap)

        vec = lambda a: a.rearrange("(n p) -> n p", p=P)
        param("c", vec(w["c"][0]))
        param("c_ctx", vec(w["c_ctx"]))
        param("c2", vec(w["c_2"][0]))
        param("c_ctx2", vec(w["c_ctx_2"]))
        param("b_ada", vec(w["b_ada"][0]))
        param("b_ada2_0", vec(w["ada_b_2"][0]))
        param("b_ada2_1", vec(w["ada_b_2"][1]))
        for l in range(2):
            param(f"norm1_{l}", vec(w["norm1_g_2"][l]))
            param(f"norm2_{l}", vec(w["norm2_g_2"][l]))
        for n in ("ln1_g", "ln1_b", "ln2_g", "ln2_b"):
            param(n, vec(w[n][0]))
        param("conv_w", w["ssd_conv_w"][0].rearrange("t (n p) -> (t n) p", p=P))
        param("conv_b", vec(w["ssd_conv_b"][0]))
        param("ssd_norm", vec(w["ssd_norm_w"][0]))
        param("pool_scale", vec(w["pool_scale"][0]))
        param("ffn_w", w["ffn_conv_w"][0].rearrange("a b (n p) -> (a b n) p", p=P))
        param("ffn_b", vec(w["ffn_conv_b"][0]))
        param("mlstm_norm", vec(w["mlstm_norm_g_2"][0]))
        param("c_q_norm", w["c_q_norm_g_2"])
        param("c_k_norm", w["c_k_norm_g_2"])
        COL["swa_q"] = sum(x.shape[0] for x in col_rows)
        COL["swa_k"] = COL["swa_q"] + 1
        n_rows = COL["swa_k"] + 1
        assert n_rows <= 768
        n_lots = (n_rows + P - 1) // P
        tok_in = big[:, 0:NCH * D].rearrange("p (c d) -> p c d", c=NCH)
        row_in = big[:, NCH * D:NCH * D + 768].rearrange("p (g f) -> p g f", f=P)
        ctx2_in = big[:, 8192:8192 + NCTX * D].rearrange("p (c d) -> p c d", c=NCTX)
        d_in = big[0:4, 12288:12288 + P]
        DT_B, A_ROW, GATE_B, SINK = 0, 16, 32, 48

        groups = []
        for g in range(n_lots):
            n = min(P, n_rows - g * P)
            groups.append(([row_in[0:n, g, :]], cols[:, g * P:g * P + n]))
        for k in range(KT):
            groups.append(([tok_in[:, c, k * P:(k + 1) * P] for c in range(NLAT)], xT[:, k, 0:LAT]))
            groups.append(([tok_in[:, NLAT + c, k * P:(k + 1) * P] for c in range(NCTX)], xT[:, k, LAT:TOK]))
        groups.append(([d_in], dskip[:, :]))
        with nc.Block() as block:
            @block.sync
            def _(sp):
                n_loads = 0

                def load(dst, src):
                    nonlocal n_loads
                    sp.dma_start(dst, src).then_inc(loaded.sem, 16)
                    n_loads += 1
                load(mats[:, :, :], w["const_mats"].rearrange("n p q -> p n q"))
                for (name, _), ap in zip(list(COL.items()), col_rows):
                    at0, n, r = COL[name], ap.shape[0], 0
                    while r < n:
                        g, p0 = divmod(at0 + r, P)
                        m = min(n - r, P - p0)
                        load(row_in[p0:p0 + m, g, :], ap[r:r + m, :])
                        r += m
                for name, src in (("swa_q", w["swa_q_norm_g_2"]), ("swa_k", w["swa_k_norm_g_2"])):
                    g, p0 = divmod(COL[name], P)
                    for half in range(2):
                        load(row_in[p0:p0 + 1, g, half * 64:half * 64 + 64], src)
                load(tok_in[:, 0:NLAT, :], w["x"][0].rearrange("(c p) d -> p c d", p=P))
                load(tok_in[:, NLAT:NCH, :], w["ctx"][0].rearrange("(c p) d -> p c d", p=P))
                load(small[0:4, 0:2], w["ssd_d"][0].rearrange("(t h) -> t h", h=2))
                for dst, src in ((DT_B, w["ssd_dt_bias"][0].rearrange("a h -> (a h)")),
                                 (A_ROW, w["ssd_a_log"][0].rearrange("a h -> (a h)")),
                                 (GATE_B, w["ab_gate_b_2"][0]), (SINK, w["swa_sink_2"][0])):
                    load(rows[:, dst:dst + src.shape[0]], src.partition_broadcast(P))
                load_slabs(sp, NS)
                n_small[0] = n_loads
            @block.vector
            def _(dve):
                dve.wait_ge(loaded.sem, loaded.at(16 * n_small[0]))
                v_order.step(dve, dve.tensor_copy(d_in.rearrange("p (h q) -> p h q", h=2),
                                                  small[0:4, 0:2].unsqueeze(2).to_broadcast([4, 2, 64])))
                transpose_out(dve, groups, 0)

            @block.tensor
            def _(pe):
                pe.wait_ge(loaded.sem, loaded.at(16 * n_small[0]))
                pe.wait_ge(v_order.sem, 1)
                transpose_pe(pe, groups)

            @block.scalar
            def _(act):
                act.wait_ge(loaded.sem, loaded.at(16 * n_small[0]))
                a = rows[:, A_ROW:A_ROW + 16]
                a_order.step(act, act.activation(a, a, ACT.Exp))
                act.activation(a, a, ACT.Copy, scale=-1.0)
                transpose_out(act, groups, 1)
        loaded.close(16 * n_small[0])
        transpose_close(groups)

        named("cleared")
        with nc.Block() as block:
            @block.vector
            def _(dve):
                dve.memset(sil[:, :, :, :], 0.0).then_inc(S["cleared"].sem, 1)

            @block.scalar
            def _(act):
                act.wait_ge(S["cleared"].sem, S["cleared"].at(1))
                for n, (a, b) in enumerate((("c", "c_ctx"), ("c2", "c_ctx2"))):
                    act.activation(sil[:, n, :, 0], cols[:, COL[a]:COL[a] + 8], ACT.Silu)
                    act.activation(sil[:, n, :, 1], cols[:, COL[b]:COL[b] + 8], ACT.Silu)

        S["cleared"].close(1)
        ada_stage(0, W["ada"], 8, 0, COL["b_ada"], None)
        LP, CP = LAT + 2, CTX + 2
        xbc_pad = big[:, 0:8 * (LP + CP)].rearrange("p (t n) -> p t n", t=8)
        o = 8 * (LP + CP)
        xbc = big[:, o:o + 8 * TOK].rearrange("p (t n) -> p t n", t=8)
        o += 8 * TOK
        zT = big[:, o:o + 4 * LAT].rearrange("p (t n) -> p t n", t=4)
        o += 4 * LAT
        fT = big[:, o:o + 2 * LAT].rearrange("p (t n) -> p t n", t=2)
        o += 2 * LAT
        PP = LAT + 16
        poolT = big[:, o:o + 2 * PP].rearrange("p (t n) -> p t n", t=2)
        o += 2 * PP
        x_tok = big[:, o:o + NCH * 512].rearrange("p (c n) -> p c n", c=NCH)
        o += NCH * 512
        b_tok = big[:, o:o + NCH * 256].rearrange("p (c n) -> p c n", c=NCH)
        o += NCH * 256
        yT = big[:, o:o + 4 * LAT].rearrange("p (t n) -> p t n", t=4)
        o += 4 * LAT
        assert o <= 24576

        units = []
        for s in range(4):
            us = []
            for m in range(2):
                t = 2 * s + m
                us.append(("tile", m, 0, LAT, xbc_pad[:, t, 1:1 + LAT], None))
                if t < 6:
                    us.append(("tile", m, LAT, CTX, xbc_pad[:, t, LP + 1:LP + 1 + CTX], None))
            units.append(us)
        for s in range(2):
            units.append([("tile", m, 0, LAT, zT[:, 2 * s + m, :], None) for m in range(2)])
        units.append([("tile", m, 0, LAT, fT[:, m, :], None) for m in range(2)])
        units.append([("tile", m, 0, LAT, poolT[:, m, 8:8 + LAT], None) for m in range(2)])
        conv_units = [(t, p0, n, t0) for t in range(N_CONV) for p0, n, t0 in ((0, LAT, 0), (LP, CTX, LAT))
                      if t < 6 or t0 == 0]
        named("conv_done")

        def convolve(dve):
            for s in range(4):
                mine = [(u, x) for u, x in enumerate(conv_units) if x[0] // 2 == s]
                marks = {}
                for tap in range(3):
                    for u, (t, p0, n, t0) in mine:
                        wcol = cols[:, COL["conv_w"] + tap * 8 + t:COL["conv_w"] + tap * 8 + t + 1]
                        src, dst = xbc_pad[:, t, p0 + tap:p0 + tap + n], xbc[:, t, t0:t0 + n]
                        if tap == 0:
                            dve.wait_ge(mm_free.sem, mm_free.at(u + 1))
                            b = cols[:, COL["conv_b"] + t:COL["conv_b"] + t + 1]
                            marks[u] = v_order.mark(dve.tensor_scalar(dst, src, wcol, b, ALU.mult, ALU.add))
                            continue
                        dve.wait_ge(v_order.sem, marks[u])
                        ins = dve.scalar_tensor_tensor(dst, src, wcol, dst, ALU.mult, ALU.add)
                        if tap == 1:
                            marks[u] = v_order.mark(ins)
                        else:
                            ins.then_inc(S["conv_done"].sem, 1)

        def silu_of_conv(act):
            for u, (t, _, n, t0) in enumerate(conv_units):
                act.wait_ge(S["conv_done"].sem, S["conv_done"].at(u + 1))
                act.activation(xbc[:, t, t0:t0 + n], xbc[:, t, t0:t0 + n], ACT.Silu)

        units_stage(W["in"], units, modulated(0, True, xT, hT, BOTH), w["w_in"][0, :, OFF_DT:OFF_DT + 16],
                    rows[:, DT_B:DT_B + 16], [(xbc_pad, 0.0), (poolT, 0.0)], (0, 0, COL["b_ada"], 8),
                    convolve, silu_of_conv)
        S["conv_done"].close(len(conv_units))

        n16 = NCH * 16
        sm = lambda i: small[:, i * n16:(i + 1) * n16]
        dt, dA, t_a, t_b, t_c = (sm(i) for i in range(5))
        named("exp_ln")
        with nc.Block() as block:
            @block.vector
            def _(dve):
                v_order.step(dve, dve.scalar_tensor_tensor(t_a, dt, -1.0, dt, ALU.mult, ALU.max))
                dve_abs[0] = v_order.n
                dve.wait_ge(S["exp_ln"].sem, S["exp_ln"].at(1))
                v_order.step(dve, dve.tensor_scalar(t_b, t_a, 1.0, None, ALU.add))
                dve_abs[1] = v_order.n
                v_order.step(dve, dve.tensor_scalar(dA, t_b, -1.0, None, ALU.add))
                dve.wait_ge(S["exp_ln"].sem, S["exp_ln"].at(2))
                v_order.step(dve, dve.tensor_scalar(t_b, dA, 0.0, None, ALU.is_equal))
                v_order.step(dve, dve.tensor_tensor(t_c, t_c, t_b, ALU.add))
                v_order.step(dve, dve.tensor_tensor(dA, dA, t_b, ALU.add))
                v_order.step(dve, dve.reciprocal(dA, dA))
                v_order.step(dve, dve.tensor_tensor(t_c, t_c, dA, ALU.mult))
                v_order.step(dve, dve.tensor_tensor(t_c, t_c, t_a, ALU.mult))
                v_order.step(dve, dve.scalar_tensor_tensor(dt, dt, 0.0, t_c, ALU.max, ALU.add))
                a_rows = rows[:, A_ROW:A_ROW + 16].unsqueeze(1).to_broadcast([P, NCH, 16])
                dve.tensor_tensor(dA.rearrange("p (c n) -> p c n", n=16), dt.rearrange("p (c n) -> p c n", n=16),
                                  a_rows, ALU.mult)

            @block.scalar
            def _(act):
                act.wait_ge(v_order.sem, dve_abs[0])
                act.activation(t_a, t_a, ACT.Exp, scale=-1.0).then_inc(S["exp_ln"].sem, 1)
                act.wait_ge(v_order.sem, dve_abs[1])
                act.activation(t_c, t_b, ACT.Ln).then_inc(S["exp_ln"].sem, 1)
        S["exp_ln"].close(2)
        tmp = big[:, 0:8 * (LP + CP)]
        Gs = tmp[:, 0:8 * P].rearrange("p (c g n) -> p c g n", c=NLAT, g=2)
        state = tmp[:, 1024:2048].rearrange("p (d g n) -> p d g n", d=2, g=2)
        xd = tmp[:, 2048:3072].rearrange("p (b k n) -> p b k n", b=2, k=2)
        seg = tmp[:, 3072:4096].rearrange("p (b h n) -> p b h n", b=2, h=4)
        lmat = tmp[:, 4096:5120].rearrange("p (b h n) -> p b h n", b=2, h=4)
        e_row = tmp[:, 5120:6144].rearrange("p (b h n) -> p b h n", b=2, h=4)
        c_dec = squares[:, 0:2, :].rearrange("p b (h n) -> p b h n", h=4)
        g_mask = mean[:, 0:256].rearrange("p (b n) -> p b n", b=2)
        neg_cs, e_tot, decay = t_a, t_b, t_c
        by_chunk = lambda a: a.rearrange("p (c n) -> p c n", n=16)
        groups = []
        for c in range(NCH):
            t0 = c * CH
            groups.append(([xbc[:, t, t0:t0 + CH] for t in range(4)], x_tok[:, c, :]))
            groups.append(([xbc[:, 4 + g, t0:t0 + CH] for g in range(2)], b_tok[:, c, :]))
        with nc.Block() as block:
            @block.tensor
            def _(pe):
                transpose_pe(pe, groups)

            @block.vector
            def _(dve):
                transpose_out(dve, groups, 0)

            @block.scalar
            def _(act):
                transpose_out(act, groups, 1)
        transpose_close(groups)
        named("cs", "cb", "log_decay")
        with nc.Block() as block:
            @block.tensor
            def _(pe):
                for c in range(NCH):
                    for d, tri in enumerate((U_LE, U_GE)):
                        o = c * 16 + d * 8
                        pe.matmul(ps[:, 0, o:o + 8], mats[:, tri, :], dA[:, o:o + 8], start=True, stop=True)
                pe.matmul(ps[:, 1, 0:n16], ones, dA, start=True, stop=True).then_inc(S["cs"].sem, 1)
                for c in range(NLAT):
                    for g in range(2):
                        u = c * 2 + g
                        pe.matmul(ps[:, 2 + u // 4, (u % 4) * P:(u % 4 + 1) * P],
                                  xbc[:, 4 + g, c * CH:(c + 1) * CH], xbc[:, 6 + g, c * CH:(c + 1) * CH],
                                  start=True, stop=True).then_inc(S["cb"].sem, 1)

            @block.vector
            def _(dve):
                dve.wait_ge(S["cs"].sem, S["cs"].at(1))
                v_order.step(dve, dve.tensor_scalar(neg_cs, ps[:, 0, 0:n16], -1.0, None, ALU.mult))
                dve.tensor_tensor(decay, ps[:, 1, 0:n16], neg_cs, ALU.add).then_inc(S["log_decay"].sem, 1)
                dve.memset(tmp[:, 1024:2048], 0.0)

            @block.scalar
            def _(act):
                act.wait_ge(S["log_decay"].sem, S["log_decay"].at(1))
                act.activation(e_tot, ps[:, 1, 0:n16], ACT.Exp)
                act.activation(decay, decay, ACT.Exp)
                for q in range(2):
                    act.wait_ge(S["cb"].sem, S["cb"].at(4 * (q + 1)))
                    act.activation(tmp[:, q * 512:(q + 1) * 512], ps[:, 2 + q, :], ACT.Copy)
        S["cs"].close(1)
        S["cb"].close(8)
        S["log_decay"].close(1)

        order_of = [[4, 5, 0, 1, 2, 3], [5, 4, 3, 2, 1, 0]]
        steps = [(d, order_of[d][k], g, k) for k in range(NCH) for d in range(2) for g in range(2)]
        outs = [s for s, (_, _, _, k) in enumerate(steps) if k >= NCTX]
        ups = [s for s, (_, _, _, k) in enumerate(steps) if k < NCH - 1]
        upto = lambda lst, s: sum(1 for x in lst if x < s)
        heads = lambda a, d, c, g: by_chunk(a)[:, c, d * 8 + g * 4:d * 8 + g * 4 + 4]
        R = named("xdt", "bc", "seg", "lmat", "erow", "m", "cdec", "y", "y_out", "ds", "state")
        sig = lambda ins, n: ins.then_inc(R[n].sem, 1)
        wait = lambda eng, n, v: eng.wait_ge(R[n].sem, R[n].at(v))

        with nc.Block() as block:
            @block.gpsimd
            def _(pool):
                for s, (d, c, g, k) in enumerate(steps):
                    b = s % 2
                    if s >= 2:
                        if s - 2 in ups:
                            wait(pool, "ds", upto(ups, s - 1))
                        if s - 2 in outs:
                            wait(pool, "y", upto(outs, s - 1))
                    x3 = x_tok[:, c, g * 256:(g + 1) * 256].rearrange("p (h q) -> p h q", h=4)
                    v = [xd[:, b, j, :].rearrange("p (h q) -> p h q", h=4) for j in range(2)]
                    g_order.step(pool, pool.tensor_tensor(
                        v[0], x3, heads(dt, d, c, g).unsqueeze(2).to_broadcast([P, 4, 64]), ALU.mult))
                    sig(pool.tensor_tensor(
                        v[1], v[0], heads(decay, d, c, g).unsqueeze(2).to_broadcast([P, 4, 64]), ALU.mult), "xdt")
                    if s in outs:
                        i = outs.index(s)
                        wait(pool, "erow", i + 1)
                        if i >= 2:
                            wait(pool, "y", i - 1)
                        cT = xbc[:, 6 + g, c * CH:(c + 1) * CH].unsqueeze(1).to_broadcast([P, 4, CH])
                        sig(pool.tensor_tensor(c_dec[:, i % 2, :, :], e_row[:, i % 2, :, :], cT, ALU.mult), "cdec")

            @block.tensor
            def _(pe):
                def rows_of_cs(i):
                    d, c, g, _ = steps[outs[i]]
                    if i >= 2:
                        wait(pe, "seg", i - 1)
                        wait(pe, "erow", i - 1)
                    for h in range(4):
                        col = heads(dA, d, c, g)[:, h:h + 1]
                        ins = pe.matmul(ps[:, i % 2, h * P:(h + 1) * P], col.to_broadcast([P, P]),
                                        mats[:, (U_LE, U_GE)[d], :], start=True, stop=True)
                    sig(ins, "bc")

                rows_of_cs(0)
                for s, (d, c, g, k) in enumerate(steps):
                    wait(pe, "xdt", s + 1)
                    if s in ups:
                        i = ups.index(s)
                        if i >= 2:
                            wait(pe, "state", i - 1)
                        sig(pe.matmul(ps[:, 4 + i % 2, 0:256], b_tok[:, c, g * P:(g + 1) * P], xd[:, s % 2, 1, :],
                                      start=True, stop=True), "ds")
                    if s in outs:
                        i = outs.index(s)
                        if i + 1 < len(outs):
                            rows_of_cs(i + 1)
                        wait(pe, "m", i + 1)
                        wait(pe, "cdec", i + 1)
                        wait(pe, "state", upto(ups, s - 3))
                        if i >= 2:
                            wait(pe, "y_out", i - 1)
                        for h in range(4):
                            o = ps[64 * (h % 2):64 * (h % 2) + 64, 2 + i % 2, (h // 2) * P:(h // 2 + 1) * P]
                            pe.matmul(o, xd[:, s % 2, 0, h * 64:(h + 1) * 64], lmat[:, i % 2, h, :],
                                      start=True, stop=False, skip_group_check=True)
                            ins = pe.matmul(o, state[:, d, g, h * 64:(h + 1) * 64], c_dec[:, i % 2, h, :],
                                            start=False, stop=True, skip_group_check=True)
                        sig(ins, "y")

            @block.vector
            def _(dve):
                def finish(s):
                    d, c, g, k = steps[s]
                    if s in outs:
                        i = outs.index(s)
                        wait(dve, "y", i + 1)
                        dst = yT[:, 2 * g:2 * g + 2, c * CH:(c + 1) * CH]
                        src = ps[:, 2 + i % 2, 0:2 * P].rearrange("p (t n) -> p t n", t=2)
                        if k < NCTX + NLAT // 2:
                            sig(dve.tensor_copy(dst, src), "y_out")
                        else:
                            wait(dve, "y_out", i - 1)
                            sig(dve.tensor_tensor(dst, src, dst, ALU.add), "y_out")
                    if s in ups:
                        i = ups.index(s)
                        st = state[:, d, g, :]
                        st3 = st.rearrange("p (h q) -> p h q", h=4)
                        wait(dve, "ds", i + 1)
                        if i >= 4:
                            wait(dve, "state", i - 3)
                        v_order.step(dve, dve.tensor_tensor(
                            st3, st3, heads(e_tot, d, c, g).unsqueeze(2).to_broadcast([P, 4, 64]), ALU.mult))
                        sig(dve.tensor_tensor(st, ps[:, 4 + i % 2, 0:256], st, ALU.add), "state")

                for s, (d, c, g, k) in enumerate(steps):
                    if s in outs:
                        i = outs.index(s)
                        b = i % 2
                        wait(dve, "erow", i + 1)
                        if i >= 2:
                            wait(dve, "lmat", i - 1)
                        for h in range(4):
                            ins = dve.tensor_scalar(seg[:, b, h, :], ps[:, b, h * P:(h + 1) * P],
                                                    heads(neg_cs, d, c, g)[:, h:h + 1], 0.0, ALU.add, ALU.min)
                        sig(ins, "seg")
                        if i >= 2:
                            wait(dve, "m", i - 1)
                        v_order.step(dve, dve.tensor_tensor(g_mask[:, b, :], Gs[:, c, g, :],
                                                            mats[:, (U_LE, U_GE)[d], :], ALU.mult))
                    if s >= 1:
                        finish(s - 1)
                    if s in outs:
                        wait(dve, "lmat", i + 1)
                        sig(dve.tensor_tensor(lmat[:, b, :, :], lmat[:, b, :, :],
                                              g_mask[:, b, :].unsqueeze(1).to_broadcast([P, 4, P]), ALU.mult), "m")
                finish(len(steps) - 1)

            @block.scalar
            def _(act):
                for i in range(len(outs)):
                    b = i % 2
                    wait(act, "bc", i + 1)
                    if i >= 2:
                        wait(act, "cdec", i - 1)
                    sig(act.activation(e_row[:, b, :, :].rearrange("p h n -> p (h n)"), ps[:, b, :], ACT.Exp), "erow")
                    wait(act, "seg", i + 1)
                    if i >= 2:
                        wait(act, "y", i - 1)
                    sig(act.activation(lmat[:, b, :, :], seg[:, b, :, :], ACT.Exp), "lmat")
        for n in ("bc", "seg", "lmat", "erow", "m", "cdec", "y", "y_out"):
            R[n].close(len(outs))
        R["xdt"].close(len(steps))
        R["ds"].close(len(ups))
        R["state"].close(len(ups))

        dft = big[:, 0:4096].rearrange("p (a k n) -> p a k n", a=2, k=NLAT)
        w4 = small[:, :].rearrange("p (a n) -> p a n", a=4)
        W12 = tmp[:, 4096:4608].rearrange("p (t n) -> p t n", t=2)
        f_tok = tmp[:, 4608:5632].rearrange("p (c n) -> p c n", c=NLAT)
        cnt = x_tok.rearrange("p c n -> p (c n)")[:, 0:1024].rearrange("p (t n) -> p t n", t=2)
        sums = xbc.rearrange("p t n -> p (t n)")[:, 3072:3072 + 4 * PP].rearrange("p (t s n) -> p t s n", t=2, s=2)
        pooled = x_tok.rearrange("p c n -> p (c n)")[:, 1024:2048].rearrange("p (t n) -> p t n", t=2)
        gated = b_tok.rearrange("p c n -> p (c n)")[:, 0:1024].rearrange("p (t n) -> p t n", t=2)
        R = named("zero", "silu", "y", "sq", "var", "std", "w12", "w12_out", "ftok", "ftok_out", "dft", "pooled", "pool")
        with nc.Block() as block:
            @block.gpsimd
            def _(pool):
                sig(pool.memset(small[:, :], 0.0), "zero")
                sig(pool.memset(sums, 0.0), "zero")

            @block.sync
            def _(sp):
                wait(sp, "zero", 1)
                for a, name in enumerate(("fnet_w", "pool_w")):
                    for g in range(4):
                        h = 64 * (g % 2)
                        sp.dma_start(w4[h:h + 64, 2 * a + g // 2, h:h + 64], w[name][0, g]).then_inc(loaded.sem, 16)
                sp.dma_start(cnt, w["const_tables"][T_CNT:T_CNT + 2].rearrange("t p n -> p t n"))\
                  .then_inc(loaded.sem, 16)
                for a in range(2):
                    sp.dma_start(dft[:, a, :, :], w["const_dft"][a].rearrange("(k p) n -> p k n", p=P))\
                      .then_inc(loaded.sem, 16)

            @block.scalar
            def _(act):
                for t in range(4):
                    sig(act.activation(zT[:, t, :], zT[:, t, :], ACT.Silu), "silu")
                for t in range(4):
                    wait(act, "y", t + 1)
                    if t >= 3:
                        wait(act, "var", t - 2)
                    sig(act.activation(squares[:, t % 3, :], yT[:, t, :], ACT.Square), "sq")
                wait(act, "w12", 4)
                for t in range(2):
                    sig(act.activation(W12[:, t, :], ps[:, 2, t * 256:(t + 1) * 256], ACT.Copy), "w12_out")
                for t in range(2):
                    for c in range(NLAT):
                        u = t * NLAT + c
                        wait(act, "ftok", 2 * (u // 2 + 1))
                        if u >= NLAT:
                            wait(act, "dft", 1)
                        sig(act.activation(f_tok[:, c, :], ps[:, 3 + (u // 2) % 2, (u % 2) * 256:(u % 2 + 1) * 256],
                                           ACT.Copy), "ftok_out")
                    wait(act, "dft", t + 1)
                    act.activation(hT[:, 4 + t, 0:LAT], ps[:, 5, :], ACT.Copy).then_inc(mm_free.sem, 1)
                for t in range(2):
                    wait(act, "pool", t + 1)
                    sc = cols[:, COL["pool_scale"] + t:COL["pool_scale"] + t + 1]
                    act.activation(hT[:, 6 + t, 0:LAT], ps[:, 6 + t, :], ACT.Copy, scale=sc)
                for g in range(2):
                    wait(act, "var", 2 * g + 2)
                    sig(act.activation(rstd[:, 0:LAT] if g == 0 else mean[:, 0:LAT], ps[:, g, :], ACT.Sqrt,
                                       bias=eps_col, scale=1.0 / 256), "std")

            @block.tensor
            def _(pe):
                for t in range(4):
                    wait(pe, "sq", t + 1)
                    sig(pe.matmul(ps[:, t // 2, :], ones, squares[:, t % 3, :], start=(t % 2 == 0),
                                  stop=(t % 2 == 1)), "var")
                pe.wait_ge(loaded.sem, loaded.at(16 * 11))
                for t in range(2):
                    for a, m in enumerate((DFT_C, DFT_S)):
                        sig(pe.matmul(ps[:, 2, t * 256 + a * P:t * 256 + (a + 1) * P], mats[:, m, :], w4[:, t, :],
                                      start=True, stop=True), "w12")
                for t in range(2):
                    wait(pe, "w12_out", t + 1)
                    for c in range(NLAT):
                        u = t * NLAT + c
                        if u >= NLAT:
                            wait(pe, "ftok_out", u // 2 * 2 - 2)
                        sig(pe.matmul(ps[:, 3 + (u // 2) % 2, (u % 2) * 256:(u % 2 + 1) * 256],
                                      fT[:, t, c * CH:(c + 1) * CH], W12[:, t, :], start=True, stop=True), "ftok")
                    if t == 1:
                        pe.wait_ge(mm_free.sem, mm_free.at(1))
                    for a in range(2):
                        for c in range(NLAT):
                            wait(pe, "ftok_out", t * NLAT + c + 1)
                            ins = pe.matmul(ps[:, 5, :], f_tok[:, c, a * P:(a + 1) * P], dft[:, a, c, :],
                                            start=(a == 0 and c == 0), stop=(a == 1 and c == NLAT - 1))
                    sig(ins, "dft")
                for t in range(2):
                    wait(pe, "pooled", t + 1)
                    sig(pe.matmul(ps[:, 6 + t, :], w4[:, 2 + t, :], pooled[:, t, :], start=True, stop=True), "pool")

            @block.vector
            def _(dve):
                for t in range(4):
                    v_order.step(dve, dve.scalar_tensor_tensor(yT[:, t, :], xbc[:, t, 0:LAT], dskip[:, t:t + 1],
                                                               yT[:, t, :], ALU.mult, ALU.add))
                    wait(dve, "silu", t + 1)
                    sig(dve.tensor_tensor(yT[:, t, :], yT[:, t, :], zT[:, t, :], ALU.mult), "y")
                wait(dve, "zero", 2)
                dve.wait_ge(loaded.sem, loaded.at(16 * 11))
                for t in range(2):
                    src = poolT[:, t, :]
                    for lvl in range(4 if t else 2):
                        dst = sums[:, t, lvl % 2, :]
                        h = 1 if lvl == 0 else 2 ** (lvl - 1)
                        lo, n = 8, LAT
                        if lvl == 0:
                            a, b, e0, e1 = 1, 0, 1, PP
                        else:
                            a, b, e0, e1 = h, h, 2 ** lvl, PP - 2 ** lvl
                        v_order.step(dve, dve.tensor_tensor(dst[:, e0:e1], src[:, e0 - a:e1 - a],
                                                            src[:, e0 + b:e1 + b], ALU.add))
                        part = slice(0, 64) if lvl % 2 == 0 else slice(64, P)
                        if lvl // 2 == t:
                            v_order.step(dve, dve.tensor_tensor(pooled[part, t, :], dst[part, 8:8 + LAT],
                                                                cnt[part, t, :], ALU.mult))
                        src = dst
                    sig(dve.tensor_tensor(pooled[:, t, :], pooled[:, t, :], poolT[:, t, 8:8 + LAT],
                                          ALU.subtract), "pooled")
                for g in range(2):
                    wait(dve, "std", g + 1)
                    r = rstd[:, 0:LAT] if g == 0 else mean[:, 0:LAT]
                    v_order.step(dve, dve.reciprocal(r, r))
                    for t in (2 * g, 2 * g + 1):
                        wn = cols[:, COL["ssd_norm"] + t:COL["ssd_norm"] + t + 1]
                        dve.scalar_tensor_tensor(hT[:, t, 0:LAT], yT[:, t, :], wn, r, ALU.mult, ALU.mult)
        for n, v in (("zero", 2), ("silu", 4), ("y", 4), ("sq", 4), ("var", 4), ("std", 2), ("w12", 4), ("w12_out", 2),
                     ("ftok", 8), ("ftok_out", 8), ("dft", 2), ("pooled", 2), ("pool", 2)):
            R[n].close(v)
        loaded.close(16 * 11)
        mm_free.close(2)

        def add_gated(gate):
            lay = cur[0]

            def take(t, r, bank):
                x = tile_of(xT, t, TOK, BOTH[r][0], BOTH[r][1])
                gates = mods[:, lay, :, :].rearrange("p m c -> p (m c)")
                return nc.vector.scalar_tensor_tensor(x, bank, column_of(gates, t * 2 + 2 * gate + r), x,
                                                      ALU.mult, ALU.add)
            return take

        def alpha_x(dve):
            for k in range(KT):
                v_order.step(dve, dve.tensor_scalar(xT[:, k, 0:LAT], xT[:, k, 0:LAT], ALPHA, None, ALU.mult))

        def post_norm(g, b):
            norm_stage(Norm(True, ONLY_LAT, xT, xT, lambda k, r: cols[:, COL[g] + k:COL[g] + k + 1],
                            lambda k, r: cols[:, COL[b] + k:COL[b] + k + 1]))

        def output_projection(name, ranges, more=None):
            stage.close()
            with ExitStack() as scope:
                def parts(what, tiles, n):
                    return [sb(f"{name}_{what}_{p}", [P, tiles, n], scope, F32R) for p in ("hi", "lo")]
                h_parts = parts("h", KT, sum(r[1] for r in ranges))
                w_parts = list(zip(parts("w0", KT, P), parts("w1", KT, P)))
                halves, gated = Halves(ranges, *h_parts, more), add_gated(16)
                items = []
                for j in range(4):
                    hooks = {"k": lambda pe, i, k, r: halves.ready(pe, r, k)} if j == 0 else {}
                    items.append(("w", W[name] + j, KT, (*h_parts, 0), ranges, "dve",
                                  lambda i, m, r, bank, un, j=j: gated(2 * j + m, r, bank), hooks))
                split_stage(w_parts, [(items, 1)], halves)

        output_projection("out", ONLY_LAT, alpha_x)
        post_norm("ln1_g", "ln1_b")

        mixer.close()
        ffn = ExitStack()
        def ffn_parts(what, tiles, n):
            return [sb(f"ffn_{what}_{p}", [P, tiles, n], ffn, F32R) for p in ("hi", "lo")]
        h_parts = ffn_parts("h", KT, LAT)
        ffn_w = list(zip(ffn_parts("w0", KT, P), ffn_parts("w1", KT, P)))
        act_ff = sb("act_ff", [P, FT, LAT], ffn)
        GRID = (GRID_H + 2) * (GRID_W + 2)
        gate_bufs = sb("gate_bufs", [P, 4, LAT], ffn)
        grid_mem = sb("grid", [P, 4, GRID], ffn)
        h_all = sb("ffn_h", [P, 4, LAT], ffn)
        sq = squares[:, :, :].rearrange("p a n -> p (a n)")
        grids = [g.rearrange("p (h w) -> p h w", w=GRID_W + 2) for g in
                 [grid_mem[:, b, :] for b in range(4)] + [sq[:, 0:GRID], sq[:, GRID:2 * GRID], mean[:, 0:GRID],
                                                          rstd[:, 0:GRID]]]
        R = named("zero", "conv", "gelu", "ff", "alpha")
        ada_first[0] = 0
        CW = COL["ffn_w"]
        CENTRE = 4
        TAPS = [t for t in range(9) if t != CENTRE]
        PER_STEP = 4 * (len(TAPS) - 1)
        DOWN_BANKS = (4, 0, 1, 2, 3, 6, 7, 5)
        gated = add_gated(40)
        v_base = v_order.n
        norm = modulated(1, True, xT, None, ONLY_LAT, (*h_parts, h_all))

        def unit_tile(i, j, q):
            return at(i, 4, 2 * j + q % 2) + (FT if q >= 2 else 0)

        def unit_sum(i, j, q):
            if q < 2:
                return tile_of(act_ff, at(i, 4, 2 * j + q), LAT)
            return gate_bufs[:, 2 * (j % 2) + q - 2, :]

        on_grid = lambda a: a.rearrange("p (h w) -> p h w", w=GRID_W)

        def take_up(j, half):
            def take(i, m, r, bank, un):
                q = 2 * half + m
                u, tile = 4 * j + q, unit_tile(i, j, q)
                if half == 0 and m == 0 and j < 2 and i is None:
                    wait(nc.scalar, "zero", j + 1)
                if u >= 8 or i is not None:
                    turn_wait(nc.scalar, R["conv"], u - 7, i, 8)
                    if half:
                        turn_wait(nc.scalar, R["ff"], 2 * j - 2, i, 4)
                nc.scalar.activation(grids[u % 8][:, 1:1 + GRID_H, 1:1 + GRID_W], on_grid(bank), ACT.Copy)
                return nc.scalar.activation(unit_sum(i, j, q), bank, ACT.Identity,
                                            scale=column_of(cols, tile + (CW + CENTRE * 2 * FT)),
                                            bias=column_of(cols, tile + COL["ffn_b"]))
            return take

        def convolve_step(dve, i, j):
            for tap_no, tap in enumerate(TAPS):
                dy, dx = divmod(tap, 3)
                for q in range(4):
                    u = 4 * j + q
                    dst = on_grid(unit_sum(i, j, q))
                    mine = v_base + j * PER_STEP + tap_no * 4 + q + 1
                    if tap_no == 0:
                        turn_wait(dve, mm_free, u + 1, i, 8)
                    else:
                        dve.wait_ge(v_order.sem, val(mine - 4, i, 2 * PER_STEP))
                    ins = dve.scalar_tensor_tensor(dst, grids[u % 8][:, dy:dy + GRID_H, dx:dx + GRID_W],
                                                   column_of(cols, unit_tile(i, j, q) + (CW + tap * 2 * FT)), dst,
                                                   ALU.mult, ALU.add)
                    if tap_no < len(TAPS) - 1:
                        ins.then_inc(v_order.sem, 1)
                    else:
                        sig(ins, "conv")

        def gelus(act, i, j):
            for m in range(2):
                turn_wait(act, R["conv"], 4 * j + 2 + m + 1, i, 8)
                g = gate_bufs[:, 2 * (j % 2) + m, :]
                sig(act.activation(g, g, ACT.Gelu_apprx_tanh), "gelu")

        def products(pool, i, j):
            for m in range(2):
                turn_wait(pool, R["gelu"], 2 * j + m + 1, i, 4)
                v = tile_of(act_ff, at(i, 4, 2 * j + m), LAT)
                sig(pool.tensor_tensor(v, v, gate_bufs[:, 2 * (j % 2) + m, :], ALU.mult), "ff")

        def gate_hooks(j):
            hooks = {"dve_half": lambda dve, i, m: convolve_step(dve, i, j) if m else None}
            if j:
                hooks["act_half"] = lambda act, i, m: gelus(act, i, j - 1) if m else None
                hooks["pool_half"] = lambda pool, i, m: products(pool, i, j - 1) if m else None
            return hooks

        def step_items(j):
            n, last = W["up"] + 4 * j, j == FT // 2 - 1
            first = {"k": lambda pe, i, k, r: norm.ready(pe, r, k)} if j == 0 else {}
            adas = 4 if last else 2
            return [("w", n, KT, (*h_parts, 0), ONLY_LAT, "act", take_up(j, 0), first)] + \
                   [("ada", n + 1 + a, 1, 2 * j + a) for a in range(adas)] + \
                   [("w", n + 1 + adas, KT, (*h_parts, 0), ONLY_LAT, "act", take_up(j, 1), gate_hooks(j))]

        def zero_grids(pool):
            sig(pool.memset(grid_mem[:, :, :], 0.0), "zero")
            for a in (sq[:, 0:2 * GRID], mean[:, 0:GRID], rstd[:, 0:GRID]):
                ins = pool.memset(a, 0.0)
            sig(ins, "zero")

        def down_products(pe):
            pe.wait_ge(mm_free.sem, mm_free.at(2 * FT))
            for g, (_, kt) in enumerate(DOWN_ROWS):
                for c in range(4):
                    n = W["down"] + 4 * g + c
                    wait_slab(pe, n)
                    for m in range(2):
                        bank = DOWN_BANKS[2 * c + m]
                        if g == 0 and bank == 5:
                            wait(pe, "alpha", 1)
                        for k in range(kt):
                            if c == 0 and m == 0:
                                wait(pe, "ff", g * KT + k + 1)
                            ins = pe.matmul(ps[:, bank, :], ring[:, n % NS, k, m * P:(m + 1) * P],
                                            act_ff[:, g * KT + k, :], start=(g == 0 and k == 0),
                                            stop=(g == len(DOWN_ROWS) - 1 and k == kt - 1))
                        ins.then_inc(mm_done, 1)

        def down_takes(dve):
            ada_finish(dve, 1, 0, 24, COL["b_ada2_0"], (COL["norm1_0"], COL["norm2_0"]))
            for k in range(KT):
                sig(dve.tensor_scalar(xT[:, k, 0:LAT], xT[:, k, 0:LAT], ALPHA, None, ALU.mult), "alpha")
            wait(dve, "alpha", KT)
            for t, bank in enumerate(DOWN_BANKS):
                dve.wait_ge(mm_done, signals[W["down"] + 8 + t // 2] + t % 2 + 1)
                gated(t, 0, ps[:, bank, :])

        LAST = FT // 2 - 1
        v_order.n += (LAST + 1) * PER_STEP
        split_stage(ffn_w, [(step_items(0) + step_items(1), 1), (step_items(2) + step_items(3), 4),
                            (step_items(LAST), 1)], norm, down_takes,
                    after_of={"pe": down_products, "act": lambda act: gelus(act, None, LAST),
                              "pool": lambda pool: products(pool, None, LAST), "pool_start": zero_grids},
                    until=W["down"] + 12)
        ada_close(24)
        for n, v in (("zero", 2), ("conv", 2 * FT), ("gelu", FT), ("ff", FT), ("alpha", KT)):
            R[n].close(v)
        ffn.close()
        hT, big = sb("hT1", [P, KT, TOK], mixer), own_memory("1")
        post_norm("ln2_g", "ln2_b")
        def mlp_stage(layer, ranges):
            with ExitStack() as scope:
                def parts(name, tiles, n):
                    return [sb(f"{name}_{p}{layer}", [P, tiles, n], scope, F32R) for p in ("hi", "lo")]
                n_tok = sum(r[1] for r in ranges)
                h_parts, m_parts = parts("h", KT, n_tok), parts("hidden", KT, n_tok)
                w_parts = list(zip(parts("w0", KT, P), parts("w1", KT, P)))
                norm = modulated(1, False, xT, None, ranges, (*h_parts, sb(f"h{layer}", [P, 4, LAT], scope)))
                mlp(layer, ranges, norm, h_parts, m_parts, w_parts)

        def mlp(layer, ranges, norm, h_parts, m_parts, w_parts):
            (h_hi, h_lo), (m_hi, m_lo) = h_parts, m_parts
            n_r = len(ranges)
            R = named("m_hi", "m_lo")
            gated = add_gated(40)
            first = W[f"mlp_{layer}"]
            n_u, per_q = 2 * n_r, 8 * n_r
            relus = [squares[:, b, :] for b in range(3)] + [rstd[:, 0:LAT]]
            v_at = v_order.n
            ada_first[0] = 0

            def hidden(q, j, last_w2):
                def relu(i, m, r, bank, un):
                    u = q * per_q + j * n_u + m * n_r + r
                    if u >= 4:
                        turn_wait(nc.scalar, R["m_lo"], u - 3, i, per_q)
                    return nc.scalar.activation(relus[u % 4][:, 0:ranges[r][1]], bank, ACT.Relu)

                def high(dve, i, m):
                    if q and j == 0 and m == 0:
                        v = signals[last_w2]
                        dve.wait_ge(mm_done, val(v, i, signals[last_w2] - signals[last_w2 - (8 if layer else 12)]))
                    for r, (t0, nt) in enumerate(ranges):
                        u = q * per_q + j * n_u + m * n_r + r
                        sq = relus[u % 4][:, 0:nt]
                        turn_wait(dve, mm_free, u + 1, i, per_q)
                        dve.tensor_tensor(sq, sq, sq, ALU.mult).then_inc(v_order.sem, 1)
                        dve.wait_ge(v_order.sem, val(v_at + u + 1, i, per_q))
                        dve.tensor_copy(m_hi[:, 2 * j + m, t0:t0 + nt], sq).then_inc(R["m_hi"].sem, 1)

                def low(pool, i, m):
                    for r, (t0, nt) in enumerate(ranges):
                        u = q * per_q + j * n_u + m * n_r + r
                        turn_wait(pool, R["m_hi"], u + 1, i, per_q)
                        pool.tensor_tensor(m_lo[:, 2 * j + m, t0:t0 + nt], relus[u % 4][:, 0:nt],
                                           m_hi[:, 2 * j + m, t0:t0 + nt].bitcast(F32), ALU.subtract)\
                            .then_inc(R["m_lo"].sem, 1)
                hooks = {"dve_half": high, "pool_half": low}
                if q == 0 and j == 0:
                    hooks["k"] = lambda pe, i, k, r: norm.ready(pe, r, k)
                return relu, hooks

            def back(q, j):
                def take(i, m, r, bank, un):
                    if q:
                        turn_wait(nc.vector, mm_free_v, un["idx"] - per_q + 1, i, per_q)
                    return gated(2 * j + m, r, bank)

                def operand(pe, i, k, r):
                    turn_wait(pe, R["m_lo"], q * per_q + k * n_r + r + 1, i, per_q)
                return take, ({"k": operand} if j == 0 else {})

            segments, n, ada_no = [], first, 0
            for q in range(4):
                items, last_w2 = [], n
                for j in range(4):
                    take, hooks = hidden(q, j, last_w2)
                    items.append(("w", n, KT, (h_hi, h_lo, 0), ranges, "act", take, hooks))
                    n += 1
                    if layer == 0:
                        k = 1 if q else (2, 2, 2, 3)[j]
                        items += [("ada", n + x, 1, ada_no + x) for x in range(k)]
                        n, ada_no = n + k, ada_no + k
                for j in range(4):
                    take, hooks = back(q, j)
                    items.append(("w", n, KT, (m_hi, m_lo, 0), ranges, "dve", take, hooks))
                    n += 1
                    if layer == 0 and q == 0 and j < 3:
                        items.append(("ada", n, 1, ada_no))
                        n, ada_no = n + 1, ada_no + 1
                segments.append((items, 1))
            segments = [segments[0], (segments[1][0], 2), segments[3]]
            after = None
            if layer == 0:
                after = lambda dve: ada_finish(dve, 2, 0, 24, COL["b_ada2_1"], (COL["norm1_1"], COL["norm2_1"]))
            v_order.n += 4 * per_q
            split_stage(w_parts, segments, norm, after)
            R["m_hi"].close(4 * per_q)
            R["m_lo"].close(4 * per_q)
            if layer == 0:
                ada_close(24)

        def head_norms(jobs, load=None):
            R = named("sq", "var", "std")
            temps = [rstd[:, 0:LAT], mean[:, 0:LAT]]
            v_at = v_order.n
            with nc.Block() as block:
                @block.sync
                def _(sp):
                    if load is not None:
                        load(sp)

                @block.tensor
                def _(pe):
                    for u, (src, n, _, hd_mat, hd) in enumerate(jobs):
                        pe.wait_ge(R["sq"].sem, R["sq"].at(u + 1))
                        if u >= 4:
                            pe.wait_ge(R["std"].sem, R["std"].at(u - 3))
                        pe.matmul(ps[:, u % 4, 0:n], hd_mat, squares[:, u % 3, 0:n], start=True, stop=True)\
                          .then_inc(R["var"].sem, 1)

                @block.scalar
                def _(act):
                    def root(u):
                        n, hd = jobs[u][1], jobs[u][4]
                        act.wait_ge(R["var"].sem, R["var"].at(u + 1))
                        if u >= 2:
                            act.wait_ge(v_order.sem, v_at + 2 * (u - 1))
                        act.activation(temps[u % 2][:, 0:n], ps[:, u % 4, 0:n], ACT.Sqrt, bias=eps_col,
                                       scale=1.0 / hd).then_inc(R["std"].sem, 1)
                    for u, (src, n, _, _, _) in enumerate(jobs):
                        if u >= 3:
                            act.wait_ge(R["var"].sem, R["var"].at(u - 2))
                        act.activation(squares[:, u % 3, 0:n], src, ACT.Square).then_inc(R["sq"].sem, 1)
                        if u >= 1:
                            root(u - 1)
                    root(len(jobs) - 1)

                @block.vector
                def _(dve):
                    for u, (src, n, gain, _, _) in enumerate(jobs):
                        t = temps[u % 2][:, 0:n]
                        dve.wait_ge(R["std"].sem, R["std"].at(u + 1))
                        v_order.step(dve, dve.reciprocal(t, t))
                        v_order.mark(dve.scalar_tensor_tensor(src, src, gain, t, ALU.mult, ALU.mult))
            for n in R:
                R[n].close(len(jobs))

        def rope(tiles, rot, cos, sin):
            R = named("rot", "sin")
            with nc.Block() as block:
                @block.tensor
                def _(pe):
                    for u, t in enumerate(tiles):
                        if u >= 4:
                            pe.wait_ge(R["sin"].sem, R["sin"].at(u - 3))
                        pe.matmul(ps[:, u % 4, :], mats[:, rot, :], t, start=True, stop=True)\
                          .then_inc(R["rot"].sem, 1)

                @block.vector
                def _(dve):
                    for u, t in enumerate(tiles):
                        dve.wait_ge(R["rot"].sem, R["rot"].at(u + 1))
                        v_order.step(dve, dve.tensor_tensor(t, t, cos, ALU.mult))
                        ins = dve.tensor_tensor(squares[:, u % 3, :], ps[:, u % 4, :], sin, ALU.mult)
                        ins.then_inc(R["sin"].sem, 1)
                        dve.wait_ge(R["sin"].sem, R["sin"].at(u + 1))
                        v_order.step(dve, dve.tensor_tensor(t, t, squares[:, u % 3, :], ALU.add))
            for n in R:
                R[n].close(len(tiles))

        def attention(jobs, scale, bufs, side=()):
            sc, pt, stat = bufs
            R = named("qk", "top", "max", "exp", "norm", "turned", "turned_out", "pv", "pv_out")
            sig = lambda ins, n: ins.then_inc(R[n].sem, 1)
            wait = lambda eng, n, v: eng.wait_ge(R[n].sem, R[n].at(v))
            flat = ps[:, :, :].rearrange("p b n -> p (b n)")
            n_jobs = len(jobs)
            with nc.Block() as block:
                @block.gpsimd
                def _(pool):
                    for dst, factor in side:
                        pool.tensor_tensor(dst, dst, factor, ALU.mult)

                @block.tensor
                def _(pe):
                    def scores(j):
                        q, keys, _, _, _, _ = jobs[j]
                        if j >= 2:
                            wait(pe, "exp", j - 1)
                        for k_ap, c0, mask in keys:
                            dst = flat[:, (j % 2) * 1024 + c0:(j % 2) * 1024 + c0 + k_ap.shape[1]]
                            ins = pe.matmul(dst, q, k_ap, start=True, stop=mask is None)
                            if mask is not None:
                                ins = pe.matmul(dst, ident, mask, start=False, stop=True)
                        sig(ins, "qk")

                    def turn(j):
                        width = jobs[j][2]
                        wait(pe, "norm", j + 1)
                        if j >= 1:
                            wait(pe, "turned_out", j)
                        for c in range(width // P):
                            ins = pe.transpose(flat[:, 2048 + c * P:2048 + (c + 1) * P],
                                               sc[:, j % 2, c * P:(c + 1) * P], ident)
                        sig(ins, "turned")

                    def values(j):
                        _, _, width, v, _, o = jobs[j]
                        wait(pe, "turned_out", j + 1)
                        if j >= 2:
                            wait(pe, "pv_out", j - 1)
                        p0, d = o.start_partition(), v[0].shape[1]
                        for c in range(width // P):
                            ins = pe.matmul(ps[p0:p0 + d, 6 + j % 2, 0:P], v[c], pt[:, j % 2, c * P:(c + 1) * P],
                                            start=(c == 0), stop=(c == width // P - 1))
                        sig(ins, "pv")

                    scores(0)
                    scores(1)
                    for j in range(n_jobs):
                        turn(j)
                        if j + 2 < n_jobs:
                            scores(j + 2)
                        if j >= 1:
                            values(j - 1)
                    values(n_jobs - 1)

                @block.vector
                def _(dve):
                    def top(j):
                        _, _, width, _, sink, _ = jobs[j]
                        b = j % 2
                        m, t = stat[:, b, 0:1], stat[:, b, 3:4]
                        wait(dve, "qk", j + 1)
                        sig(dve.tensor_reduce(t, flat[:, b * 1024:b * 1024 + width], AX_X, ALU.max), "top")
                        wait(dve, "top", j + 1)
                        if j >= 2:
                            wait(dve, "exp", j - 1)
                        if sink is None:
                            sig(dve.tensor_scalar(m, t, -scale, None, ALU.mult), "max")
                        else:
                            v_order.step(dve, dve.scalar_tensor_tensor(t, t, scale, sink, ALU.mult, ALU.max))
                            sig(dve.tensor_scalar(m, t, -1.0, None, ALU.mult), "max")

                    def norm(j):
                        _, _, width, _, sink, _ = jobs[j]
                        b = j % 2
                        wait(dve, "exp", j + 1)
                        den = stat[:, b, 1:2]
                        if sink is not None:
                            v_order.step(dve, dve.tensor_tensor(den, den, stat[:, b, 2:3], ALU.add))
                        v_order.step(dve, dve.reciprocal(den, den))
                        sig(dve.tensor_scalar(sc[:, b, 0:width], sc[:, b, 0:width], den, None, ALU.mult), "norm")

                    top(0)
                    for j in range(n_jobs):
                        if j + 1 < n_jobs:
                            top(j + 1)
                        norm(j)

                @block.scalar
                def _(act):
                    def expo(j):
                        _, _, width, _, sink, _ = jobs[j]
                        b = j % 2
                        wait(act, "max", j + 1)
                        if j >= 2:
                            wait(act, "turned", j - 1)
                        if sink is not None:
                            a_order.step(act, act.activation(stat[:, b, 2:3], sink, ACT.Exp, bias=stat[:, b, 0:1]))
                        sig(act.activation(sc[:, b, 0:width], flat[:, b * 1024:b * 1024 + width], ACT.Exp,
                                           bias=stat[:, b, 0:1], scale=scale, accum_out=stat[:, b, 1:2]), "exp")

                    def take(j):
                        width = jobs[j][2]
                        wait(act, "turned", j + 1)
                        if j >= 2:
                            wait(act, "pv", j - 1)
                        sig(act.activation(pt[:, j % 2, 0:width], flat[:, 2048:2048 + width], ACT.Copy),
                            "turned_out")

                    def give(j):
                        o = jobs[j][5]
                        p0, d = o.start_partition(), o.shape[0]
                        wait(act, "pv", j + 1)
                        sig(act.activation(o, ps[p0:p0 + d, 6 + j % 2, 0:P], ACT.Copy), "pv_out")

                    expo(0)
                    for j in range(n_jobs):
                        if j + 1 < n_jobs:
                            expo(j + 1)
                        take(j)
                        if j >= 1:
                            give(j - 1)
                    give(n_jobs - 1)
            for n in R:
                R[n].close(n_jobs)

        groups = [([ctx2_in[:, c, k * P:(k + 1) * P] for c in range(NCTX)], xT[:, k, LAT:TOK]) for k in range(KT)]
        with nc.Block() as block:
            @block.sync
            def _(sp):
                sp.dma_start(ctx2_in, w["ctx_2"][0].rearrange("(c p) d -> p c d", p=P)).then_inc(loaded.sem, 16)

            @block.tensor
            def _(pe):
                pe.wait_ge(loaded.sem, loaded.at(16))
                transpose_pe(pe, groups)

            @block.vector
            def _(dve):
                transpose_out(dve, groups, 0)

            @block.scalar
            def _(act):
                transpose_out(act, groups, 1)
        loaded.close(16)
        transpose_close(groups)
        cur[0] = 1

        def part(n, pattern, **kw):
            used[0] += n
            assert used[0] <= 24576
            return big[:, used[0] - n:used[0]].rearrange(pattern, **kw)
        used = [0]
        qa = part(4 * TOK, "p (t n) -> p t n", t=4)
        ka = part(4 * TOK, "p (t n) -> p t n", t=4)
        va = part(NCH * 4 * 129, "p (c h e) -> p c h e", c=NCH, h=4)
        oa = part(4 * TOK, "p (t n) -> p t n", t=4)
        qb = part(4 * TOK, "p (t n) -> p t n", t=4)
        kb = part(2 * TOK, "p (t n) -> p t n", t=2)
        vb = part(NCH * P, "p (c n) -> p c n", c=NCH)
        k_tok = part(NCH * 512, "p (c n) -> p c n", c=NCH)
        free0 = used[0]
        units = []
        for buf, sc_ in ((qa, None), (ka, float(P) ** -0.5)):
            for s in range(2):
                units.append([("tile", m, t0, nt, buf[:, 2 * s + m, t0:t0 + nt], sc_)
                              for m in range(2) for t0, nt in BOTH])
        for s in range(2):
            units.append([("rows", c, 0, SLAB, va[:, c, 2 * s:2 * s + 2, 0:P], None) for c in range(NCH)])
        for buf in (oa, qb):
            for s in range(2):
                units.append([("tile", m, t0, nt, buf[:, 2 * s + m, t0:t0 + nt], None)
                              for m in range(2) for t0, nt in BOTH])
        units.append([("tile", 0, t0, nt, kb[:, 0, t0:t0 + nt], None) for t0, nt in BOTH] +
                     [("rows", c, P, P, vb[:, c, :], None) for c in range(NCH)])
        head_jobs = [[] for _ in range(8)] + \
                    [[(qb[:, 2 * s + m, t0:t0 + n], n, cols[:, COL["swa_q"]:COL["swa_q"] + 1])
                      for m in range(2) for t0, n in BOTH] for s in range(2)]
        units_stage(W["ab"], units, modulated(0, False, xT, hT, BOTH), w["ab_w_in_2"][0, :, AB_G:AB_G + 16],
                    rows[:, GATE_B:GATE_B + 16], [(va, 1.0)], head_jobs=head_jobs, head_mat=blk64, head=64)

        log_f = by_chunk(dt)
        fs = lambda a: by_chunk(a).rearrange("p c (d k h) -> p c d k h", d=2, k=2)[:, :, :, 1, :]
        raw = big[0:4, free0:free0 + 4 * TOK].rearrange("p (k n) -> p k n", k=4)
        with nc.Block() as block:
            @block.vector
            def _(dve):
                v_order.step(dve, dve.scalar_tensor_tensor(t_a, dt, -1.0, dt, ALU.mult, ALU.max))
                dve_abs[0] = v_order.n
                dve.wait_ge(S["exp_ln"].sem, S["exp_ln"].at(1))
                v_order.step(dve, dve.tensor_scalar(t_b, t_a, 1.0, None, ALU.add))
                dve_abs[1] = v_order.n
                v_order.step(dve, dve.tensor_scalar(dA, t_b, -1.0, None, ALU.add))
                dve.wait_ge(S["exp_ln"].sem, S["exp_ln"].at(2))
                v_order.step(dve, dve.tensor_scalar(t_b, dA, 0.0, None, ALU.is_equal))
                v_order.step(dve, dve.tensor_tensor(t_c, t_c, t_b, ALU.add))
                v_order.step(dve, dve.tensor_tensor(dA, dA, t_b, ALU.add))
                v_order.step(dve, dve.reciprocal(dA, dA))
                v_order.step(dve, dve.tensor_tensor(t_c, t_c, dA, ALU.mult))
                v_order.step(dve, dve.tensor_tensor(t_c, t_c, t_a, ALU.mult))
                v_order.step(dve, dve.tensor_scalar(t_b, dt, 0.0, None, ALU.min))
                v_order.step(dve, dve.tensor_tensor(t_b, t_b, t_c, ALU.subtract))
                for d in range(2):
                    o = 8 * d + 4
                    v_order.step(dve, dve.tensor_copy(by_chunk(dt)[:, :, o:o + 4], by_chunk(t_b)[:, :, o:o + 4]))

            @block.scalar
            def _(act):
                act.wait_ge(v_order.sem, dve_abs[0])
                act.activation(t_a, t_a, ACT.Exp, scale=-1.0).then_inc(S["exp_ln"].sem, 1)
                act.wait_ge(v_order.sem, dve_abs[1])
                act.activation(t_c, t_b, ACT.Ln).then_inc(S["exp_ln"].sem, 1)
        S["exp_ln"].close(2)
        groups = []
        for kind in range(4):
            lat = [dt[:, c * 16 + kind * 4:c * 16 + kind * 4 + 4] for c in range(NCH)]
            groups.append((lat[0:NLAT], raw[:, kind, 0:LAT]))
            groups.append((lat[NLAT:], raw[:, kind, LAT:TOK]))
        for c in range(NCH):
            groups.append(([ka[:, h, c * CH:(c + 1) * CH] for h in range(4)], k_tok[:, c, :]))
        with nc.Block() as block:
            @block.tensor
            def _(pe):
                transpose_pe(pe, groups)

            @block.vector
            def _(dve):
                transpose_out(dve, groups, 0)

            @block.scalar
            def _(act):
                transpose_out(act, groups, 1)
        transpose_close(groups)

        row_m = squares[:, :, :].rearrange("p a n -> p (a n)")[0:4, 0:2 * TOK].rearrange("p (q n) -> p q n", q=2)
        one_row = ones[0:4, :]
        m_col = small[0:4, 480:482]
        b_row, r_row, g_row = (small[0:4, 32 + i * CH:32 + (i + 1) * CH] for i in range(3))

        def gate_rows(dve, d, c):
            view = lambda a: a[:, ::-1] if d else a
            cut = lambda a: view(a[:, c * CH:(c + 1) * CH])
            last = (lambda a: a[:, 0:1]) if d else (lambda a: a[:, CH - 1:CH])
            ii, ff = raw[:, 2 * d, :], raw[:, 2 * d + 1, :]
            m = m_col[:, d:d + 1]
            v_order.step(dve, dve.tensor_tensor_scan(view(b_row), one_row, cut(ff), 0.0, ALU.mult, ALU.add))
            v_order.step(dve, dve.tensor_tensor(r_row, ii[:, c * CH:(c + 1) * CH], b_row, ALU.subtract))
            v_order.step(dve, dve.tensor_tensor_scan(view(g_row), view(r_row), view(r_row), m, ALU.max, ALU.max))
            v_order.mark(dve.tensor_scalar(ii[:, c * CH:(c + 1) * CH], g_row, -1.0, m, ALU.mult, ALU.add))
            v_order.mark(dve.tensor_tensor(ff[:, c * CH:(c + 1) * CH], b_row, g_row, ALU.add))
            v_order.step(dve, dve.tensor_scalar(row_m[:, d, c * CH:(c + 1) * CH], r_row, m, None, ALU.subtract))
            sig(dve.tensor_copy(m, last(ff[:, c * CH:(c + 1) * CH])), "rows")
            dve.wait_ge(S["rows"].sem, S["rows"].at(rows_made[0] + 1))
            rows_made[0] += 1
        rows_made = [0]

        used[0] = free0
        part(4 * TOK, "p (k n) -> p k n", k=4)
        wide = lambda b: b.rearrange("p h n -> p (h n)")
        c_state = [t[:, 0:4 * 129].rearrange("p (h e) -> p h e", h=4) for t in (mean, rstd)]
        hfree = hT[:, 4:8, :].rearrange("p t n -> p (t n)")
        pmat0, pmat1, iw0, em0, kw, qs0 = (hfree[:, i * 512:(i + 1) * 512].rearrange("p (h n) -> p h n", h=4)
                                           for i in range(6))
        pmats, iws = (pmat0, pmat1), (iw0, part(512, "p (h n) -> p h n", h=4))
        ems = (em0, ada_rows[:, :, :].rearrange("p b (h n) -> p (b h) n", n=P))
        qss = ((qs0[:, 0:2, :], qs0[:, 2:4, :]),
               (mats[:, DFT_C:DFT_S + 1, :], sil[:, 0, :, :].rearrange("p k n -> p (k n)")
                .rearrange("p (h n) -> p h n", h=2)))
        rp_cols = (small[:, 0:4], small[:, 8:12])
        w_cols = (small[:, 4:8], small[:, 12:16])
        order_m = [(d, order_of[d][k], k) for k in range(NCH) for d in range(2)]
        R = named("bc", "cols", "rp", "seg", "p_exp", "p", "em", "w", "masked", "m", "qs", "kw", "mem", "h", "iw", "w_exp", "rows")
        n_m = len(order_m)
        chunk4 = lambda buf, c: buf[:, :, c * CH:(c + 1) * CH]
        with nc.Block() as block:
            @block.tensor
            def _(pe):
                def front(s):
                    d, c, k = order_m[s]
                    t0 = c * CH
                    if s >= 1:
                        wait(pe, "m", s)
                        wait(pe, "em", s)
                        wait(pe, "iw", s)
                        wait(pe, "rp", s)
                        wait(pe, "w", s)
                    wait(pe, "rows", s + 1)
                    for h in range(4):
                        pe.matmul(ps[:, 0, h * P:(h + 1) * P], mats[0:4, SEL + h, :], raw[:, 2 * d, t0:t0 + CH],
                                  start=True, stop=True)
                        pe.matmul(ps[:, 1, h * P:(h + 1) * P], mats[0:4, SEL + h, :], raw[:, 2 * d + 1, t0:t0 + CH],
                                  start=True, stop=True)
                    sig(pe.transpose(ps[:, 7, 0:4], row_m[:, d, t0:t0 + CH], ident[0:4, 0:4]), "bc")
                    for h in range(4):
                        ins = pe.matmul(ps[:, 2, h * P:(h + 1) * P], ka[:, h, t0:t0 + CH], qa[:, h, t0:t0 + CH],
                                        start=True, stop=True)
                    sig(ins, "cols")

                front(0)
                for s, (d, c, k) in enumerate(order_m):
                    if s + 1 < n_m:
                        front(s + 1)
                    wait(pe, "m", s + 1)
                    wait(pe, "qs", s + 1)
                    if s >= 1:
                        wait(pe, "h", s)
                    if s >= 2:
                        wait(pe, "mem", s - 1)
                    pmat = pmats[s % 2]
                    for h in range(4):
                        q = qss[s % 2][h // 2][:, h % 2, :]
                        o, dn = ps[:, 3, h * P:(h + 1) * P], ps[:, 4, h * P:(h + 1) * P]
                        pe.matmul(o, va[:, c, h, 0:P], pmat[:, h, :], start=True, stop=False)
                        pe.matmul(o, c_state[d][:, h, 0:P], q, start=False, stop=True)
                        pe.matmul(dn, ones, pmat[:, h, :], start=True, stop=False)
                        ins = pe.matmul(dn, c_state[d][:, h, P:P + 1].to_broadcast([P, P]), q,
                                        start=False, stop=True)
                    sig(ins, "p")
                    wait(pe, "kw", s + 1)
                    if s >= 1:
                        wait(pe, "mem", s)
                    for h in range(4):
                        ins = pe.matmul(ps[:, 5 + h // 2, (h % 2) * 129:(h % 2) * 129 + 129], kw[:, h, :],
                                        va[:, c, h, :], start=True, stop=True)
                    sig(ins, "masked")

            @block.vector
            def _(dve):
                for st in c_state:
                    v_order.step(dve, dve.memset(st, 0.0))
                v_order.step(dve, dve.memset(m_col, 0.0))

                def front(s):
                    d, c, k = order_m[s]
                    rp_col, w_col, pmat = rp_cols[s % 2], w_cols[s % 2], pmats[s % 2]
                    tri = (U_LE, U_GE)[d]
                    edge = 0 if d else CH - 1
                    wait(dve, "bc", s + 1)
                    sig(dve.tensor_copy(rp_col, ps[:, 7, 0:4]), "rp")
                    wait(dve, "rp", s + 1)
                    wait(dve, "iw", s + 1)
                    if s >= 2:
                        wait(dve, "kw", s - 1)
                    last_a = ps[:, 0, :].rearrange("p (h n) -> p h n", h=4)[:, :, edge]
                    sig(dve.tensor_tensor(w_col, last_a, rp_col, ALU.add), "w")
                    for h in range(4):
                        ins = dve.tensor_scalar(pmat[:, h, :], ps[:, 0, h * P:(h + 1) * P], rp_col[:, h:h + 1], 0.0,
                                                ALU.add, ALU.min)
                    sig(ins, "seg")
                    for half in range(2):
                        ins = dve.tensor_tensor(qss[s % 2][half], qa[:, 2 * half:2 * half + 2, c * CH:(c + 1) * CH],
                                                iws[s % 2][:, 2 * half:2 * half + 2, :], ALU.mult)
                    sig(ins, "qs")
                    wait(dve, "p_exp", s + 1)
                    v_order.step(dve, dve.tensor_tensor(
                        pmat, pmat, mats[:, tri, :].unsqueeze(1).to_broadcast([P, 4, P]), ALU.mult))
                    wait(dve, "cols", s + 1)
                    sig(dve.tensor_tensor(wide(pmat), wide(pmat), ps[:, 2, :], ALU.mult), "m")

                gate_rows(dve, *order_m[0][:2])
                gate_rows(dve, *order_m[1][:2])
                front(0)
                for s, (d, c, k) in enumerate(order_m):
                    if s + 1 < n_m:
                        front(s + 1)
                    if s + 2 < n_m:
                        gate_rows(dve, *order_m[s + 2][:2])
                    edge = 0 if d else CH - 1
                    em, iw = ems[s % 2], iws[s % 2]
                    wait(dve, "p", s + 1)
                    wait(dve, "em", s + 1)
                    den = ps[:, 4, :].rearrange("p (h n) -> p h n", h=4)
                    v_order.step(dve, dve.tensor_tensor(em, den, em, ALU.max))
                    v_order.step(dve, dve.scalar_tensor_tensor(em, den, -1.0, em, ALU.mult, ALU.max))
                    v_order.step(dve, dve.reciprocal(em, em))
                    dst = chunk4(hT[:, 0:4, :], c)
                    num = ps[:, 3, :].rearrange("p (h n) -> p h n", h=4)
                    if any(x[1] == c for x in order_m[:s]):
                        v_order.step(dve, dve.tensor_tensor(em, num, em, ALU.mult))
                        sig(dve.tensor_tensor(dst, dst, em, ALU.add), "h")
                    else:
                        sig(dve.tensor_tensor(dst, num, em, ALU.mult), "h")
                    wait(dve, "h", s + 1)
                    wait(dve, "masked", s + 1)
                    for h in range(4):
                        st = c_state[d][:, h, :]
                        ins = dve.scalar_tensor_tensor(st, st, iw[:, h, edge:edge + 1],
                                                       ps[:, 5 + h // 2, (h % 2) * 129:(h % 2) * 129 + 129],
                                                       ALU.mult, ALU.add)
                    sig(ins, "mem")
                    wait(dve, "mem", s + 1)

            @block.scalar
            def _(act):
                for s, (d, c, k) in enumerate(order_m):
                    w_col, pmat = w_cols[s % 2], pmats[s % 2]
                    wait(act, "bc", s + 1)
                    if s >= 2:
                        wait(act, "mem", s - 1)
                        wait(act, "qs", s - 1)
                    sig(act.activation(iws[s % 2], ps[:, 0, :].rearrange("p (h n) -> p h n", h=4), ACT.Exp), "iw")
                    sig(act.activation(ems[s % 2], ps[:, 1, :].rearrange("p (h n) -> p h n", h=4), ACT.Exp,
                                       scale=-1.0), "em")
                    wait(act, "seg", s + 1)
                    sig(act.activation(wide(pmat), wide(pmat), ACT.Exp), "p_exp")
                    sig(act.activation(w_col, w_col, ACT.Exp), "w_exp")
                for t in range(4):
                    act.activation(oa[:, t, :], oa[:, t, :], ACT.Sigmoid)

            @block.gpsimd
            def _(pool):
                for s, (d, c, k) in enumerate(order_m):
                    wait(pool, "w_exp", s + 1)
                    if s >= 1:
                        wait(pool, "masked", s)
                    sig(pool.tensor_tensor(kw, k_tok[:, c, :].rearrange("p (h n) -> p h n", h=4),
                                           w_cols[s % 2].unsqueeze(2).to_broadcast([P, 4, P]), ALU.mult), "kw")
        for n in R:
            R[n].close(n_m)

        jobs = [(hT[:, t, t0:t0 + n], n, cols[:, COL["mlstm_norm"] + t:COL["mlstm_norm"] + t + 1], ones, P)
                for t in range(4) for t0, n in BOTH]
        jobs += [(kb[:, 0, t0:t0 + n], n, cols[:, COL["swa_k"]:COL["swa_k"] + 1], blk64, 64) for t0, n in BOTH]

        def load_tables(sp):
            sp.dma_start(qa[:, 0:2, 0:LAT], w["const_tables"][T_CB:T_CB + 2].rearrange("t p n -> p t n"))\
              .then_inc(loaded.sem, 16)
            sp.wait_ge(loaded.sem, loaded.at(16))
        head_norms(jobs, load_tables)
        loaded.close(16)

        rope([qb[:, t, 0:LAT] for t in range(4)] + [kb[:, 0, 0:LAT]], ROT32, qa[:, 0, 0:LAT], qa[:, 1, 0:LAT])
        named("swapped")
        with nc.Block() as block:
            @block.tensor
            def _(pe):
                for r, (t0, n) in enumerate(BOTH):
                    ins = pe.matmul(ps[:, r, 0:n], mats[:, SWAP, :], kb[:, 0, t0:t0 + n], start=True, stop=True)
                ins.then_inc(S["swapped"].sem, 1)

            @block.vector
            def _(dve):
                dve.wait_ge(S["swapped"].sem, S["swapped"].at(1))
                for r, (t0, n) in enumerate(BOTH):
                    dve.tensor_copy(kb[:, 1, t0:t0 + n], ps[:, r, 0:n])
        S["swapped"].close(1)
        bufs = (ka.rearrange("p t n -> p (t n)")[:, 0:2 * TOK].rearrange("p (b n) -> p b n", b=2),
                ka.rearrange("p t n -> p (t n)")[:, 2 * TOK:4 * TOK].rearrange("p (b n) -> p b n", b=2),
                small[:, 0:16].rearrange("p (b n) -> p b n", b=2))
        jobs = []
        for h in range(B_HEADS):
            kv, half = h // (B_HEADS // 2), h % 2
            rows_h = slice(64 * half, 64 * half + 64)
            keys_t = kb[rows_h, 0 if kv == half else 1, :]
            for n in range(NCH):
                keys, v, width = [], [], 0
                if n < NLAT:
                    for kn, mask in ((n - 1, M_PREV), (n, None), (n + 1, M_NEXT)):
                        if 0 <= kn < NLAT:
                            keys.append((keys_t[:, kn * CH:(kn + 1) * CH], width,
                                         None if mask is None else mats[:, mask, :]))
                            v.append(vb[:, kn, kv * 64:(kv + 1) * 64])
                            width += CH
                if width + CTX > 512 > width:
                    cut = 512 - width
                    keys += [(keys_t[:, LAT:LAT + cut], width, None), (keys_t[:, LAT + cut:TOK], 512, None)]
                else:
                    keys.append((keys_t[:, LAT:TOK], width, None))
                v += [vb[:, NLAT + i, kv * 64:(kv + 1) * 64] for i in range(NCTX)]
                width += CTX
                jobs.append((qb[rows_h, h // 2, n * CH:(n + 1) * CH], keys, width, v,
                             rows[:, SINK + h:SINK + h + 1],
                             hT[rows_h, 4 + h // 2, n * CH:(n + 1) * CH]))
        attention(jobs, 64.0 ** -0.5, bufs, [(hT[:, t, :], oa[:, t, :]) for t in range(4)])
        output_projection("ab_out", BOTH)
        mixer.close()
        mlp_stage(0, BOTH)
        hT, big = sb("hT2", [P, KT, TOK], mixer), own_memory("2")

        cur[0] = 2
        used[0] = 0
        qc = part(8 * LAT, "p (t n) -> p t n", t=8)
        kc = part(2 * TOK, "p (t n) -> p t n", t=2)
        vc = part(NCH * SLAB, "p (c n) -> p c n", c=NCH)
        tabs = part(2 * LAT, "p (t n) -> p t n", t=2)
        bufs = (part(2 * TOK, "p (b n) -> p b n", b=2), part(2 * TOK, "p (b n) -> p b n", b=2),
                small[:, 0:16].rearrange("p (b n) -> p b n", b=2))
        units = [[("tile", m, 0, LAT, qc[:, 2 * s + m, :], None) for m in range(2)] for s in range(4)]
        units.append([("tile", m, t0, nt, kc[:, m, t0:t0 + nt], None) for m in range(2) for t0, nt in BOTH])
        units.append([("rows", c, 0, SLAB, vc[:, c, :], None) for c in range(NCH)])
        with nc.Block() as block:
            @block.sync
            def _(sp):
                sp.dma_start(tabs, w["const_tables"][T_CC:T_CC + 2].rearrange("t p n -> p t n"))\
                  .then_inc(loaded.sem, 16)
                sp.wait_ge(loaded.sem, loaded.at(16))
        loaded.close(16)
        head_jobs = [[(qc[:, 2 * s + m, :], LAT, cols[:, COL["c_q_norm"]:COL["c_q_norm"] + 1]) for m in range(2)]
                     for s in range(4)]
        head_jobs.append([(kc[:, t, t0:t0 + n], n, cols[:, COL["c_k_norm"]:COL["c_k_norm"] + 1])
                          for t in range(2) for t0, n in BOTH])
        units_stage(W["c"], units, modulated(0, False, xT, hT, BOTH), None, None,
                    head_jobs=head_jobs, head_mat=ones)
        rope([qc[:, t, :] for t in range(8)] + [kc[:, t, 0:LAT] for t in range(2)], ROT64,
             tabs[:, 0, :], tabs[:, 1, :])
        jobs = []
        for h in range(8):
            kv = h // 4
            for n in range(NLAT):
                keys = [(kc[:, kv, 0:LAT], 0, None), (kc[:, kv, LAT:TOK], 512, None)]
                v = [vc[:, c, kv * P:(kv + 1) * P] for c in range(NCH)]
                jobs.append((qc[:, h, n * CH:(n + 1) * CH], keys, TOK, v, None, hT[:, h, n * CH:(n + 1) * CH]))
        attention(jobs, 128.0 ** -0.5, bufs)
        output_projection("c_out", ONLY_LAT)
        mixer.close()
        mlp_stage(1, ONLY_LAT)

        y_out = sb("y_out", [P, NLAT, D])
        groups = [([xT[:, k, c * CH:(c + 1) * CH] for k in range(4 * q, 4 * q + 4)],
                   y_out[:, c, q * 512:(q + 1) * 512]) for c in range(NLAT) for q in range(2)]
        with nc.Block() as block:
            @block.tensor
            def _(pe):
                transpose_pe(pe, groups)

            @block.vector
            def _(dve):
                transpose_out(dve, groups, 0)

            @block.scalar
            def _(act):
                transpose_out(act, groups, 1)

            @block.sync
            def _(sp):
                for c in range(NLAT):
                    sp.wait_ge(tr_free_v.sem, tr_free_v.at(c + 1))
                    sp.wait_ge(tr_free_a.sem, tr_free_a.at(c + 1))
                    sp.dma_start(out[0, c * CH:(c + 1) * CH, :], y_out[:, c, :]).then_inc(stored.sem, 16)
                sp.wait_ge(stored.sem, stored.at(16 * NLAT))
        transpose_close(groups)


_INS = ["x", "c", "ctx", "c_ctx", "w_ada", "b_ada", "w_in", "ssd_conv_w", "ssd_conv_b", "ssd_dt_bias",
        "ssd_a_log", "ssd_d", "ssd_norm_w", "fnet_w", "pool_w", "pool_scale", "w_out", "ln1_g", "ln1_b",
        "ffn_w_up", "ffn_conv_w", "ffn_conv_b", "ffn_w_down", "ln2_g", "ln2_b", "c_2", "ctx_2", "c_ctx_2",
        "ada_w_2", "ada_b_2", "norm1_g_2", "norm2_g_2", "ab_w_in_2", "ab_gate_b_2", "mlstm_norm_g_2",
        "swa_q_norm_g_2", "swa_k_norm_g_2", "swa_sink_2", "ab_w_out_2", "c_w_in_2", "c_q_norm_g_2",
        "c_k_norm_g_2", "c_w_out_2", "mlp_w1_2", "mlp_w2_2"]


def kernel(**inputs):
    import concourse.bacc as bacc
    from concourse.bass_utils import run_bass_kernel_spmd

    nc = bacc.Bacc("TRN2", target_bir_lowering=False, num_devices=1)
    arrays, w = {}, {}
    data = {n: np.ascontiguousarray(inputs[n]) for n in _INS}
    data["const_mats"], data["const_tables"], data["const_dft"] = shape_constants()
    for name, a in data.items():
        arrays[f"in_{name}"] = a
        w[name] = nc.dram_tensor(f"in_{name}", a.shape, mybir.dt.from_np(a.dtype), kind="ExternalInput").ap()
    out = nc.dram_tensor("out_0", (1, LAT, D), F32, kind="ExternalOutput").ap()
    program(nc, w, out)
    r = run_bass_kernel_spmd(nc, [arrays], core_ids=[0])
    return r.results[0]["out_0"]
```
